# Optimizing a Trainium2 kernel written in Bass

```python
import jax, jax.numpy as jnp
from jax import lax
import numpy as np

D_MODEL = 1024
BATCH = 1
SEQ = 512
DEPTH = 2
DEC_BATCH = 8
DEC_SEQ = 8
PAST_LEN = 4096
PAGE_SIZE = 128

D_MIX = D_MODEL
LRU_WIDTH = D_MIX // 4
LRU_BLOCKS = 4
LRU_BLOCK_W = LRU_WIDTH // LRU_BLOCKS
LRU_CONV_W = 4
LRU_C = 8.0
SC_WIDTH = D_MIX // 4
SC_CONV_W = 3
MLA_HEADS = 8
QK_NOPE = 64
QK_ROPE = 32
V_HEAD = (D_MIX - LRU_WIDTH - SC_WIDTH) // MLA_HEADS
Q_LORA = 256
KV_LORA = 128
ROPE_THETA = 10000.0
Q_BLOCK = 128
SM_SCALE = (QK_NOPE + QK_ROPE) ** -0.5
N_IN = 2 * LRU_WIDTH + 3 * SC_WIDTH + Q_LORA + KV_LORA + QK_ROPE
N_GROUPS = 4
EXPERTS_PER_GROUP = 4
N_EXPERTS = N_GROUPS * EXPERTS_PER_GROUP
TOP_K = 2
D_FF_EXPERT = D_MODEL // 4
ALPHA = (2 * DEPTH) ** 0.25
BETA = (8 * DEPTH) ** -0.25
LN_EPS = 1e-5
RMS_EPS = 1e-6

kernel_name = "hymba_rglru_sconv_mla_hmoe_step"

def layer_norm(x, g, b):
    xf = x.astype(jnp.float32)
    mu = jnp.mean(xf, axis=-1, keepdims=True)
    var = jnp.mean(jnp.square(xf - mu), axis=-1, keepdims=True)
    return ((xf - mu) * lax.rsqrt(var + LN_EPS) * g + b).astype(x.dtype)

def rms_norm(x, g):
    xf = x.astype(jnp.float32)
    return (xf * lax.rsqrt(jnp.mean(jnp.square(xf), axis=-1, keepdims=True) + RMS_EPS) * g).astype(x.dtype)

def rope(x, pos):
    half = x.shape[-1] // 2
    freqs = ROPE_THETA ** (-jnp.arange(half, dtype=jnp.float32) / half)
    ang = pos.astype(jnp.float32)[:, None] * freqs[None, :]
    cos = jnp.cos(ang)[None, :, None, :]
    sin = jnp.sin(ang)[None, :, None, :]
    x1 = x[..., :half].astype(jnp.float32)
    x2 = x[..., half:].astype(jnp.float32)
    return jnp.concatenate([x1 * cos - x2 * sin, x1 * sin + x2 * cos], axis=-1).astype(x.dtype)

def causal_dwconv(u, prev, w, b):
    width = w.shape[0]
    t = u.shape[1]
    full = jnp.concatenate([prev.astype(u.dtype), u], axis=1)
    out = sum(full[:, k:k + t] * w[k] for k in range(width))
    if b is not None:
        out = out + b
    return out, full[:, t:]

def block_diag(x, w, b):
    bsz, t, _ = x.shape
    xb = x.reshape(bsz, t, LRU_BLOCKS, LRU_BLOCK_W)
    return jnp.einsum('btnc,ncd->btnd', xb, w).reshape(bsz, t, LRU_WIDTH) + b

def _lin_combine(c1, c2):
    a1, b1 = c1
    a2, b2 = c2
    return a1 * a2, a2 * b1 + b2

def rglru(x, h0, gxw, gxb, gaw, gab, lam):
    i_gate = jax.nn.sigmoid(block_diag(x, gxw, gxb).astype(jnp.float32))
    r_gate = jax.nn.sigmoid(block_diag(x, gaw, gab).astype(jnp.float32))
    log_a = -LRU_C * r_gate * jax.nn.softplus(-lam.astype(jnp.float32))
    a = jnp.exp(log_a)
    mult = jnp.sqrt(-jnp.expm1(2.0 * log_a))
    b = mult * i_gate * x.astype(jnp.float32)
    b = jnp.concatenate([b[:, :1] + a[:, :1] * h0.astype(jnp.float32)[:, None, :], b[:, 1:]], axis=1)
    _, h = lax.associative_scan(_lin_combine, (a, b), axis=1)
    return h.astype(x.dtype), h[:, -1].astype(x.dtype)

def mla_attend(q_lat, q_rope, ckv, kr, q_pos, k_pos):
    s = (jnp.einsum('bqhr,bkr->bhqk', q_lat, ckv)
         + jnp.einsum('bqhp,bkp->bhqk', q_rope, kr)).astype(jnp.float32) * SM_SCALE
    s = jnp.where(k_pos[None, None, None, :] <= q_pos[None, None, :, None], s, -jnp.inf)
    p = jax.nn.softmax(s, axis=-1).astype(ckv.dtype)
    return jnp.einsum('bhqk,bkr->bqhr', p, ckv)

def causal_block_attend(q_lat, q_rope, ckv, kr, pos):
    bsz, t, h, r = q_lat.shape
    qb = min(Q_BLOCK, t)
    nb = t // qb
    q_b = q_lat.reshape(bsz, nb, qb, h, r).swapaxes(0, 1)
    r_b = q_rope.reshape(bsz, nb, qb, h, QK_ROPE).swapaxes(0, 1)
    p_b = pos.reshape(nb, qb)
    o = lax.map(lambda a: mla_attend(a[0], a[1], ckv, kr, a[2], pos), (q_b, r_b, p_b))
    return o.swapaxes(0, 1).reshape(bsz, t, h, r)

def hybrid_mixer(x, pos, past_ckv, past_kr, h0, conv_a_prev, conv_b_prev,
                 w_in, lru_conv_w, lru_conv_b, gxw, gxb, gaw, gab, lam, sc_conv_w,
                 q_norm_g, kv_norm_g, w_uq, w_uk, w_uv, w_out):
    bsz, t, _ = x.shape
    proj = jnp.einsum('btd,dn->btn', x, w_in)
    idx = [int(v) for v in np.cumsum([LRU_WIDTH, LRU_WIDTH, SC_WIDTH, SC_WIDTH, SC_WIDTH, Q_LORA, KV_LORA])]
    xa, ga, gb, gc, ub, cq, ckv, kr = jnp.split(proj, idx, axis=-1)
    xa, conv_a_new = causal_dwconv(xa, conv_a_prev, lru_conv_w, lru_conv_b)
    ya, h_last = rglru(xa, h0, gxw, gxb, gaw, gab, lam)
    ya = ya * jax.nn.gelu(ga)
    z = gc * ub
    zc, conv_b_new = causal_dwconv(z, conv_b_prev, sc_conv_w, None)
    yb = gb * zc
    q = jnp.einsum('btq,qn->btn', rms_norm(cq, q_norm_g), w_uq).reshape(bsz, t, MLA_HEADS, QK_NOPE + QK_ROPE)
    q_nope = q[..., :QK_NOPE]
    q_rope = rope(q[..., QK_NOPE:], pos)
    ckv = rms_norm(ckv, kv_norm_g)
    kr = rope(kr[:, :, None, :], pos)[:, :, 0, :]
    q_lat = jnp.einsum('bthn,rhn->bthr', q_nope, w_uk)
    if past_ckv is None:
        o_lat = causal_block_attend(q_lat, q_rope, ckv, kr, pos)
    else:
        keys_ckv = jnp.concatenate([past_ckv, ckv], axis=1)
        keys_kr = jnp.concatenate([past_kr, kr], axis=1)
        k_pos = jnp.arange(keys_ckv.shape[1], dtype=jnp.int32)
        o_lat = mla_attend(q_lat, q_rope, keys_ckv, keys_kr, pos, k_pos)
    yc = jnp.einsum('bthr,rhv->bthv', o_lat, w_uv).reshape(bsz, t, MLA_HEADS * V_HEAD)
    y = jnp.einsum('btm,md->btd', jnp.concatenate([ya, yb, yc], axis=-1), w_out)
    return y, ckv, kr, h_last, conv_a_new, conv_b_new

def hier_moe(x, rg_w, rg_b, re_w, re_b, w_gate, w_up, w_down):
    bsz, t, d = x.shape
    xt = x.reshape(bsz * t, d)
    p_group = jax.nn.softmax((xt @ rg_w + rg_b).astype(jnp.float32), axis=-1)
    g_idx = jnp.argmax(p_group, axis=-1)
    g_prob = jnp.max(p_group, axis=-1)
    logits_e = (xt @ re_w + re_b).astype(jnp.float32).reshape(-1, N_GROUPS, EXPERTS_PER_GROUP)
    logits_in = jnp.take_along_axis(logits_e, g_idx[:, None, None], axis=1)[:, 0]
    p_in = jax.nn.softmax(logits_in, axis=-1)
    top_p, top_i = lax.top_k(p_in, TOP_K)
    weights = top_p / jnp.sum(top_p, axis=-1, keepdims=True) * g_prob[:, None]
    expert_id = g_idx[:, None] * EXPERTS_PER_GROUP + top_i
    combine = jnp.sum(jax.nn.one_hot(expert_id, N_EXPERTS, dtype=jnp.float32) * weights[..., None],
                      axis=1).astype(x.dtype)
    h = jax.nn.silu(jnp.einsum('td,edf->tef', xt, w_gate)) * jnp.einsum('td,edf->tef', xt, w_up)
    y = jnp.einsum('tef,efd->td', h * combine[:, :, None], w_down)
    return y.reshape(bsz, t, d)

def setup_inputs(seed: int = 0) -> dict:
    key = jax.random.key(seed)
    ks = iter(jax.random.split(key, 48))

    def nrm(shape, scale):
        return scale * jax.random.normal(next(ks), shape, jnp.float32)

    n_pages = PAST_LEN // PAGE_SIZE
    n_used = DEC_BATCH * n_pages
    n_pool = n_used + max(1, n_used // 4)
    page_table = jax.random.permutation(next(ks), n_pool)[:n_used].reshape(DEC_BATCH, n_pages).astype(jnp.int32)
    u = jax.random.uniform(next(ks), (DEPTH, LRU_WIDTH), jnp.float32, 0.9, 0.999)
    a0 = u ** (1.0 / LRU_C)
    lru_lambda = jnp.log(a0) - jnp.log1p(-a0)
    return {
        'x_prompt': nrm((BATCH, SEQ, D_MODEL), 1.0),
        'x_sample': nrm((DEC_BATCH, DEC_SEQ, D_MODEL), 1.0),
        'cache_ckv': nrm((DEPTH, n_pool, PAGE_SIZE, KV_LORA), 1.0),
        'cache_krope': nrm((DEPTH, n_pool, PAGE_SIZE, QK_ROPE), 1.0),
        'state_lru_h': nrm((DEPTH, DEC_BATCH, LRU_WIDTH), 0.5),
        'state_lru_conv': nrm((DEPTH, DEC_BATCH, LRU_CONV_W - 1, LRU_WIDTH), 1.0),
        'state_sconv': nrm((DEPTH, DEC_BATCH, SC_CONV_W - 1, SC_WIDTH), 1.0),
        'page_table': page_table,
        'w_in': nrm((DEPTH, D_MODEL, N_IN), D_MODEL ** -0.5),
        'lru_conv_w': nrm((DEPTH, LRU_CONV_W, LRU_WIDTH), LRU_CONV_W ** -0.5),
        'lru_conv_b': nrm((DEPTH, LRU_WIDTH), 0.02),
        'lru_gate_x_w': nrm((DEPTH, LRU_BLOCKS, LRU_BLOCK_W, LRU_BLOCK_W), LRU_BLOCK_W ** -0.5),
        'lru_gate_x_b': nrm((DEPTH, LRU_WIDTH), 0.02),
        'lru_gate_a_w': nrm((DEPTH, LRU_BLOCKS, LRU_BLOCK_W, LRU_BLOCK_W), LRU_BLOCK_W ** -0.5),
        'lru_gate_a_b': nrm((DEPTH, LRU_WIDTH), 0.02),
        'lru_lambda': lru_lambda,
        'sc_conv_w': nrm((DEPTH, SC_CONV_W, SC_WIDTH), SC_CONV_W ** -0.5),
        'q_norm_g': 1.0 + nrm((DEPTH, Q_LORA), 0.02),
        'kv_norm_g': 1.0 + nrm((DEPTH, KV_LORA), 0.02),
        'w_uq': nrm((DEPTH, Q_LORA, MLA_HEADS * (QK_NOPE + QK_ROPE)), Q_LORA ** -0.5),
        'w_uk': nrm((DEPTH, KV_LORA, MLA_HEADS, QK_NOPE), KV_LORA ** -0.5),
        'w_uv': nrm((DEPTH, KV_LORA, MLA_HEADS, V_HEAD), BETA * KV_LORA ** -0.5),
        'w_out': nrm((DEPTH, D_MIX, D_MODEL), BETA * D_MIX ** -0.5),
        'ln_mix_g': 1.0 + nrm((DEPTH, D_MODEL), 0.02),
        'ln_mix_b': nrm((DEPTH, D_MODEL), 0.02),
        'router_group_w': nrm((DEPTH, D_MODEL, N_GROUPS), D_MODEL ** -0.5),
        'router_group_b': nrm((DEPTH, N_GROUPS), 0.01),
        'router_expert_w': nrm((DEPTH, D_MODEL, N_EXPERTS), D_MODEL ** -0.5),
        'router_expert_b': nrm((DEPTH, N_EXPERTS), 0.01),
        'w_gate': nrm((DEPTH, N_EXPERTS, D_MODEL, D_FF_EXPERT), D_MODEL ** -0.5),
        'w_up': nrm((DEPTH, N_EXPERTS, D_MODEL, D_FF_EXPERT), D_MODEL ** -0.5),
        'w_down': nrm((DEPTH, N_EXPERTS, D_FF_EXPERT, D_MODEL), BETA * D_FF_EXPERT ** -0.5),
        'ln_ffn_g': 1.0 + nrm((DEPTH, D_MODEL), 0.02),
        'ln_ffn_b': nrm((DEPTH, D_MODEL), 0.02),
    }

def reference(x_prompt, x_sample, cache_ckv, cache_krope, state_lru_h, state_lru_conv, state_sconv, page_table,
              w_in, lru_conv_w, lru_conv_b, lru_gate_x_w, lru_gate_x_b, lru_gate_a_w, lru_gate_a_b, lru_lambda,
              sc_conv_w, q_norm_g, kv_norm_g, w_uq, w_uk, w_uv, w_out, ln_mix_g, ln_mix_b,
              router_group_w, router_group_b, router_expert_w, router_expert_b, w_gate, w_up, w_down,
              ln_ffn_g, ln_ffn_b):
    b_p, s_p, _ = x_prompt.shape
    b_s, s_s, _ = x_sample.shape
    past_len = page_table.shape[1] * cache_ckv.shape[2]
    pos_p = jnp.arange(s_p, dtype=jnp.int32)
    pos_s = past_len + jnp.arange(s_s, dtype=jnp.int32)
    xp, xs = x_prompt, x_sample
    ckv_p_l, kr_p_l, h_p_l, ca_p_l, cb_p_l = [], [], [], [], []
    ckv_s_l, kr_s_l, h_s_l, ca_s_l, cb_s_l = [], [], [], [], []
    for l in range(DEPTH):
        mix_w = (w_in[l], lru_conv_w[l], lru_conv_b[l], lru_gate_x_w[l], lru_gate_x_b[l],
                 lru_gate_a_w[l], lru_gate_a_b[l], lru_lambda[l], sc_conv_w[l],
                 q_norm_g[l], kv_norm_g[l], w_uq[l], w_uk[l], w_uv[l], w_out[l])
        moe_w = (router_group_w[l], router_group_b[l], router_expert_w[l], router_expert_b[l],
                 w_gate[l], w_up[l], w_down[l])
        h0_p = jnp.zeros((b_p, LRU_WIDTH), xp.dtype)
        ca0_p = jnp.zeros((b_p, LRU_CONV_W - 1, LRU_WIDTH), xp.dtype)
        cb0_p = jnp.zeros((b_p, SC_CONV_W - 1, SC_WIDTH), xp.dtype)
        yp, ckv_p, kr_p, h_p, ca_p, cb_p = hybrid_mixer(xp, pos_p, None, None, h0_p, ca0_p, cb0_p, *mix_w)
        past_ckv = cache_ckv[l][page_table].reshape(b_s, past_len, KV_LORA)
        past_kr = cache_krope[l][page_table].reshape(b_s, past_len, QK_ROPE)
        ys, ckv_s, kr_s, h_s, ca_s, cb_s = hybrid_mixer(xs, pos_s, past_ckv, past_kr, state_lru_h[l],
                                                        state_lru_conv[l], state_sconv[l], *mix_w)
        xp = layer_norm(ALPHA * xp + yp, ln_mix_g[l], ln_mix_b[l])
        xs = layer_norm(ALPHA * xs + ys, ln_mix_g[l], ln_mix_b[l])
        xp = layer_norm(ALPHA * xp + hier_moe(xp, *moe_w), ln_ffn_g[l], ln_ffn_b[l])
        xs = layer_norm(ALPHA * xs + hier_moe(xs, *moe_w), ln_ffn_g[l], ln_ffn_b[l])
        ckv_p_l.append(ckv_p); kr_p_l.append(kr_p); h_p_l.append(h_p); ca_p_l.append(ca_p); cb_p_l.append(cb_p)
        ckv_s_l.append(ckv_s); kr_s_l.append(kr_s); h_s_l.append(h_s); ca_s_l.append(ca_s); cb_s_l.append(cb_s)
    return (xp, xs,
            jnp.stack(ckv_p_l), jnp.stack(kr_p_l), jnp.stack(h_p_l), jnp.stack(ca_p_l), jnp.stack(cb_p_l),
            jnp.stack(ckv_s_l), jnp.stack(kr_s_l), jnp.stack(h_s_l), jnp.stack(ca_s_l), jnp.stack(cb_s_l))


_drawn_inputs = setup_inputs


def setup_inputs(seed=0):
    import zlib

    import numpy as np

    out = dict(_drawn_inputs(seed))
    spreads = {}
    factors = {'cache_ckv': 5.986,
     'cache_krope': 8.0,
     'lru_gate_x_b': 8.0,
     'lru_gate_a_b': 8.0,
     'q_norm_g': 8.0,
     'kv_norm_g': 2.869,
     'router_group_b': 6.62,
     'router_expert_b': 8.0}
    for name, (base, spread) in spreads.items():
        noise = np.random.default_rng([zlib.crc32(name.encode()), seed]).standard_normal(out[name].shape)
        drawn = base * np.exp(spread * noise) if base else spread * noise
        out[name] = __import__('jax').numpy.asarray(drawn.astype(out[name].dtype))
    for name, factor in factors.items():
        out[name] = (out[name] * factor).astype(out[name].dtype)
    return out
```

```python
from contextlib import ExitStack

import numpy as np

import concourse.bass as bass
from concourse import mybir

F32 = mybir.dt.float32
I32 = mybir.dt.int32
ALU = mybir.AluOpType
ACT = mybir.ActivationFunctionType
AX = mybir.AxisListType.X

P = 128
D = 1024
DEPTH = 2
SEQ = 512
NB = 8
NS = 8
NTOK = SEQ + NB * NS
TILES = 5
KC = D // P
W = 256
NH, NOPE, ROPE, VH = 8, 64, 32, 64
QK = NOPE + ROPE
QL, R = 256, 128
PAST, PAGE = 4096, 128
KEYS_ROW = 8
ROWS_PAGE = PAGE // KEYS_ROW
PAGES_CH = P // ROWS_PAGE
CHUNKS = PAST // PAGE // PAGES_CH
NE, FF = 16, 256
C = 128
SCALE = QK ** -0.5
ALPHA = (2 * DEPTH) ** 0.25
LN_EPS, RMS_EPS = 1e-5, 1e-6
MORE = (NTOK - 1) // C
OVER = 2 * NTOK // (C + 1)
SLOTS = (NE + OVER) * C
NEG = -1e30

LA = 3 + SEQ + NB * (3 + NS)
LZ = 2 + SEQ + NB * (2 + NS)
LP = 604
P_CW, P_CB, P_GXB, P_GAB, P_LAM, P_SW, P_QG, P_H0, P_CS, P_SS = 0, 4, 5, 6, 7, 8, 11, 12, 20, 44
NPAR = 60
ST_H, ST_C, ST_S, NST = 0, 9, 36, 54
C_ID, C_TRI, C_ONE, C_MASK, C_NEW, C_CS, C_SEL, C_P16, C_VAL, C_PRI, C_EC, C_GAP, C_IOTA, NCONST = np.cumsum(
    [0, 128, 128, 128, 512, 512, 160, 8, 1, 5, 4, 16, 16, 16]).tolist()

RING = 6
SLAB = KC * W
FIRST_E = 12
LOADS = [10, 9, 10, 10, 10, 10]


def rows(t):
    return P if t < 4 else NTOK - SEQ


def cols(t):
    return slice(P * t, P * t + rows(t))


def loaded(l, slot, k):
    return l * (16 * LOADS[slot]) + (k * 16 + 16)


def eload(slot, i):
    return i + (1 if slot == 1 else 2)


class Own:

    def __init__(self, eng, sem, base=0):
        self.eng, self.sem, self.base, self.n = eng, sem, base, 0

    def __call__(self, ins):
        self.n += 1
        ins.then_inc(self.sem, 1)

    def settle(self):
        self.eng.wait_ge(self.sem, self.base + self.n)

    def link(self, ins):
        self(ins)
        self.settle()


def build(nc, a, o):
    ctx = ExitStack()
    with ctx:
        def sb(name, shape, dt=F32):
            return ctx.enter_context(nc.sbuf_tensor(name, shape, dt))

        lasting = {}
        for name in ["x_loaded", "table_loaded", "const_loaded", "xs_zeroed", "arena_clear", "zero_ready",
                     "idx_base", "layer_end", "layer_go"]:
            lasting[name] = ctx.enter_context(nc.semaphore(name))
        x_loaded, table_loaded, const_loaded = (lasting[n] for n in ["x_loaded", "table_loaded", "const_loaded"])
        xs_zeroed, arena_clear, zero_ready = (lasting[n] for n in ["xs_zeroed", "arena_clear", "zero_ready"])
        idx_base, layer_end, layer_go = (lasting[n] for n in ["idx_base", "layer_end", "layer_go"])
        ring_loaded = [ctx.enter_context(nc.semaphore(f"ring_loaded{i}")) for i in range(RING)]

        kv_loaded = [ctx.enter_context(nc.semaphore(f"kv_loaded{i}")) for i in range(2 * CHUNKS)]
        scattered = ctx.enter_context(nc.semaphore("scattered"))
        g_loaded = [ctx.enter_context(nc.semaphore(f"g_loaded{i}")) for i in range(2)]

        per_layer = []

        def sem(name):
            s = ctx.enter_context(nc.semaphore(name))
            per_layer.append(s)
            return s

        dve_own, act_own = sem("dve_own"), sem("act_own")
        dve_back = sem("dve_back")
        pe_held, pool_held, sp_held = sem("pe_held"), sem("pool_held"), sem("sp_held")
        par_loaded, uq_loaded, uk_loaded, uv_loaded = sem("par_loaded"), sem("uq_loaded"), sem("uk_loaded"), sem("uv_loaded")
        gatew_loaded, rout_loaded, kvg_loaded, ln_loaded = sem("gatew_loaded"), sem("rout_loaded"), sem("kvg_loaded"), sem("ln_loaded")
        xt_made, xt_act, xt_dve = sem("xt_made"), sem("xt_act"), sem("xt_dve")
        fm_made, fm_act, fm_dve = sem("fm_made"), sem("fm_act"), sem("fm_dve")
        tm_made, tm_taken = sem("tm_made"), sem("tm_taken")
        conv_ready, gate_made, gate_taken = sem("conv_ready"), sem("gate_made"), sem("gate_taken")
        ssq_ready, rms_ready, norm_ready = sem("ssq_ready"), sem("rms_ready"), sem("norm_ready")
        kt_made, cqt_ready, ckt_ready = sem("kt_made"), sem("cqt_ready"), sem("ckt_ready")
        q_made, q_taken, q_roped = sem("q_made"), sem("q_taken"), sem("q_roped")
        qt_made, qt_act, qt_dve = sem("qt_made"), sem("qt_act"), sem("qt_dve")
        kn_made, kn_taken, v_made, v_taken, kr_ready = sem("kn_made"), sem("kn_taken"), sem("v_made"), sem("v_taken"), sem("kr_ready")
        loga_ready, expa_ready, mult2_ready, mult_ready = sem("loga_ready"), sem("expa_ready"), sem("mult2_ready"), sem("mult_ready")
        lam_exp, lam_ln = sem("lam_exp"), sem("lam_ln")
        st_ready, st_made, st_taken = sem("st_ready"), sem("st_made"), sem("st_taken")
        mixed_ab = sem("mixed_ab")
        s_made, s_taken, nm_ready, p_ready = sem("s_made"), sem("s_taken"), sem("nm_ready"), sem("p_ready")
        pt_made, pt_taken, pv_made, o_ready, ot_made, ot_taken = (
            sem("pt_made"), sem("pt_taken"), sem("pv_made"), sem("o_ready"), sem("ot_made"), sem("ot_taken"))
        ql_made, ql_taken, sn_made, sn_taken, qrb_ready, qrb_zero = (
            sem("ql_made"), sem("ql_taken"), sem("sn_made"), sem("sn_taken"), sem("qrb_ready"), sem("qrb_zero"))
        idx_ready, slot_idx = sem("idx_ready"), sem("slot_idx")
        lat_made, lat_act, lat_dve = sem("lat_made"), sem("lat_act"), sem("lat_dve")
        sc_made, sc_taken = sem("sc_made"), sem("sc_taken")
        m1_ready, mt_made, md_ready, mb_made = sem("m1_ready"), sem("mt_made"), sem("md_ready"), sem("mb_made")
        sub_ready, exp_ready, ps_ready = sem("sub_ready"), sem("exp_ready"), sem("ps_ready")
        pvl_made, sum_made, ol_taken = sem("pvl_made"), sem("sum_made"), sem("ol_taken")
        yc_made, yc_act, yc_dve = sem("yc_made"), sem("yc_act"), sem("yc_dve")
        y_made, y_taken = sem("y_made"), sem("y_taken")
        var_ready, std_ready, g_ready, x_ready = sem("var_ready"), sem("std_ready"), sem("g_ready"), sem("x_ready")
        rt_made, lg_ready, re_ready, le_ready, ree_ready = (
            sem("rt_made"), sem("lg_ready"), sem("re_ready"), sem("le_ready"), sem("ree_ready"))
        m_ready, pos_made, slots_ready = sem("m_ready"), sem("pos_made"), sem("slots_ready")
        ax_ready = sem("ax_ready")
        xe_loaded = [sem("xe_loaded0"), sem("xe_loaded1")]
        xet_made, xet_act, xet_dve = sem("xet_made"), sem("xet_act"), sem("xet_dve")
        gu_made, silu_ready, h_ready = sem("gu_made"), sem("silu_ready"), sem("h_ready")
        dn_made, ye_act, ye_dve = sem("dn_made"), sem("ye_act"), sem("ye_dve")
        ye_stored = [sem("ye_stored0"), sem("ye_stored1")]
        ov_loaded, ov_pe, ov_act, ov_dve, ov_stored, ov_done = (
            sem("ov_loaded"), sem("ov_pe"), sem("ov_act"), sem("ov_dve"), sem("ov_stored"), sem("ov_done"))
        v_used, out_stored, states_stored = sem("v_used"), sem("out_stored"), sem("states_stored")
        numbers = [s.num for s in per_layer]
        layer_range = range(min(numbers), max(numbers) + 1)
        assert len(layer_range) == len(per_layer)

        X = sb("X", [P, TILES, D])
        xt_mem = sb("xt_mem", [P, KC * NTOK])
        ring = sb("ring", [P, RING, SLAB])
        catT = sb("catT", [P, KC, NTOK])
        CKV = sb("CKV", [P, TILES, R])
        KR = sb("KR", [P, TILES, ROPE])
        CKT = sb("CKT", [P, NTOK])
        KRT = sb("KRT", [ROPE, NTOK])
        wq_mem = sb("wq_mem", [P, 2 * D])
        gatew = sb("gatew", [P, 2, 2, P])
        w_ukT = sb("w_ukT", [NOPE, NH, R])
        w_uv = sb("w_uv", [P, NH * VH])
        wr = sb("wr", [P, KC, 20])
        par = sb("par", [P, 2, NPAR])
        kvg = sb("kvg", [P, R])
        rbias = sb("rbias", [P, 20])
        const = sb("const", [P, NCONST])
        zero = sb("zero", [P, 256])
        arena = sb("arena", [P, 17800])
        small = sb("small", [P, 64])
        idx_f = sb("idx_f", [P, NB * CHUNKS])
        idx_i = sb("idx_i", [P, NB * CHUNKS], I32)
        idx_1 = sb("idx_1", [P, 2 * CHUNKS], I32)
        w12 = sb("w12", [P, 2, TILES])
        slot_i = sb("slot_i", [P, 2, TILES], I32)
        over_i = sb("over_i", [1, 1 + OVER], I32)
        PS = ctx.enter_context(nc.psum_tensor("PS", [P, 8, 512], F32))

        xT = xt_mem[:, :].rearrange("p (c t) -> p c t", c=KC)
        QTp = xt_mem[0:QK, 0:NH * SEQ].rearrange("p (h t) -> p h t", h=NH)
        QTs = xt_mem[0:QK, NH * SEQ:KC * NTOK].rearrange("p (h t) -> p h t", h=NH)
        S_sb = xt_mem[:, 0:2 * CHUNKS * 512].rearrange("p (b g c) -> p b g c", b=2, g=CHUNKS)
        w_uq = wq_mem[:, 0:2 * 768].rearrange("p (k n) -> p k n", k=2)
        w_uk = wq_mem[:, 2 * 768:2 * D]
        ln_rows = wq_mem[:, :].rearrange("p (a n) -> p a n", a=2)

        ident = const[:, C_ID:C_ID + P]
        tri = const[:, C_TRI:C_TRI + P]
        ones = const[:, C_ONE:C_ONE + P]
        mask = const[:, C_MASK:C_MASK + SEQ]
        mask_new = const[0:NB * NS, C_NEW:C_NEW + NB * NH * NS]
        cs = const[:, C_CS:C_CS + 160].rearrange("p (t n) -> p t n", t=TILES)
        sel = const[:, C_SEL:C_SEL + PAGES_CH]
        p16 = const[:, C_P16:C_P16 + 1]
        valid = const[:, C_VAL:C_VAL + TILES]
        pri = const[:, C_PRI:C_PRI + 4]
        first_slot = const[:, C_EC:C_EC + NE]
        gap = const[:, C_GAP:C_GAP + NE]
        iota = const[0:1, C_IOTA:C_IOTA + OVER]

        table = arena[:, 512:768].bitcast(I32)
        at = [0]

        def take(n):
            at[0] += n
            assert at[0] <= 17800, at[0]
            return arena[:, at[0] - n:at[0]]

        def v3(ap, k):
            return ap.rearrange("p (a b) -> p a b", a=k)

        PT = v3(take(TILES * 416), TILES)
        cqT = v3(take(2 * NTOK), 2)
        Q = v3(take(2 * 768), 2)
        at[0] = 0
        KT = v3(take(NH * SEQ)[0:QK, :], NH)
        V = v3(take(4 * NH * VH), 4)
        lru_at = at[0]
        xa_pad, z_pad, XC, SI, SR, A, U = (v3(take(2 * LP), 2) for _ in range(7))
        ZC = U
        rope_tmp = v3(take(4 * 640), 4)
        junk = take(QL)
        ST = v3(take(2 * NST), 2)
        ST2 = take(2 * P)[0:NST, :]
        at[0] = lru_at
        S2, P2, PT2 = (v3(take(2 * 512), 2) for _ in range(3))
        O2 = v3(take(2 * 512), 2)
        at[0] = 0
        latT = take(2 * KEYS_ROW * P).rearrange("p (b k n) -> p b k n", b=2, k=KEYS_ROW)
        ropT = take(2 * 2 * P).rearrange("p (b k n) -> p b k n", b=2, k=2)
        QLb = take(NB * NH * NS).rearrange("p (b h s) -> p b h s", b=NB, h=NH)
        QRB = take(NB * 4 * 64).rearrange("p (b k c) -> p b k c", b=NB, k=4)
        SN = take(NB * 64)[0:64, :]
        OLT = take(NH * 64).rearrange("p (h t) -> p h t", h=NH)
        M1, MD, PS1, PN, RS, PNs, MB = (take(n) for n in (2 * 64, P, 2 * 64, 2 * 64, 64, 64, 64))
        KV = take(2 * CHUNKS * KEYS_ROW * (R + ROPE)).rearrange("p (s n) -> p s n", s=2 * CHUNKS)
        at[0] = 0
        VV = v3(take(2 * D), 2)
        XE = v3(take(2 * D), 2)
        XET = take(2 * D).rearrange("p (b k n) -> p b k n", b=2, k=KC)
        SG = v3(take(2 * 2 * C), 2)
        HT = take(2 * 2 * C).rearrange("p (b k n) -> p b k n", b=2, k=2)
        YE = v3(take(2 * D), 2)
        G = take(4 * D).rearrange("p (b k n) -> p b k n", b=2, k=2)
        rt = take(1200)

        SSQ, RST = small[:, 0:10], small[:, 10:20]
        sp8, lam_t = small[:, 20:22], small[:, 22:26]
        MX, NM = small[:, 26:28], small[:, 28:30]
        MC = small[0:64, 30:31]
        BN = sb("BN", [P, 2, 16])
        LSUM = sb("LSUM", [P, 4, NH])
        RL = sb("RL", [P, 4, NH])
        eps = sb("eps", [P, 2])
        HS = sb("HS", [P, 2, NB])

        xs = nc.dram_tensor("xs", (SLOTS, D), F32, kind="Internal").ap()
        ys = nc.dram_tensor("ys", (SLOTS, D), F32, kind="Internal").ap()

        def slot_of(e_half, par_, k):
            return 3 * par_ + k

        def slab(slot):
            return ring[:, slot, :]

        def seg_a(buf, j, lo, n):
            return v3(buf[:, j, 3 + SEQ:LA], NB)[:, :, lo:lo + n]

        def seg_z(buf, j, lo, n):
            return v3(buf[:, j, 2 + SEQ:LZ], NB)[:, :, lo:lo + n]

        def lay(ap, l):
            sub = ap[bass.ds(l, 1)]
            names = "bcdef"[:len(ap.shape) - 1]
            return sub.rearrange(f"a {names[0]} {' '.join(names[1:])} -> (a {names[0]}) {' '.join(names[1:])}")

        def fm_free(m):
            if m < 2:
                return fm_dve, m + 1
            if m < 8:
                return fm_act, m - 1
            return fm_dve, m - 5

        block = ctx.enter_context(nc.Block())

        @block.sync
        def _(sp):
            sp.dma_start(const[:, :], a["const"]).then_inc(const_loaded, 16)
            sp.dma_start(X[:, 0:4, :], a["x_prompt"].rearrange("a (t p) d -> p (a t) d", p=P)).then_inc(x_loaded, 16)
            sp.dma_start(X[0:64, 4, :], a["x_sample"].rearrange("b s d -> (b s) d")).then_inc(x_loaded, 16)

            def w_in_load(l, n):
                sp.dma_start(slab(n % RING), lay(a["w_in"], l)[:, n, :]).then_inc(ring_loaded[n % RING], 16)

            for n in range(RING):
                w_in_load(0, n)
            sp.wait_ge(zero_ready, 1)
            sp.dma_start(xs.rearrange("(p k) (j n) -> p (k j) n", p=P, n=256),
                         zero[:, :].unsqueeze(1).to_broadcast([P, SLOTS // P * 4, 256])).then_inc(xs_zeroed, 16)
            sp.dma_start(ys[NE * C:SLOTS, :].rearrange("(p k) (j n) -> p (k j) n", p=P, n=256),
                         zero[:, :].unsqueeze(1).to_broadcast([P, OVER * C // P * 4, 256])).then_inc(xs_zeroed, 16)

            with sp.Fori(0, DEPTH) as l:
                def w_out_load(n):
                    sp.dma_start(slab(2 + n), lay(a["w_out"], l)[:, n, :]).then_inc(ring_loaded[2 + n], 16)

                def expert_load(e, slot, k):
                    src = lay(a[["w_gate", "w_up", "w_down"][k]], l)[bass.ds(e, 1)]
                    if k < 2:
                        src = src.rearrange("e (p c) f -> (e p) (c f)", c=KC)
                        sp.dma_start(slab(slot), src).then_inc(ring_loaded[slot], 16)
                    else:
                        src = src.rearrange("e (k p) d -> p (e k) d", p=P)
                        sp.dma_start(v3(slab(slot), 2), src).then_inc(ring_loaded[slot], 16)

                sp.wait_ge(fm_made, 2)
                sp.dma_start(slab(0), lay(a["w_in"], l)[:, 6, :]).then_inc(ring_loaded[0], 16)
                sp.wait_ge(fm_made, 4)
                expert_load(0, 1, 1)
                for n in range(3):
                    sp.wait_ge(fm_made, 6 + 2 * n)
                    w_out_load(n)
                sp.wait_ge(tm_made, TILES)
                w_out_load(3)
                expert_load(0, 0, 0)
                sp.wait_ge(norm_ready, TILES + 1)
                sp.dma_start(lay(o["ckv_p"], l).rearrange("b (t p) r -> p (b t) r", p=P), CKV[:, 0:4, :]).then_inc(out_stored, 16)
                sp.dma_start(lay(o["kr_p"], l).rearrange("b (t p) r -> p (b t) r", p=P), KR[:, 0:4, :]).then_inc(out_stored, 16)
                sp.dma_start(lay(o["ckv_s"], l).rearrange("b s r -> (b s) r"), CKV[0:64, 4, :]).then_inc(out_stored, 16)
                sp.dma_start(lay(o["kr_s"], l).rearrange("b s r -> (b s) r"), KR[0:64, 4, :]).then_inc(out_stored, 16)
                sp.wait_ge(kn_made, NH)
                sp.dma_start(ln_rows, lay(a["ln_mix"], l).partition_broadcast(P)).then_inc(ln_loaded, 16)
                sp.wait_ge(st_taken, 1)
                for name, at0, n in [("h_p", ST_H, 1), ("h_s", ST_H + 1, NB), ("ca_p", ST_C, 3), ("ca_s", ST_C + 3, 3 * NB),
                                     ("cb_p", ST_S, 2), ("cb_s", ST_S + 2, 2 * NB)]:
                    dst = lay(o[name], l)
                    if len(dst.shape) == 3:
                        dst = dst.rearrange("b k w -> (b k) w")
                    sp.dma_start(dst, ST2[at0:at0 + n, :]).then_inc(out_stored, 16)
                sp.wait_ge(out_stored, 16 * 10)
                sp.sem_inc(states_stored, 1)
                sp.wait_ge(y_made, TILES)
                expert_load(0, 2, 2)
                for k in range(3):
                    expert_load(1, 3 + k, k)
                sp.wait_ge(x_ready, TILES)
                sp.dma_start(ln_rows, lay(a["ln_ffn"], l).partition_broadcast(P)).then_inc(ln_loaded, 16)

                def xe_load(e, q):
                    sp.dma_start(XE[:, q, :], xs.rearrange("(e s) d -> e s d", s=C)[bass.ds(e, 1)].rearrange("e s d -> (e s) d")
                                 ).then_inc(xe_loaded[q], 16)

                def ye_store(e, q):
                    sp.wait_ge(ye_act, e + 1)
                    sp.wait_ge(ye_dve, e + 1)
                    sp.sem_inc(sp_held, 1)
                    sp.dma_start(ys.rearrange("(e s) d -> e s d", s=C)[bass.ds(e, 1)].rearrange("e s d -> (e s) d"),
                                 YE[:, q, :]).then_inc(ye_stored[q], 16)

                def moe_step(e, q, load_x=True, load_gu=True, load_dn=True):
                    if load_x:
                        sp.wait_ge(xet_made, 2 * e + 2)
                        sp.sem_inc(sp_held, 1)
                        xe_load(e + 2, q)
                    if load_gu:
                        sp.wait_ge(gu_made, e + 1)
                        sp.sem_inc(sp_held, 1)
                        for k in range(2):
                            expert_load(e + 2, 3 * q + k, k)
                    if load_dn:
                        sp.wait_ge(dn_made, 2 * e)
                        sp.sem_inc(sp_held, 1)
                        expert_load(e + 1, 3 * (1 - q) + 2, 2)
                    ye_store(e - 1, 1 - q)

                sp.wait_ge(scattered, l * (16 * 2 * TILES) + 16 * 2 * TILES)
                xe_load(0, 0)
                xe_load(1, 1)
                sp.wait_ge(xet_made, 2)
                xe_load(2, 0)
                sp.wait_ge(gu_made, 1)
                for k in range(2):
                    expert_load(2, k, k)
                with sp.Fori(0, 6) as i:
                    moe_step(2 * i + 1, 1)
                    moe_step(2 * i + 2, 0)
                moe_step(13, 1)
                moe_step(14, 0, load_x=False, load_gu=False)
                ye_store(14, 0)
                ye_store(15, 1)
                for q in range(2):
                    sp.wait_ge(ye_stored[q], 16 * NE // 2)

                n_over = sp.value_load(over_i[0:1, 0:1], min_val=0, max_val=OVER)
                with sp.If(n_over > 0):
                    with sp.Fori(0, n_over) as i:
                        e = sp.value_load(over_i[0:1, bass.ds(i + 1, 1)], min_val=0, max_val=NE - 1)
                        for k in range(2):
                            src = lay(a[["w_gate", "w_up"][k]], l)[bass.ds(e, 1)].rearrange("e (p c) f -> (e p) (c f)", c=KC)
                            sp.dma_start(slab(k), src).then_inc(ov_loaded, 16)
                        src = lay(a["w_down"], l)[bass.ds(e, 1)].rearrange("e (k p) d -> p (e k) d", p=P)
                        sp.dma_start(v3(slab(2), 2), src).then_inc(ov_loaded, 16)
                        view = xs.rearrange("(e s) d -> e s d", s=C)[bass.ds(i + NE, 1)].rearrange("e s d -> (e s) d")
                        sp.dma_start(XE[:, 0, :], view).then_inc(ov_loaded, 16)
                        sp.wait_ge(ov_act, 3 * i + 3)
                        sp.wait_ge(ov_dve, 3 * i + 3)
                        sp.sem_inc(sp_held, 1)
                        view = ys.rearrange("(e s) d -> e s d", s=C)[bass.ds(i + NE, 1)].rearrange("e s d -> (e s) d")
                        sp.dma_start(view, YE[:, 0, :]).then_inc(ov_stored, 16)
                        sp.wait_ge(ov_stored, i * 16 + 16)
                        sp.sem_inc(sp_held, 1)
                sp.sem_inc(ov_done, 1)

                with sp.If(l < DEPTH - 1):
                    for n in range(RING):
                        w_in_load((l + 1) % DEPTH, n)
                sp.wait_ge(x_ready, 2 * TILES)
                sp.sem_inc(layer_end, 1)
                sp.wait_ge(layer_go, l + 1)
                sp.sem_inc(sp_held, 1)

            sp.dma_start(o["y_p"].rearrange("a (t p) d -> p (a t) d", p=P), X[:, 0:4, :]).then_inc(x_loaded, 16)
            sp.dma_start(o["y_s"].rearrange("b s d -> (b s) d"), X[0:64, 4, :]).then_inc(x_loaded, 16)
            sp.wait_ge(x_loaded, 64)

        @block.gpsimd
        def _(pool):
            pool.memset(zero[:, :], 0.0).then_inc(zero_ready, 1)
            pool.memset(arena[:, :], 0.0).then_inc(arena_clear, 1)
            pool.wait_ge(arena_clear, 1)
            pool.dma_start(table, a["page_table"].partition_broadcast(P)).then_inc(table_loaded, 16)

            with pool.Fori(0, DEPTH) as l:
                pool.wait_ge(ot_taken, 4)
                pool.wait_ge(pt_made, 4 * NH)
                pool.wait_ge(states_stored, 1)
                pool.memset(QRB, 0.0).then_inc(qrb_zero, 1)

                def gather(b, q, g):
                    s = CHUNKS * q + g
                    pool.tensor_copy(idx_1[:, s:s + 1], idx_i[:, bass.ds(b * CHUNKS + g, 1)]).then_inc(slot_idx, 1)
                    pool.wait_ge(slot_idx, b * CHUNKS + g + 1)
                    pool.sem_inc(pool_held, 1)
                    pool.indirect_dma_start(out=KV[:, s, :], out_offset=None, in_=a["cache"],
                                            in_offset=bass.IndirectOffsetOnAxis(ap=idx_1[:, s:s + 1], axis=0)
                                            ).then_inc(kv_loaded[s], 16)

                pool.wait_ge(idx_ready, 1)
                for b in range(2):
                    for g in range(CHUNKS):
                        gather(b, b, g)
                with pool.Fori(0, NB // 2 - 1) as i:
                    for q in range(2):
                        for g in range(CHUNKS):
                            pool.wait_ge(pvl_made, (2 * i + q) * CHUNKS + g + 1)
                            gather(2 * i + 2 + q, q, g)

                for t in range(TILES):
                    pool.wait_ge(g_ready, t + 1)
                    pool.tensor_tensor(X[0:rows(t), t, :], X[0:rows(t), t, :], ln_rows[0:rows(t), 1, :], ALU.add
                                       ).then_inc(x_ready, 1)

                pool.wait_ge(slots_ready, 1)
                pool.wait_ge(xs_zeroed, 32)
                pool.wait_ge(x_ready, TILES)
                for t in range(TILES):
                    for k in range(2):
                        pool.indirect_dma_start(out=xs, out_offset=bass.IndirectOffsetOnAxis(ap=slot_i[0:rows(t), k, t:t + 1], axis=0),
                                                in_=X[0:rows(t), t, :], in_offset=None).then_inc(scattered, 16)
                pool.wait_ge(ov_done, 1)
                for t in range(TILES):
                    if t >= 2:
                        pool.wait_ge(v_used, t - 1)
                    for k in range(2):
                        pool.indirect_dma_start(out=G[0:rows(t), t % 2, k, :], out_offset=None, in_=ys,
                                                in_offset=bass.IndirectOffsetOnAxis(ap=slot_i[0:rows(t), k, t:t + 1], axis=0)
                                                ).then_inc(g_loaded[t % 2], 16)
                for t in range(TILES):
                    pool.wait_ge(g_ready, TILES + t + 1)
                    pool.tensor_tensor(X[0:rows(t), t, :], X[0:rows(t), t, :], ln_rows[0:rows(t), 1, :], ALU.add
                                       ).then_inc(x_ready, 1)
                pool.wait_ge(x_ready, 2 * TILES)
                pool.wait_ge(layer_end, l * 4 + 4)
                pool.sem_inc(pool_held, 1)
                pool.drain()
                pool.sem_clear(layer_range)
                pool.sem_inc(layer_go, 1)

        @block.scalar
        def _(act):
            act.wait_ge(const_loaded, 16)
            with act.Fori(0, DEPTH) as l:
                own = Own(act, act_own)
                act.dma_start(par[:, :, :], lay(a["par"], l)).then_inc(par_loaded, 16)
                act.dma_start(gatew[:, :, :, :], lay(a["gatew"], l)).then_inc(gatew_loaded, 16)
                act.dma_start(kvg[:, :], lay(a["kvg"], l).partition_broadcast(P)).then_inc(kvg_loaded, 16)
                act.dma_start(w_uq, lay(a["w_uq"], l).rearrange("(k p) n -> p k n", p=P)).then_inc(uq_loaded, 16)
                act.dma_start(w_uk, lay(a["w_uk"], l)).then_inc(uk_loaded, 16)
                act.dma_start(w_ukT[:, :, :], lay(a["w_ukT"], l)).then_inc(uk_loaded, 16)
                act.dma_start(w_uv[:, :], lay(a["w_uv"], l)).then_inc(uv_loaded, 16)
                act.dma_start(wr[:, :, :], lay(a["wr"], l)).then_inc(rout_loaded, 16)
                act.dma_start(rbias[:, :], lay(a["rbias"], l).partition_broadcast(P)).then_inc(rout_loaded, 16)

                def xt_copy(n):
                    for t in range(TILES):
                        act.wait_ge(xt_made, 10 * n + 2 * t + 1)
                        act.activation(xT[:, 0:4, cols(t)], v3(PS[:, 4 * n + (2 * t) % 4, :], 4)[:, :, 0:rows(t)], ACT.Copy
                                       ).then_inc(xt_act, 1)

                xt_copy(0)
                for m in range(2, 8):
                    act.wait_ge(fm_made, m + 1)
                    j = m % 2
                    if m < 6:
                        f = ACT.Gelu_apprx_tanh if m < 4 else ACT.Copy
                        act.activation(catT[:, m - 2, 0:SEQ], PS[:, m % 2, :], f)
                        act.activation(catT[:, m - 2, SEQ:NTOK], PS[:, 2 + m % 2, 0:64], f).then_inc(fm_act, 1)
                    else:
                        if m == 6:
                            act.wait_ge(arena_clear, 1)
                        act.activation(z_pad[:, j, 2:2 + SEQ], PS[:, m % 2, :], ACT.Copy)
                        act.activation(seg_z(z_pad, j, 2, NS), v3(PS[:, 2 + m % 2, 0:64], NB), ACT.Copy).then_inc(fm_act, 1)
                for t in range(TILES):
                    act.wait_ge(tm_made, t + 1)
                    act.activation(PT[0:rows(t), t, :], PS[0:rows(t), 4 + t % 4, 0:416], ACT.Copy).then_inc(tm_taken, 1)
                act.wait_ge(par_loaded, 16)
                for g in range(2):
                    for j in range(2):
                        n = 2 * g + j
                        act.wait_ge(gate_made, n + 1)
                        dst, bias = (SI, SR)[g], par[:, j, P_GXB + g:P_GXB + g + 1]
                        act.activation(dst[:, j, 0:512], PS[:, n % 2, :], ACT.Sigmoid, bias=bias)
                        act.activation(dst[:, j, 512:600], PS[:, 2 + n % 2, 0:88], ACT.Sigmoid, bias=bias).then_inc(gate_taken, 1)
                act.wait_ge(ssq_ready, 1)
                act.activation(RST, SSQ, ACT.Sqrt, bias=eps[:, 0:1]).then_inc(rms_ready, 1)
                for t in range(TILES):
                    act.wait_ge(kt_made, t + 1)
                    for k in range(2):
                        ins = act.activation(cqT[:, k, cols(t)], PS[:, t % 2, P * k:P * k + rows(t)], ACT.Identity,
                                             scale=par[:, k, P_QG:P_QG + 1])
                    ins.then_inc(cqt_ready, 1)
                act.wait_ge(lam_exp, 1)
                own.link(act.activation(lam_t[:, 0:2], lam_t[:, 0:2], ACT.Exp))
                act.activation(lam_t[:, 0:2], lam_t[:, 0:2], ACT.Ln, bias=1.0).then_inc(lam_ln, 1)

                def qt_copy(t):
                    act.wait_ge(qt_made, 2 * t + 1)
                    src = v3(PS[0:QK, 2, :], 4)[:, :, 0:rows(t)]
                    dst = QTp[:, 0:4, cols(t)] if t < 4 else QTs[:, 0:4, :]
                    act.activation(dst, src, ACT.Copy).then_inc(qt_act, 1)

                for t in range(TILES):
                    act.wait_ge(q_made, t + 1)
                    if t >= 2:
                        act.wait_ge(qt_made, 2 * t - 2)
                    act.activation(Q[0:rows(t), t % 2, 0:512], PS[0:rows(t), 4 + 2 * (t % 2), :], ACT.Copy)
                    act.activation(Q[0:rows(t), t % 2, 512:768], PS[0:rows(t), 5 + 2 * (t % 2), 0:256], ACT.Copy
                                   ).then_inc(q_taken, 1)
                    if t >= 1:
                        qt_copy(t - 1)
                qt_copy(4)
                for h in range(NH):
                    act.wait_ge(kn_made, h + 1)
                    act.activation(KT[0:NOPE, h, :], PS[0:NOPE, h % 2, :], ACT.Copy).then_inc(kn_taken, 1)
                act.wait_ge(loga_ready, 1)
                act.activation(A[:, :, 0:600], SR[:, :, 0:600], ACT.Exp)
                act.activation(U[:, :, 0:600], SR[:, :, 0:600], ACT.Tanh, scale=-1.0).then_inc(expa_ready, 1)
                act.wait_ge(mult2_ready, 1)
                act.activation(U[:, :, 0:600], SR[:, :, 0:600], ACT.Sqrt).then_inc(mult_ready, 1)
                act.wait_ge(st_made, 1)
                act.activation(ST2, PS[0:NST, 2, 0:2 * P], ACT.Copy).then_inc(st_taken, 1)

                def ot_copy(qb):
                    act.wait_ge(ot_made, qb + 1)
                    act.activation(catT[:, 4:8, P * qb:P * qb + P], v3(PS[:, 6 + qb % 2, :], 4), ACT.Copy).then_inc(ot_taken, 1)

                for i in range(4 * NH):
                    qb, h = i // NH, i % NH
                    nk = P * (qb + 1)
                    act.wait_ge(nm_ready, i + 1)
                    if i >= 2:
                        act.wait_ge(pt_made, i - 1)
                    act.activation(P2[:, i % 2, 0:nk], S2[:, i % 2, 0:nk], ACT.Exp, bias=NM[:, i % 2:i % 2 + 1], scale=SCALE,
                                   accum_out=LSUM[:, qb, h:h + 1]).then_inc(p_ready, 1)
                    if h == 3 and qb > 0:
                        ot_copy(qb - 1)
                ot_copy(3)

                def lat_copy(b, g):
                    n = b * CHUNKS + g
                    act.wait_ge(lat_made, n * 3 + 1)
                    act.activation(latT[:, g % 2, 0:4, :], v3(PS[:, 2 * (g % 2), :], 4), ACT.Copy).then_inc(lat_act, 1)
                    act.wait_ge(lat_made, n * 3 + 3)
                    act.activation(ropT[:, g % 2, :, :], v3(PS[:, 4, 0:256], 2), ACT.Copy
                                   ).then_inc(lat_act, 1)

                def sc_copy(b, q, g):
                    act.wait_ge(sc_made, b * CHUNKS + g + 1)
                    act.activation(S_sb[:, q, g, :], PS[:, 5 + g % 2, :], ACT.Copy).then_inc(sc_taken, 1)

                def exps(b, q):
                    for g in range(CHUNKS):
                        act.wait_ge(sub_ready, b * (CHUNKS + 1) + g + 1)
                        act.activation(S_sb[:, q, g, :], S_sb[:, q, g, :], ACT.Exp, scale=SCALE).then_inc(exp_ready, 1)
                    act.wait_ge(sub_ready, b * (CHUNKS + 1) + CHUNKS + 1)
                    act.activation(PN[0:64, 64 * q:64 * q + 64], PNs[0:64, :], ACT.Exp, scale=SCALE).then_inc(exp_ready, 1)

                def step(b, q, back=True):
                    lat_copy(b, 0)
                    lat_copy(b, 1)
                    sc_copy(b, q, 0)
                    lat_copy(b, 2)
                    sc_copy(b, q, 1)
                    lat_copy(b, 3)
                    sc_copy(b, q, 2)
                    if back:
                        exps(b - 1, 1 - q)
                    sc_copy(b, q, 3)

                step(0, 0, back=False)
                with act.Fori(0, NB // 2 - 1) as i:
                    step(2 * i + 1, 1)
                    step(2 * i + 2, 0)
                step(NB - 1, 1)
                exps(NB - 1, 1)
                act.wait_ge(yc_made, 1)
                act.activation(catT[0:64, 4:8, SEQ:NTOK], v3(PS[0:64, 0, 0:256], 4), ACT.Copy).then_inc(yc_act, 1)

                def stds(n):
                    for t in range(TILES):
                        r = rows(t)
                        act.wait_ge(var_ready, n * TILES + t + 1)
                        act.activation(BN[0:r, t % 2, 14:15], BN[0:r, t % 2, 13:14], ACT.Sqrt, bias=eps[0:r, 1:2]
                                       ).then_inc(std_ready, 1)

                stds(0)
                xt_copy(1)
                act.wait_ge(lg_ready, 1)
                act.activation(rt[:, 100:120], rt[:, 100:120], ACT.Exp).then_inc(re_ready, 1)
                act.wait_ge(le_ready, 1)
                act.activation(rt[:, 240:260], rt[:, 240:260], ACT.Exp).then_inc(ree_ready, 1)
                act.wait_ge(scattered, l * (16 * 2 * TILES) + 16 * 2 * TILES)
                act.activation(X[:, 0:4, :], X[:, 0:4, :], ACT.Copy, scale=ALPHA)
                act.activation(X[0:64, 4, :], X[0:64, 4, :], ACT.Copy, scale=ALPHA).then_inc(ax_ready, 1)

                def xet_copy(e, q):
                    act.wait_ge(xet_made, 2 * e + 1)
                    act.activation(XET[:, q, 0:4, :], v3(PS[:, 0, :], 4), ACT.Copy).then_inc(xet_act, 1)

                def silu(e, q):
                    act.wait_ge(gu_made, e + 1)
                    act.activation(SG[:, q, :], PS[:, 2 + q, 0:2 * C], ACT.Silu).then_inc(silu_ready, 1)

                def ye_copy(e, q, wait_store):
                    act.wait_ge(dn_made, 2 * e + 1)
                    if wait_store is not None:
                        act.wait_ge(ye_stored[q], wait_store)
                    act.activation(YE[:, q, 0:512], PS[:, 4 + 2 * q, :], ACT.Copy).then_inc(ye_act, 1)

                xet_copy(0, 0)
                silu(0, 0)
                xet_copy(1, 1)
                silu(1, 1)
                xet_copy(2, 0)
                ye_copy(0, 0, None)
                silu(2, 0)
                xet_copy(3, 1)
                ye_copy(1, 1, None)
                with act.Fori(0, 6) as i:
                    for q in range(2):
                        silu(2 * i + 3 + q, 1 - q)
                        xet_copy(2 * i + 4 + q, q)
                        ye_copy(2 * i + 2 + q, q, i * 16 + 16)
                silu(15, 1)
                ye_copy(14, 0, 16 * 7)
                ye_copy(15, 1, 16 * 7)

                n_over = act.value_load(over_i[0:1, 0:1], min_val=0, max_val=OVER)
                with act.If(n_over > 0):
                    with act.Fori(0, n_over) as i:
                        act.wait_ge(ov_pe, 3 * i + 1)
                        act.activation(XET[:, 0, 0:4, :], v3(PS[:, 0, :], 4), ACT.Copy).then_inc(ov_act, 1)
                        act.wait_ge(ov_pe, 3 * i + 2)
                        act.activation(SG[:, 0, :], PS[:, 2, 0:2 * C], ACT.Silu).then_inc(ov_act, 1)
                        act.wait_ge(ov_pe, 3 * i + 3)
                        act.wait_ge(ye_stored[0], 16 * NE // 2)
                        act.activation(YE[:, 0, 0:512], PS[:, 4, :], ACT.Copy).then_inc(ov_act, 1)

                stds(1)
                act.drain()
                act.sem_inc(layer_end, 1)
                act.wait_ge(layer_go, l + 1)

        @block.vector
        def _(dve):
            dve.memset(eps[:, 0:1], RMS_EPS).then_inc(idx_base, 1)
            dve.memset(eps[:, 1:2], LN_EPS).then_inc(idx_base, 1)
            dve.memset(small[:, :], 1.0).then_inc(idx_base, 1)
            dve.wait_ge(const_loaded, 16)
            dve.wait_ge(table_loaded, 16)
            dve.wait_ge(arena_clear, 1)
            pages = v3(arena[:, 0:256], NB * CHUNKS)
            dve.tensor_tensor(pages, v3(table, NB * CHUNKS), sel.unsqueeze(1).to_broadcast([P, NB * CHUNKS, PAGES_CH]),
                              ALU.mult).then_inc(idx_base, 1)
            dve.wait_ge(idx_base, 4)
            dve.tensor_reduce(idx_f[:, :], pages, AX, ALU.add).then_inc(idx_base, 1)
            dve.wait_ge(idx_base, 5)
            dve.tensor_scalar(idx_f[:, :], idx_f[:, :], float(ROWS_PAGE), p16, ALU.mult, ALU.add).then_inc(idx_base, 1)
            dve.wait_ge(idx_base, 6)
            layer_rows = float(a["cache"].shape[0] // DEPTH)

            with dve.Fori(0, DEPTH) as l:
                own = Own(dve, dve_own)

                def xt_copy(n):
                    for t in range(TILES):
                        dve.wait_ge(xt_made, 10 * n + 2 * t + 2)
                        dve.tensor_copy(xT[:, 4:8, cols(t)], v3(PS[:, 4 * n + (2 * t + 1) % 4, :], 4)[:, :, 0:rows(t)]
                                        ).then_inc(xt_dve, 1)

                dve.tensor_copy(idx_i[:, :], idx_f[:, :]).then_inc(idx_ready, 1)
                dve.wait_ge(idx_ready, 1)
                own(dve.tensor_scalar(idx_f[:, :], idx_f[:, :], layer_rows, None, ALU.add))
                dve.wait_ge(par_loaded, 16)
                own(dve.memset(xa_pad[:, :, 0:3], 0.0))
                own(dve.memset(z_pad[:, :, 0:2], 0.0))
                for j in range(2):
                    own(dve.tensor_copy(seg_a(xa_pad, j, 0, 3), v3(par[:, j, P_CS:P_CS + 3 * NB], NB)))
                    own(dve.tensor_copy(seg_z(z_pad, j, 0, 2), v3(par[:, j, P_SS:P_SS + 2 * NB], NB)))
                own.link(dve.tensor_scalar(lam_t[:, 2:4], par[:, :, P_LAM], -1.0, None, ALU.mult))
                dve.tensor_tensor(lam_t[:, 0:2], lam_t[:, 2:4], par[:, :, P_LAM], ALU.min).then_inc(lam_exp, 1)
                xt_copy(0)
                for j in range(2):
                    dve.wait_ge(fm_made, j + 1)
                    dve.tensor_copy(xa_pad[:, j, 3:3 + SEQ], PS[:, j, :])
                    dve.tensor_copy(seg_a(xa_pad, j, 3, NS), v3(PS[:, 2 + j, 0:64], NB)).then_inc(fm_dve, 1)
                dve.wait_ge(fm_dve, 2)
                own.settle()
                n = LA - 3
                for j in range(2):
                    own.link(dve.tensor_scalar(XC[:, j, 0:n], xa_pad[:, j, 0:n], par[:, j, P_CW:P_CW + 1],
                                               par[:, j, P_CB:P_CB + 1], ALU.mult, ALU.add))
                    for k in range(1, 4):
                        ins = dve.scalar_tensor_tensor(out=XC[:, j, 0:n], in0=xa_pad[:, j, k:k + n], scalar=par[:, j, P_CW + k:P_CW + k + 1],
                                                       in1=XC[:, j, 0:n], op0=ALU.mult, op1=ALU.add)
                        if k < 3:
                            own.link(ins)
                        else:
                            ins.then_inc(conv_ready, 1)
                dve.wait_ge(fm_act, 6)
                for j in range(2):
                    dve.wait_ge(fm_made, 9 + j)
                    dve.tensor_tensor(z_pad[:, j, 2:2 + SEQ], z_pad[:, j, 2:2 + SEQ], PS[:, j, :], ALU.mult)
                    dve.tensor_tensor(seg_z(z_pad, j, 2, NS), seg_z(z_pad, j, 2, NS), v3(PS[:, 2 + j, 0:64], NB), ALU.mult
                                      ).then_inc(fm_dve, 1)
                dve.wait_ge(fm_dve, 4)
                n = LZ - 2
                for j in range(2):
                    own.link(dve.tensor_scalar(ZC[:, j, 0:n], z_pad[:, j, 0:n], par[:, j, P_SW:P_SW + 1], None, ALU.mult))
                    for k in range(1, 3):
                        own.link(dve.scalar_tensor_tensor(out=ZC[:, j, 0:n], in0=z_pad[:, j, k:k + n],
                                                          scalar=par[:, j, P_SW + k:P_SW + k + 1], in1=ZC[:, j, 0:n],
                                                          op0=ALU.mult, op1=ALU.add))
                    own(dve.tensor_tensor(catT[:, 2 + j, 0:SEQ], catT[:, 2 + j, 0:SEQ], ZC[:, j, 0:SEQ], ALU.mult))
                    own(dve.tensor_tensor(v3(catT[:, 2 + j, SEQ:NTOK], NB), v3(catT[:, 2 + j, SEQ:NTOK], NB),
                                          seg_z(ZC, j, 0, NS), ALU.mult))

                for t in range(TILES):
                    r = rows(t)
                    dve.wait_ge(tm_taken, t + 1)
                    for k, (lo, n) in enumerate([(0, QL), (QL, R)]):
                        own.link(dve.tensor_tensor_reduce(out=junk[0:r, 0:n], in0=PT[0:r, t, lo:lo + n], in1=PT[0:r, t, lo:lo + n],
                                                          scale=1.0 / n, scalar=0.0, op0=ALU.mult, op1=ALU.add,
                                                          accum_out=SSQ[0:r, 2 * t + k:2 * t + k + 1]))
                dve.sem_inc(ssq_ready, 1)
                cos = cs[:, :, 0:16]
                sin = cs[:, :, 16:32]
                x1, x2 = PT[:, :, 384:400], PT[:, :, 400:416]
                r4 = [v3(rope_tmp[:, k, 0:80], TILES) for k in range(4)]
                own(dve.tensor_tensor(r4[0], x1, cos, ALU.mult))
                own(dve.tensor_tensor(r4[1], x2, sin, ALU.mult))
                own(dve.tensor_tensor(r4[2], x1, sin, ALU.mult))
                own.link(dve.tensor_tensor(r4[3], x2, cos, ALU.mult))
                own(dve.tensor_tensor(KR[:, :, 0:16], r4[0], r4[1], ALU.subtract))
                own.link(dve.tensor_tensor(KR[:, :, 16:32], r4[2], r4[3], ALU.add))
                dve.wait_ge(rms_ready, 1)
                dve.wait_ge(kvg_loaded, 16)
                own.link(dve.reciprocal(RST, RST))
                for t in range(TILES):
                    r = rows(t)
                    own(dve.tensor_scalar(PT[0:r, t, 0:QL], PT[0:r, t, 0:QL], RST[0:r, 2 * t:2 * t + 1], None, ALU.mult))
                    dve.scalar_tensor_tensor(out=CKV[0:r, t, :], in0=PT[0:r, t, QL:QL + R], scalar=RST[0:r, 2 * t + 1:2 * t + 2],
                                             in1=kvg[0:r, :], op0=ALU.mult, op1=ALU.mult).then_inc(norm_ready, 1)
                own.settle()
                dve.sem_inc(norm_ready, 1)
                for t in range(TILES):
                    r = rows(t)
                    dve.wait_ge(kt_made, t + 1)
                    dve.tensor_copy(CKT[:, cols(t)], PS[:, 2 + t % 2, 0:r])
                    dve.tensor_copy(KRT[:, cols(t)], PS[0:ROPE, 2 + t % 2, P:P + r]).then_inc(ckt_ready, 1)

                def qt_copy(t):
                    dve.wait_ge(qt_made, 2 * t + 2)
                    src = v3(PS[0:QK, 3, :], 4)[:, :, 0:rows(t)]
                    dst = QTp[:, 4:8, cols(t)] if t < 4 else QTs[:, 4:8, :]
                    dve.tensor_copy(dst, src).then_inc(qt_dve, 1)

                for t in range(TILES):
                    r = rows(t)
                    dve.wait_ge(q_taken, t + 1)
                    qv = v3(Q[0:r, t % 2, :], NH)
                    x1, x2 = qv[:, :, 64:80], qv[:, :, 80:96]
                    cb = cs[0:r, t, 0:16].unsqueeze(1).to_broadcast([r, NH, 16])
                    sn_ = cs[0:r, t, 16:32].unsqueeze(1).to_broadcast([r, NH, 16])
                    r4 = [v3(rope_tmp[0:r, k, 0:128], NH) for k in range(4)]
                    own.settle()
                    own(dve.tensor_tensor(r4[0], x1, cb, ALU.mult))
                    own(dve.tensor_tensor(r4[1], x2, sn_, ALU.mult))
                    own(dve.tensor_tensor(r4[2], x1, sn_, ALU.mult))
                    own.link(dve.tensor_tensor(r4[3], x2, cb, ALU.mult))
                    own(dve.tensor_tensor(x1, r4[0], r4[1], ALU.subtract))
                    dve.tensor_tensor(x2, r4[2], r4[3], ALU.add).then_inc(q_roped, 1)
                    dve.wait_ge(q_roped, t + 1)
                    if t >= 1:
                        qt_copy(t - 1)
                qt_copy(4)
                own.settle()
                dve.tensor_copy(KT[NOPE:QK, :, :], KRT[:, 0:SEQ].unsqueeze(1).to_broadcast([ROPE, NH, SEQ])).then_inc(kr_ready, 1)
                dve.wait_ge(lam_ln, 1)
                own.link(dve.scalar_tensor_tensor(out=sp8, in0=lam_t[:, 2:4], scalar=0.0, in1=lam_t[:, 0:2], op0=ALU.max, op1=ALU.add))
                own.link(dve.tensor_scalar(sp8, sp8, -8.0, None, ALU.mult))
                dve.wait_ge(gate_taken, 4)
                own(dve.tensor_scalar(SR[:, 0, 0:600], SR[:, 0, 0:600], sp8[:, 0:1], None, ALU.mult))
                own.link(dve.tensor_scalar(SR[:, 1, 0:600], SR[:, 1, 0:600], sp8[:, 1:2], None, ALU.mult))
                dve.sem_inc(loga_ready, 1)
                own.link(dve.tensor_tensor(SI[:, :, 0:600], SI[:, :, 0:600], XC[:, :, 0:600], ALU.mult))
                dve.wait_ge(expa_ready, 1)
                own.link(dve.tensor_scalar(SR[:, :, 0:600], U[:, :, 0:600], 1.0, None, ALU.add))
                own.link(dve.reciprocal(SR[:, :, 0:600], SR[:, :, 0:600]))
                dve.scalar_tensor_tensor(out=SR[:, :, 0:600], in0=U[:, :, 0:600], scalar=2.0, in1=SR[:, :, 0:600],
                                         op0=ALU.mult, op1=ALU.mult).then_inc(mult2_ready, 1)
                for t in range(4):
                    dve.wait_ge(v_made, t + 1)
                    dve.tensor_copy(V[:, t, :], PS[:, 4 + t, :]).then_inc(v_taken, 1)
                dve.wait_ge(mult_ready, 1)
                own.link(dve.tensor_tensor(SI[:, :, 0:600], SI[:, :, 0:600], U[:, :, 0:600], ALU.mult))
                for j in range(2):
                    fa, fb = seg_a(A, j, 0, 1), seg_a(SI, j, 0, 1)
                    own.link(dve.tensor_tensor(HS[:, j, :].unsqueeze(2), fa, par[:, j, P_H0:P_H0 + NB].unsqueeze(2), ALU.mult))
                    own(dve.tensor_tensor(fb, fb, HS[:, j, :].unsqueeze(2), ALU.add))
                    own.link(dve.memset(fa, 0.0))
                    own.link(dve.tensor_tensor_scan(XC[:, j, 0:600], A[:, j, 0:600], SI[:, j, 0:600], 0.0, ALU.mult, ALU.add))
                    own(dve.tensor_tensor(catT[:, j, 0:SEQ], catT[:, j, 0:SEQ], XC[:, j, 0:SEQ], ALU.mult))
                    own(dve.tensor_tensor(v3(catT[:, j, SEQ:NTOK], NB), v3(catT[:, j, SEQ:NTOK], NB), seg_a(XC, j, 0, NS), ALU.mult))
                    own(dve.tensor_copy(ST[:, j, 0:1], XC[:, j, SEQ - 1:SEQ]))
                    own(dve.tensor_copy(ST[:, j, 1:9].unsqueeze(2), seg_a(XC, j, NS - 1, 1)))
                    own(dve.tensor_copy(ST[:, j, ST_C:ST_C + 3], xa_pad[:, j, SEQ:SEQ + 3]))
                    own(dve.tensor_copy(v3(ST[:, j, ST_C + 3:ST_S], NB), seg_a(xa_pad, j, NS, 3)))
                    own(dve.tensor_copy(ST[:, j, ST_S:ST_S + 2], z_pad[:, j, SEQ:SEQ + 2]))
                    own(dve.tensor_copy(v3(ST[:, j, ST_S + 2:NST], NB), seg_z(z_pad, j, NS, 2)))
                own.settle()
                dve.sem_inc(st_ready, 1)
                dve.wait_ge(st_made, 1)

                def pt_copy(i):
                    n = i // NH + 1
                    dve.wait_ge(pt_made, i + 1)
                    if i >= 2:
                        dve.wait_ge(pv_made, i - 1)
                    dve.tensor_copy(PT2[:, i % 2, 0:P * n], PS[:, 2 + i % 2, 0:P * n]).then_inc(pt_taken, 1)

                def o_scale(qb):
                    dve.wait_ge(pv_made, NH * (qb + 1))
                    if qb >= 2:
                        dve.wait_ge(ot_made, qb - 1)
                    own.link(dve.reciprocal(RL[:, qb, :], LSUM[:, qb, :]))
                    dve.tensor_tensor(v3(O2[:, qb % 2, :], NH), v3(PS[:, 4 + qb % 2, :], NH),
                                      RL[:, qb, :].unsqueeze(2).to_broadcast([P, NH, VH]), ALU.mult).then_inc(o_ready, 1)

                for i in range(4 * NH):
                    qb, h = i // NH, i % NH
                    nk = P * (qb + 1)
                    dve.wait_ge(s_made, i + 1)
                    if i >= 2:
                        dve.wait_ge(p_ready, i - 1)
                    dve.tensor_tensor_reduce(out=S2[:, i % 2, 0:nk], in0=PS[:, i % 2, 0:nk], in1=mask[:, SEQ - nk:SEQ], scale=1.0,
                                             scalar=-3e38, op0=ALU.add, op1=ALU.max, accum_out=MX[:, i % 2:i % 2 + 1]
                                             ).then_inc(s_taken, 1)
                    dve.wait_ge(s_taken, i + 1)
                    dve.tensor_scalar(NM[:, i % 2:i % 2 + 1], MX[:, i % 2:i % 2 + 1], -SCALE, None, ALU.mult).then_inc(nm_ready, 1)
                    if i >= 1:
                        pt_copy(i - 1)
                    if h == 2 and qb > 0:
                        o_scale(qb - 1)
                pt_copy(4 * NH - 1)
                o_scale(3)

                dve.wait_ge(ql_made, 1)
                dve.tensor_copy(QLb.rearrange("p b h s -> p h b s"), PS[:, 5, :].rearrange("p (h b s) -> p h b s", h=NH, b=NB)
                                ).then_inc(ql_taken, 1)
                dve.wait_ge(qrb_zero, 1)
                dve.wait_ge(qt_act, TILES)
                for k in range(4):
                    dve.tensor_copy(QRB[32 * k:32 * k + 32, :, k, :].rearrange("p b (h s) -> p b h s", h=NH),
                                    QTs[NOPE:QK, :, :].rearrange("p h (b s) -> p b h s", b=NB)).then_inc(qrb_ready, 1)
                dve.wait_ge(sn_made, 1)
                dve.tensor_tensor(SN, PS[0:64, 7, :], mask_new, ALU.add).then_inc(sn_taken, 1)

                def lat_copy(b, g):
                    dve.wait_ge(lat_made, (b * CHUNKS + g) * 3 + 2)
                    dve.tensor_copy(latT[:, g % 2, 4:8, :], v3(PS[:, 2 * (g % 2) + 1, :], 4)).then_inc(lat_dve, 1)

                def back_1(b, q):
                    dve.wait_ge(sc_taken, b * CHUNKS + CHUNKS)
                    chain = Own(dve, dve_back, b * 4)
                    m1 = M1[:, 64 * q:64 * q + 64]
                    chain.link(dve.tensor_reduce(m1, S_sb[:, q, :, :].rearrange("p g (k c) -> p c g k", c=64), mybir.AxisListType.XY, ALU.max))
                    dve.tensor_tensor(m1[0:64, :], m1[0:64, :], SN[:, bass.ds(b * 64, 64)], ALU.max).then_inc(m1_ready, 1)

                def back_2(b, q):
                    chain = Own(dve, dve_back, b * 4 + 1)
                    dve.wait_ge(mt_made, b + 1)
                    chain.link(dve.tensor_reduce(MC, PS[0:64, 7, 128:256], AX, ALU.max))
                    dve.tensor_scalar(MD[0:64, :], ones[0:64, :], MC, None, ALU.mult).then_inc(md_ready, 1)

                def back_3(b, q):
                    dve.wait_ge(mb_made, b + 1)
                    chain = Own(dve, dve_back, b * 4 + 2)
                    chain.link(dve.tensor_copy(MB, PS[:, 7, 256:320]))
                    mb = MB
                    for g in range(CHUNKS):
                        s = v3(S_sb[:, q, g, :], KEYS_ROW)
                        dve.tensor_tensor(s, s, mb.unsqueeze(1).to_broadcast([P, KEYS_ROW, 64]), ALU.subtract).then_inc(sub_ready, 1)
                    dve.tensor_tensor(PNs[0:64, :], SN[:, bass.ds(b * 64, 64)], mb[0:64, :], ALU.subtract).then_inc(sub_ready, 1)

                def back_4(b, q):
                    dve.wait_ge(exp_ready, b * (CHUNKS + 1) + CHUNKS)
                    dve.tensor_reduce(PS1[:, 64 * q:64 * q + 64], S_sb[:, q, :, :].rearrange("p g (k c) -> p c g k", c=64),
                                      mybir.AxisListType.XY, ALU.add).then_inc(ps_ready, 1)

                def back_5(b, q):
                    chain = Own(dve, dve_back, b * 4 + 3)
                    dve.wait_ge(sum_made, b + 1)
                    chain.link(dve.reciprocal(RS, PS[:, 7, 64:128]))
                    dve.tensor_tensor(OLT[:, :, bass.ds(b * NS, NS)], v3(PS[:, 7, 0:64], NH), v3(RS, NH), ALU.mult).then_inc(ol_taken, 1)

                def step(b, q, back=True):
                    lat_copy(b, 0)
                    lat_copy(b, 1)
                    if back:
                        back_2(b - 1, 1 - q)
                    lat_copy(b, 2)
                    if back:
                        back_3(b - 1, 1 - q)
                    lat_copy(b, 3)
                    if back:
                        back_4(b - 1, 1 - q)
                        back_5(b - 1, 1 - q)
                    back_1(b, q)

                step(0, 0, back=False)
                with dve.Fori(0, NB // 2 - 1) as i:
                    step(2 * i + 1, 1)
                    step(2 * i + 2, 0)
                step(NB - 1, 1)
                for back in [back_2, back_3, back_4, back_5]:
                    back(NB - 1, 1)
                dve.wait_ge(yc_made, 1)
                dve.tensor_copy(catT[64:P, 4:8, SEQ:NTOK], v3(PS[0:64, 1, 0:256], 4)).then_inc(yc_dve, 1)

                def norm(n, t):
                    r, v, bn = rows(t), VV[0:rows(t), t % 2, :], BN[0:rows(t), t % 2, :]
                    own(dve.bn_stats(bn[:, 0:6], v[:, 0:512]))
                    own.link(dve.bn_stats(bn[:, 6:12], v[:, 512:1024]))
                    dve.bn_aggr(bn[:, 12:14], bn[:, 0:12]).then_inc(var_ready, 1)
                    dve.wait_ge(std_ready, n * TILES + t + 1)
                    own.link(dve.reciprocal(bn[:, 15:16], bn[:, 14:15]))
                    own.link(dve.tensor_scalar(v, v, bn[:, 12:13], bn[:, 15:16], ALU.subtract, ALU.mult))
                    dve.tensor_tensor(X[0:r, t, :], v, ln_rows[0:r, 0, :], ALU.mult).then_inc(g_ready, 1)

                dve.wait_ge(ln_loaded, 16)
                for t in range(TILES):
                    r = rows(t)
                    dve.wait_ge(y_made, t + 1)
                    b = 2 * (t % 2)
                    dve.scalar_tensor_tensor(out=VV[0:r, t % 2, :], in0=X[0:r, t, :], scalar=ALPHA,
                                             in1=PS[0:r, b:b + 2, :].rearrange("p a b -> p (a b)"),
                                             op0=ALU.mult, op1=ALU.add).then_inc(y_taken, 1)
                    dve.wait_ge(y_taken, t + 1)
                    norm(0, t)
                xt_copy(1)

                def r5(lo, *dims):
                    n = int(np.prod(dims))
                    ap = rt[:, lo:lo + TILES * n].rearrange("p (t n) -> p t n", t=TILES)
                    return ap if len(dims) == 1 else ap.rearrange("p t (g e) -> p t g e", g=dims[0])

                LG = r5(0, 20)
                GE, EE = r5(100, 4), r5(240, 4)
                G1, E1, E2 = r5(120, 4), r5(260, 4), r5(280, 4)
                TMP, PR = r5(140, 16), r5(220, 4)
                sc5 = rt[:, 300:380].rearrange("p (k t) -> p k t", k=16)
                MM = rt[:, 400:640].rearrange("p (k t e) -> p k t e", k=3, t=TILES)
                CUM = rt[:, 640:640 + 96].rearrange("p (t e) -> p t e", t=TILES + 1)
                SL = r5(740, 16)
                NE_, OT, INC, OB = (rt[:, 820 + 16 * k:836 + 16 * k] for k in range(4))
                T2 = r5(890, 16)
                OVT = rt[0:1, 980:980 + OVER * NE].rearrange("p (i e) -> p i e", i=OVER)
                OVF = rt[0:1, 1120:1120 + 1 + OVER]

                def bc(ap, n):
                    return ap.unsqueeze(2).to_broadcast([P, TILES, n])

                def first_of(dst, val, top):
                    own.link(dve.tensor_tensor(dst, val, bc(top, 4), ALU.is_equal))
                    own.link(dve.tensor_tensor(PR, dst, pri.unsqueeze(1).to_broadcast([P, TILES, 4]), ALU.mult))
                    own.link(dve.tensor_reduce(sc5[:, 15, :], PR, AX, ALU.max))
                    own.link(dve.tensor_tensor(dst, PR, bc(sc5[:, 15, :], 4), ALU.is_equal))

                dve.wait_ge(rt_made, 1)
                dve.wait_ge(rout_loaded, 32)
                own.link(dve.memset(LG[:, 4, :], 0.0))
                own(dve.tensor_tensor(LG[:, 0:4, :], v3(PS[:, 2, 0:128], 4)[:, :, 0:20],
                                      rbias[:, :].unsqueeze(1).to_broadcast([P, 4, 20]), ALU.add))
                own.link(dve.tensor_tensor(LG[0:64, 4, :], PS[0:64, 2, 128:148], rbias[0:64, :], ALU.add))
                own.link(dve.tensor_reduce(sc5[:, 0, :], LG[:, :, 0:4], AX, ALU.max))
                dve.tensor_tensor(GE, LG[:, :, 0:4], bc(sc5[:, 0, :], 4), ALU.subtract).then_inc(lg_ready, 1)
                dve.wait_ge(re_ready, 1)
                own(dve.tensor_reduce(sc5[:, 1, :], GE, AX, ALU.add))
                own.link(dve.tensor_reduce(sc5[:, 2, :], GE, AX, ALU.max))
                own.link(dve.reciprocal(sc5[:, 3, :], sc5[:, 1, :]))
                own.link(dve.tensor_tensor(sc5[:, 3, :], sc5[:, 3, :], sc5[:, 2, :], ALU.mult))
                first_of(G1, GE, sc5[:, 2, :])
                el = LG[:, :, 4:20].rearrange("p t (g e) -> p t g e", g=4)
                t4 = TMP.rearrange("p t (g e) -> p t g e", g=4)
                own.link(dve.tensor_tensor(t4, el, G1.unsqueeze(3).to_broadcast([P, TILES, 4, 4]), ALU.mult))
                own.link(dve.tensor_reduce(EE, t4.rearrange("p t g e -> p t e g"), AX, ALU.add))
                own.link(dve.tensor_reduce(sc5[:, 4, :], EE, AX, ALU.max))
                dve.tensor_tensor(EE, EE, bc(sc5[:, 4, :], 4), ALU.subtract).then_inc(le_ready, 1)
                dve.wait_ge(ree_ready, 1)
                own.link(dve.tensor_reduce(sc5[:, 5, :], EE, AX, ALU.max))
                first_of(E1, EE, sc5[:, 5, :])
                own.link(dve.scalar_tensor_tensor(out=EE, in0=E1, scalar=-2.0, in1=EE, op0=ALU.mult, op1=ALU.add))
                own.link(dve.tensor_reduce(sc5[:, 6, :], EE, AX, ALU.max))
                first_of(E2, EE, sc5[:, 6, :])
                own.link(dve.tensor_tensor(sc5[:, 7, :], sc5[:, 5, :], sc5[:, 6, :], ALU.add))
                own.link(dve.reciprocal(sc5[:, 7, :], sc5[:, 7, :]))
                own.link(dve.tensor_tensor(sc5[:, 7, :], sc5[:, 7, :], sc5[:, 3, :], ALU.mult))
                own(dve.tensor_tensor(w12[:, 0, :], sc5[:, 5, :], sc5[:, 7, :], ALU.mult))
                own(dve.tensor_tensor(w12[:, 1, :], sc5[:, 6, :], sc5[:, 7, :], ALU.mult))
                own.link(dve.tensor_tensor(G1, G1, bc(valid, 4), ALU.mult))
                g4 = G1.unsqueeze(3).to_broadcast([P, TILES, 4, 4])
                for k, e in enumerate([E1, E2]):
                    own.link(dve.tensor_tensor(MM[:, k, :, :].rearrange("p t (g e) -> p t g e", g=4), g4,
                                               e.unsqueeze(2).to_broadcast([P, TILES, 4, 4]), ALU.mult))
                own(dve.memset(CUM[:, 0, :], 0.0))
                own.link(dve.tensor_tensor(MM[:, 2, :, :], MM[:, 0, :, :], MM[:, 1, :, :], ALU.add))
                for t in range(TILES):
                    own.link(dve.tensor_tensor(CUM[:, t + 1, :], CUM[:, t, :], MM[:, 2, t, :], ALU.add))
                dve.sem_inc(m_ready, 1)
                dve.wait_ge(pos_made, 1)
                POS = v3(PS[:, 3, 0:TILES * NE], TILES)
                own.link(dve.tensor_copy(NE_, PS[:, 3, 256:256 + NE]))
                own.link(dve.tensor_scalar(OT, NE_, float(C), None, ALU.is_gt))
                for k in range(2, MORE + 1):
                    own.link(dve.scalar_tensor_tensor(out=OT, in0=NE_, scalar=float(C * k), in1=OT, op0=ALU.is_gt, op1=ALU.add))
                own.link(dve.tensor_tensor_scan(INC, ones[:, 0:NE], OT, 0.0, ALU.mult, ALU.add))
                own.link(dve.tensor_tensor(OB, INC, OT, ALU.subtract))
                own.link(dve.scalar_tensor_tensor(out=OB, in0=OB, scalar=float(C), in1=gap, op0=ALU.mult, op1=ALU.add))
                own.link(dve.tensor_scalar(T2, POS, float(C), None, ALU.is_ge))
                own.link(dve.tensor_tensor(T2, T2, OB.unsqueeze(1).to_broadcast([P, TILES, NE]), ALU.mult))
                own.link(dve.tensor_tensor(SL, POS, first_slot.unsqueeze(1).to_broadcast([P, TILES, NE]), ALU.add))
                own.link(dve.tensor_tensor(SL, SL, T2, ALU.add))
                for k in range(2):
                    own.link(dve.tensor_tensor(T2, SL, MM[:, k, :, :], ALU.mult))
                    own.link(dve.tensor_reduce(sc5[:, 8 + k, :], T2, AX, ALU.add))
                own(dve.tensor_copy(slot_i[:, :, :], sc5[:, 8:10, :]))
                own.link(dve.tensor_tensor(OVT, INC[0:1, :].unsqueeze(1).to_broadcast([1, OVER, NE]),
                                           iota.unsqueeze(2).to_broadcast([1, OVER, NE]), ALU.is_le))
                own.link(dve.tensor_reduce(OVF[:, 1:1 + OVER], OVT, AX, ALU.add))
                own.link(dve.tensor_scalar(OVF[:, 1:1 + OVER], OVF[:, 1:1 + OVER], float(NE - 1), None, ALU.min))
                own.link(dve.tensor_copy(OVF[:, 0:1], INC[0:1, NE - 1:NE]))
                own.link(dve.tensor_copy(over_i[:, :], OVF))
                dve.sem_inc(slots_ready, 1)

                def xet_copy(e, q):
                    dve.wait_ge(xet_made, 2 * e + 2)
                    dve.tensor_copy(XET[:, q, 4:8, :], v3(PS[:, 1, :], 4)).then_inc(xet_dve, 1)

                def h_mul(e, q):
                    dve.wait_ge(silu_ready, e + 1)
                    dve.tensor_tensor(HT[:, q, :, :], v3(SG[:, q, :], 2), v3(PS[:, 2 + q, 2 * C:4 * C], 2), ALU.mult).then_inc(h_ready, 1)

                def ye_copy(e, q, wait_store):
                    dve.wait_ge(dn_made, 2 * e + 2)
                    if wait_store is not None:
                        dve.wait_ge(ye_stored[q], wait_store)
                    dve.tensor_copy(YE[:, q, 512:1024], PS[:, 5 + 2 * q, :]).then_inc(ye_dve, 1)

                xet_copy(0, 0)
                h_mul(0, 0)
                xet_copy(1, 1)
                h_mul(1, 1)
                xet_copy(2, 0)
                ye_copy(0, 0, None)
                h_mul(2, 0)
                xet_copy(3, 1)
                ye_copy(1, 1, None)
                with dve.Fori(0, 6) as i:
                    for q in range(2):
                        h_mul(2 * i + 3 + q, 1 - q)
                        xet_copy(2 * i + 4 + q, q)
                        ye_copy(2 * i + 2 + q, q, i * 16 + 16)
                h_mul(15, 1)
                ye_copy(14, 0, 16 * 7)
                ye_copy(15, 1, 16 * 7)

                n_over = dve.value_load(over_i[0:1, 0:1], min_val=0, max_val=OVER)
                with dve.If(n_over > 0):
                    with dve.Fori(0, n_over) as i:
                        dve.wait_ge(ov_pe, 3 * i + 1)
                        dve.tensor_copy(XET[:, 0, 4:8, :], v3(PS[:, 1, :], 4)).then_inc(ov_dve, 1)
                        dve.wait_ge(ov_act, 3 * i + 2)
                        dve.tensor_tensor(HT[:, 0, :, :], v3(SG[:, 0, :], 2), v3(PS[:, 2, 2 * C:4 * C], 2), ALU.mult).then_inc(ov_dve, 1)
                        dve.wait_ge(ov_pe, 3 * i + 3)
                        dve.wait_ge(ye_stored[0], 16 * NE // 2)
                        dve.tensor_copy(YE[:, 0, 512:1024], PS[:, 5, :]).then_inc(ov_dve, 1)

                dve.wait_ge(ln_loaded, 32)
                dve.wait_ge(ax_ready, 1)
                for t in range(TILES):
                    r, q = rows(t), t % 2
                    dve.wait_ge(g_loaded[q], l * (32 * (3 - q)) + 32 * (t // 2 + 1))
                    own.link(dve.scalar_tensor_tensor(out=VV[0:r, q, :], in0=G[0:r, q, 0, :], scalar=w12[0:r, 0, t:t + 1],
                                                      in1=X[0:r, t, :], op0=ALU.mult, op1=ALU.add))
                    dve.scalar_tensor_tensor(out=VV[0:r, q, :], in0=G[0:r, q, 1, :], scalar=w12[0:r, 1, t:t + 1],
                                             in1=VV[0:r, q, :], op0=ALU.mult, op1=ALU.add).then_inc(v_used, 1)
                    dve.wait_ge(v_used, t + 1)
                    norm(1, t)
                dve.drain()
                dve.sem_inc(layer_end, 1)
                dve.wait_ge(layer_go, l + 1)

        @block.tensor
        def _(pe):
            pe.wait_ge(const_loaded, 16)
            pe.wait_ge(x_loaded, 32)
            with pe.Fori(0, DEPTH) as l:
                def turn_x(n):
                    for t in range(TILES):
                        r = rows(t)
                        if n == 1:
                            pe.wait_ge(x_ready, t + 1)
                        for half in range(2):
                            k = 2 * t + half
                            if k >= 4:
                                pe.wait_ge((xt_act, xt_dve)[half], TILES * n + (k - 4) // 2 + 1)
                            for i in range(4):
                                ins = pe.transpose(PS[:, 4 * n + k % 4, P * i:P * i + r], X[0:r, t, 4 * half + i::KC], ident[0:r, 0:r])
                            ins.then_inc(xt_made, 1)
                    pe.wait_ge(xt_act, TILES * (n + 1))
                    pe.wait_ge(xt_dve, TILES * (n + 1))

                turn_x(0)
                for m in range(10):
                    s, j = m // 2, m % 2
                    if j == 0:
                        pe.wait_ge(ring_loaded[s], loaded(l, s, 0))
                    if m >= 2:
                        pe.wait_ge(*fm_free(m - 2))
                    w = v3(slab(s), KC)
                    for lo, n, bank in [(0, SEQ, j), (SEQ, 64, 2 + j)]:
                        for c in range(KC):
                            ins = pe.matmul(PS[:, bank, 0:n], w[:, c, P * j:P * j + P], xT[:, c, lo:lo + n], start=(c == 0), stop=(c == KC - 1))
                    ins.then_inc(fm_made, 1)
                pe.wait_ge(ring_loaded[5], loaded(l, 5, 0))
                pe.wait_ge(ring_loaded[0], loaded(l, 0, 1))
                for t in range(TILES):
                    if t == 4:
                        pe.wait_ge(tm_taken, 1)
                    for c in range(KC):
                        pe.matmul(PS[0:rows(t), 4 + t % 4, 0:256], xT[:, c, cols(t)], v3(slab(5), KC)[:, c, :], start=(c == 0), stop=(c == KC - 1))
                    for c in range(KC):
                        ins = pe.matmul(PS[0:rows(t), 4 + t % 4, 256:416], xT[:, c, cols(t)], v3(slab(0)[:, 0:KC * 160], KC)[:, c, :],
                                        start=(c == 0), stop=(c == KC - 1))
                    ins.then_inc(tm_made, 1)
                pe.wait_ge(gatew_loaded, 16)
                pe.wait_ge(conv_ready, 2)
                pe.wait_ge(*fm_free(9))
                for g in range(2):
                    for j in range(2):
                        n = 2 * g + j
                        if n >= 2:
                            pe.wait_ge(gate_taken, n - 1)
                        pe.matmul(PS[:, n % 2, :], gatew[:, g, j, :], XC[:, j, 0:512], start=True, stop=True)
                        pe.matmul(PS[:, 2 + n % 2, 0:88], gatew[:, g, j, :], XC[:, j, 512:600], start=True, stop=True).then_inc(gate_made, 1)
                pe.wait_ge(norm_ready, TILES + 1)
                pe.wait_ge(gate_taken, 4)
                for t in range(TILES):
                    r = rows(t)
                    if t >= 2:
                        pe.wait_ge(cqt_ready, t - 1)
                        pe.wait_ge(ckt_ready, t - 1)
                    for k in range(2):
                        pe.transpose(PS[:, t % 2, P * k:P * k + r], PT[0:r, t, P * k:P * k + P], ident[0:r, 0:r])
                    pe.transpose(PS[:, 2 + t % 2, 0:r], CKV[0:r, t, :], ident[0:r, 0:r])
                    pe.transpose(PS[0:ROPE, 2 + t % 2, P:P + r], KR[0:r, t, :], ident[0:r, 0:r]).then_inc(kt_made, 1)

                def queries(t):
                    r, b = rows(t), 4 + 2 * (t % 2)
                    pe.wait_ge(cqt_ready, t + 1)
                    if t >= 2:
                        pe.wait_ge(q_taken, t - 1)
                    for lo, n in [(0, 512), (512, 256)]:
                        for k in range(2):
                            ins = pe.matmul(PS[0:r, b + lo // 512, 0:n], cqT[:, k, cols(t)], w_uq[:, k, lo:lo + n], start=(k == 0), stop=(k == 1))
                    ins.then_inc(q_made, 1)

                def turn_q(t):
                    r = rows(t)
                    pe.wait_ge(q_roped, t + 1)
                    for half in range(2):
                        if t >= 1:
                            pe.wait_ge((qt_act, qt_dve)[half], t)
                        for i in range(4):
                            h = 4 * half + i
                            ins = pe.transpose(PS[0:QK, 2 + half, P * i:P * i + r], Q[0:r, t % 2, QK * h:QK * h + QK], ident[0:r, 0:r])
                        ins.then_inc(qt_made, 1)

                pe.wait_ge(uq_loaded, 16)
                pe.wait_ge(tm_taken, TILES)
                pe.wait_ge(ckt_ready, TILES)
                queries(0)
                for t in range(TILES):
                    if t + 1 < TILES:
                        queries(t + 1)
                    turn_q(t)
                pe.wait_ge(uk_loaded, 32)
                pe.wait_ge(ckt_ready, TILES)
                pe.wait_ge(cqt_ready, TILES)
                for h in range(NH):
                    if h >= 2:
                        pe.wait_ge(kn_taken, h - 1)
                    pe.matmul(PS[0:NOPE, h % 2, :], w_uk[:, NOPE * h:NOPE * h + NOPE], CKT[:, 0:SEQ], start=True, stop=True).then_inc(kn_made, 1)
                pe.wait_ge(uv_loaded, 16)
                pe.wait_ge(q_taken, TILES)
                for t in range(4):
                    pe.matmul(PS[:, 4 + t, :], CKT[:, cols(t)], w_uv[:, :], start=True, stop=True).then_inc(v_made, 1)
                pe.wait_ge(st_ready, 1)
                pe.wait_ge(qt_act, TILES)
                for j in range(2):
                    ins = pe.transpose(PS[0:NST, 2, P * j:P * j + P], ST[:, j, :], ident)
                ins.then_inc(st_made, 1)

                def scores(i):
                    qb, h = i // NH, i % NH
                    if i >= 2:
                        pe.wait_ge(s_taken, i - 1)
                    pe.matmul(PS[:, i % 2, 0:P * (qb + 1)], QTp[:, h, cols(qb)], KT[:, h, 0:P * (qb + 1)], start=True, stop=True
                              ).then_inc(s_made, 1)

                def turn_p(i):
                    pe.wait_ge(p_ready, i + 1)
                    if i >= 2:
                        pe.wait_ge(pt_taken, i - 1)
                    for j in range(i // NH + 1):
                        ins = pe.transpose(PS[:, 2 + i % 2, P * j:P * j + P], P2[:, i % 2, P * j:P * j + P], ident)
                    ins.then_inc(pt_made, 1)

                def weigh(i):
                    qb, h = i // NH, i % NH
                    if h == 0 and qb >= 2:
                        pe.wait_ge(o_ready, qb - 1)
                    pe.wait_ge(pt_taken, i + 1)
                    for j in range(qb + 1):
                        ins = pe.matmul(PS[:, 4 + qb % 2, VH * h:VH * h + VH], PT2[:, i % 2, P * j:P * j + P], V[:, j, VH * h:VH * h + VH],
                                        start=(j == 0), stop=(j == qb))
                    ins.then_inc(pv_made, 1)

                def turn_o(qb):
                    pe.wait_ge(o_ready, qb + 1)
                    if qb >= 2:
                        pe.wait_ge(ot_taken, qb - 1)
                    for j in range(4):
                        ins = pe.transpose(PS[:, 6 + qb % 2, P * j:P * j + P], O2[:, qb % 2, P * j:P * j + P], ident)
                    ins.then_inc(ot_made, 1)

                pe.wait_ge(kn_taken, NH)
                pe.wait_ge(kr_ready, 1)
                pe.wait_ge(v_taken, 4)
                pe.wait_ge(st_taken, 1)
                pe.wait_ge(qt_dve, TILES)
                scores(0)
                for i in range(4 * NH):
                    if i + 1 < 4 * NH:
                        scores(i + 1)
                    turn_p(i)
                    if i >= 1:
                        weigh(i - 1)
                    if i % NH == 3 and i > NH:
                        turn_o(i // NH - 1)
                weigh(4 * NH - 1)
                turn_o(3)

                pe.wait_ge(o_ready, 4)
                for h in range(NH):
                    ins = pe.matmul(PS[:, 5, 64 * h:64 * h + 64], w_ukT[:, h, :], QTs[0:NOPE, h, :], start=True, stop=True)
                ins.then_inc(ql_made, 1)
                pe.wait_ge(ot_taken, 4)
                pe.wait_ge(qrb_ready, 4)
                pe.wait_ge(ql_taken, 1)
                pe.matmul(PS[0:64, 7, :], CKT[:, SEQ:NTOK], QLb.rearrange("p b h s -> p (b h s)"), start=True, stop=False)
                pe.matmul(PS[0:64, 7, :], KRT[:, SEQ:NTOK], QRB[0:ROPE, :, 0, :], start=False, stop=True).then_inc(sn_made, 1)

                def turn_kv(b, q, g):
                    n, s = b * CHUNKS + g, CHUNKS * q + g
                    pe.wait_ge(kv_loaded[s], l * (16 * NB // 2) + kv_count(b, q))
                    if not (isinstance(b, int) and b == 0 and g < 2):
                        pe.wait_ge(lat_act, 2 * n - 2)
                        pe.wait_ge(lat_dve, n - 1)
                    lat = KV[:, s, 0:KEYS_ROW * R]
                    rop = KV[:, s, KEYS_ROW * R:]
                    for h in range(2):
                        for k in range(4):
                            ins = pe.transpose(PS[:, 2 * (g % 2) + h, P * k:P * k + P], lat[:, P * (4 * h + k):P * (4 * h + k) + P], ident)
                        ins.then_inc(lat_made, 1)
                    if not (isinstance(b, int) and b == 0 and g == 0):
                        pe.wait_ge(lat_act, 2 * n)
                    for k in range(2):
                        ins = pe.transpose(PS[:, 4, P * k:P * k + P], rop[:, P * k:P * k + P], ident)
                    ins.then_inc(lat_made, 1)

                def kv_count(b, q):
                    return 16 * (b // 2 + 1) if isinstance(b, int) else b * 8 + (16 - 8 * q)

                def score_kv(b, q, g):
                    n = b * CHUNKS + g
                    pe.wait_ge(lat_act, 2 * n + 2)
                    pe.wait_ge(lat_dve, n + 1)
                    if not (isinstance(b, int) and b == 0 and g < 2):
                        pe.wait_ge(sc_taken, n - 1)
                    bank = PS[:, 5 + g % 2, :]
                    qr = QRB[:, bass.ds(b, 1), :, :].rearrange("p b k c -> p (b k c)")
                    ql = QLb[:, bass.ds(b, 1), :, :].rearrange("p b h s -> p (b h s)")
                    for h in range(2):
                        pe.matmul(bank[:, 256 * h:256 * h + 256], ropT[:, g % 2, h, :], qr, start=True, stop=True)
                        for k in range(4 * h, 4 * h + 4):
                            ins = pe.matmul(bank[:, 64 * k:64 * k + 64], latT[:, g % 2, k, :], ql, start=False, stop=True,
                                            skip_group_check=True)
                    ins.then_inc(sc_made, 1)

                def turn_max(b, q):
                    pe.wait_ge(m1_ready, b + 1)
                    pe.sem_inc(pe_held, 1)
                    pe.transpose(PS[0:64, 7, 128:256], M1[:, 64 * q:64 * q + 64], ident).then_inc(mt_made, 1)

                def spread_max(b):
                    pe.wait_ge(md_ready, b + 1)
                    pe.matmul(PS[:, 7, 256:320], MD[0:64, :], ident[0:64, 0:64], start=True, stop=True).then_inc(mb_made, 1)

                def weigh_kv(b, q, g):
                    pe.wait_ge(exp_ready, b * (CHUNKS + 1) + g + 1)
                    lat = KV[:, CHUNKS * q + g, 0:KEYS_ROW * R]
                    for k in range(KEYS_ROW):
                        ins = pe.matmul(PS[:, 7, 0:64], lat[:, P * k:P * k + P], S_sb[:, q, g, 64 * k:64 * k + 64],
                                        start=(g == 0 and k == 0), stop=False)
                    ins.then_inc(pvl_made, 1)

                def weigh_new(b, q):
                    pe.wait_ge(exp_ready, b * (CHUNKS + 1) + CHUNKS + 1)
                    pn = PN[0:64, 64 * q:64 * q + 64]
                    pe.matmul(PS[:, 7, 0:64], CKV[0:64, 4, :], pn, start=False, stop=True)
                    pe.wait_ge(ps_ready, b + 1)
                    pe.matmul(PS[:, 7, 64:128], ones, PS1[:, 64 * q:64 * q + 64], start=True, stop=False)
                    pe.matmul(PS[:, 7, 64:128], ones[0:64, :], pn, start=False, stop=True).then_inc(sum_made, 1)

                def step(b, q, back=True):
                    turn_kv(b, q, 0)
                    turn_kv(b, q, 1)
                    score_kv(b, q, 0)
                    if back:
                        turn_max(b - 1, 1 - q)
                    turn_kv(b, q, 2)
                    score_kv(b, q, 1)
                    if back:
                        spread_max(b - 1)
                    turn_kv(b, q, 3)
                    score_kv(b, q, 2)
                    if back:
                        weigh_kv(b - 1, 1 - q, 0)
                        weigh_kv(b - 1, 1 - q, 1)
                    score_kv(b, q, 3)
                    if back:
                        weigh_kv(b - 1, 1 - q, 2)
                        weigh_kv(b - 1, 1 - q, 3)
                        weigh_new(b - 1, 1 - q)

                pe.wait_ge(sn_taken, 1)
                step(0, 0, back=False)
                with pe.Fori(0, NB // 2 - 1) as i:
                    step(2 * i + 1, 1)
                    step(2 * i + 2, 0)
                step(NB - 1, 1)
                turn_max(NB - 1, 1)
                spread_max(NB - 1)
                for g in range(CHUNKS):
                    weigh_kv(NB - 1, 1, g)
                weigh_new(NB - 1, 1)
                pe.wait_ge(ol_taken, NB)
                for h in range(NH):
                    ins = pe.matmul(PS[0:VH, h % 2, 64 * (h // 2):64 * (h // 2) + 64], w_uv[:, VH * h:VH * h + VH], OLT[:, h, :], start=True, stop=True)
                ins.then_inc(yc_made, 1)

                pe.wait_ge(yc_act, 1)
                pe.wait_ge(yc_dve, 1)
                for s in range(2, 6):
                    pe.wait_ge(ring_loaded[s], loaded(l, s, 1))
                for t in range(TILES):
                    if t >= 2:
                        pe.wait_ge(y_taken, t - 1)
                    for n in range(4):
                        for c in range(KC):
                            ins = pe.matmul(PS[0:rows(t), 2 * (t % 2) + n // 2, 256 * (n % 2):256 * (n % 2) + 256], catT[:, c, cols(t)],
                                            v3(slab(2 + n), KC)[:, c, :], start=(c == 0), stop=(c == KC - 1))
                    ins.then_inc(y_made, 1)
                turn_x(1)
                pe.wait_ge(rout_loaded, 32)
                pe.wait_ge(y_taken, TILES)
                for t in range(TILES):
                    for c in range(KC):
                        ins = pe.matmul(PS[0:rows(t), 2, 32 * t:32 * t + 20], xT[:, c, cols(t)], wr[:, c, :], start=(c == 0), stop=(c == KC - 1))
                ins.then_inc(rt_made, 1)
                pe.wait_ge(m_ready, 1)
                MM2 = rt[:, 400 + 2 * TILES * NE:400 + 3 * TILES * NE]
                pe.matmul(PS[:, 3, 0:TILES * NE], tri, MM2, start=True, stop=False)
                pe.matmul(PS[:, 3, 0:TILES * NE], ones, rt[:, 640:640 + TILES * NE], start=False, stop=True)
                pe.matmul(PS[:, 3, 256:256 + NE], ones, rt[:, 640 + TILES * NE:640 + (TILES + 1) * NE], start=True, stop=True
                          ).then_inc(pos_made, 1)
                pe.wait_ge(slots_ready, 1)

                def turn_e(src, ins_sem):
                    for half in range(2):
                        for i in range(4):
                            ins = pe.transpose(PS[:, half, P * i:P * i + C], src[:, 4 * half + i::KC], ident)
                        if ins_sem is xet_made or half == 1:
                            ins.then_inc(ins_sem, 1)

                def gate_up(q, slots, ins_sem):
                    for n in range(4):
                        w = v3(slab(slots[n // 2]), KC)
                        for c in range(KC):
                            ins = pe.matmul(PS[:, 2 + q, C * n:C * n + C], w[:, c, P * (n % 2):P * (n % 2) + P], XET[:, q, c, :],
                                            start=(c == 0), stop=(c == KC - 1))
                    ins.then_inc(ins_sem, 1)

                def down(q, slot, ins_sem):
                    for n in range(2):
                        for k in range(2):
                            ins = pe.matmul(PS[:, 4 + 2 * q + n, :], HT[:, q, k, :], v3(slab(slot), 2)[:, k, 512 * n:512 * n + 512],
                                            start=(k == 0), stop=(k == 1))
                        if ins_sem is dn_made or n == 1:
                            ins.then_inc(ins_sem, 1)

                def t_step(e, q, i):
                    pe.wait_ge(xe_loaded[q], i * 16 + 16)
                    if not isinstance(e, int) or e > 0:
                        pe.wait_ge(xet_act, e)
                        pe.wait_ge(xet_dve, e)
                    turn_e(XE[:, q, :], xet_made)

                def g_step(e, q, i):
                    for k in range(2):
                        pe.wait_ge(ring_loaded[3 * q + k], loaded(l, 3 * q + k, eload(3 * q + k, i)))
                    pe.wait_ge(xet_act, e + 1)
                    pe.wait_ge(xet_dve, e + 1)
                    if not isinstance(e, int) or e >= 2:
                        pe.wait_ge(h_ready, e - 1)
                    gate_up(q, [3 * q, 3 * q + 1], gu_made)

                def d_step(e, q, i):
                    pe.wait_ge(ring_loaded[3 * q + 2], loaded(l, 3 * q + 2, eload(3 * q + 2, i)))
                    pe.wait_ge(h_ready, e + 1)
                    if not isinstance(e, int) or e >= 2:
                        pe.wait_ge(ye_act, e - 1)
                        pe.wait_ge(ye_dve, e - 1)
                    down(q, 3 * q + 2, dn_made)

                t_step(0, 0, 0)
                g_step(0, 0, 0)
                t_step(1, 1, 0)
                g_step(1, 1, 0)
                t_step(2, 0, 1)
                d_step(0, 0, 0)
                g_step(2, 0, 1)
                t_step(3, 1, 1)
                d_step(1, 1, 0)
                with pe.Fori(0, 6) as i:
                    g_step(2 * i + 3, 1, i + 1)
                    t_step(2 * i + 4, 0, i + 2)
                    d_step(2 * i + 2, 0, i + 1)
                    g_step(2 * i + 4, 0, i + 2)
                    t_step(2 * i + 5, 1, i + 2)
                    d_step(2 * i + 3, 1, i + 1)
                g_step(15, 1, 7)
                d_step(14, 0, 7)
                d_step(15, 1, 7)

                n_over = pe.value_load(over_i[0:1, 0:1], min_val=0, max_val=OVER)
                with pe.If(n_over > 0):
                    pe.wait_ge(ye_act, NE)
                    pe.wait_ge(ye_dve, NE)
                    with pe.Fori(0, n_over) as i:
                        pe.wait_ge(ov_loaded, i * 64 + 64)
                        turn_e(XE[:, 0, :], ov_pe)
                        pe.wait_ge(ov_act, 3 * i + 1)
                        pe.wait_ge(ov_dve, 3 * i + 1)
                        gate_up(0, [0, 1], ov_pe)
                        pe.wait_ge(ov_dve, 3 * i + 2)
                        down(0, 2, ov_pe)
                        pe.wait_ge(ov_act, 3 * i + 3)
                        pe.wait_ge(ov_dve, 3 * i + 3)
                pe.drain()
                pe.sem_inc(layer_end, 1)
                pe.wait_ge(layer_go, l + 1)


_OUTS = [("y_p", (1, 512, 1024)), ("y_s", (8, 8, 1024)), ("ckv_p", (2, 1, 512, 128)), ("kr_p", (2, 1, 512, 32)),
         ("h_p", (2, 1, 256)), ("ca_p", (2, 1, 3, 256)), ("cb_p", (2, 1, 2, 256)), ("ckv_s", (2, 8, 8, 128)),
         ("kr_s", (2, 8, 8, 32)), ("h_s", (2, 8, 256)), ("ca_s", (2, 8, 3, 256)), ("cb_s", (2, 8, 2, 256))]


def _constants():
    c = np.zeros((P, NCONST), np.float32)
    p = np.arange(P)
    c[:, C_ID:C_ID + P] = np.eye(P)
    c[:, C_TRI:C_TRI + P] = p[:, None] < p[None, :]
    c[:, C_ONE:C_ONE + P] = 1
    c[:, C_MASK:C_MASK + SEQ] = np.where(np.arange(SEQ)[None] - (SEQ - P) <= p[:, None], 0, NEG)
    key, col = np.arange(64)[:, None], np.arange(512)[None]
    seen = (key // NS == col // 64) & (key % NS <= col % NS)
    c[0:64, C_NEW:C_NEW + 512] = np.where(seen, 0, NEG)
    pos = np.concatenate([np.arange(SEQ), PAST + np.arange(NB * NS) % NS, np.zeros(64)]).astype(np.float32)
    freqs = np.float32(10000.0) ** (-np.arange(16, dtype=np.float32) / np.float32(16))
    ang = pos[:, None] * freqs[None, :]
    both = np.concatenate([np.cos(ang), np.sin(ang)], 1).reshape(TILES, P, 32)
    c[:, C_CS:C_CS + 160] = both.transpose(1, 0, 2).reshape(P, 160)
    c[:, C_SEL:C_SEL + PAGES_CH] = p[:, None] // ROWS_PAGE == np.arange(PAGES_CH)[None]
    c[:, C_P16] = p % ROWS_PAGE
    c[:, C_VAL:C_VAL + 5] = (np.arange(5)[None] * P + p[:, None]) < NTOK
    c[:, C_PRI:C_PRI + 4] = [4, 3, 2, 1]
    e = np.arange(NE)
    c[:, C_EC:C_EC + NE] = e * C
    c[:, C_GAP:C_GAP + NE] = (NE - 1) * C - e * C
    c[:, C_IOTA:C_IOTA + NE] = e
    return c


def kernel(**inputs):
    import concourse.bacc as _bacc
    from concourse.bass_utils import run_bass_kernel_spmd as _run

    g = {k: np.asarray(v) for k, v in inputs.items()}
    L = DEPTH
    arr = {"const": _constants(), "x_prompt": g["x_prompt"], "x_sample": g["x_sample"]}
    w = g["w_in"].reshape(L, P, KC, 1696)
    w_in = np.zeros((L, P, 7, SLAB), np.float32)
    for s in range(6):
        w_in[:, :, s] = w[..., 256 * s:256 * s + 256].reshape(L, P, SLAB)
    w_in[:, :, 6, 0:KC * 160] = w[..., 1536:1696].reshape(L, P, KC * 160)
    arr["w_in"] = w_in
    arr["w_out"] = g["w_out"].reshape(L, KC, P, 4, 256).transpose(0, 2, 3, 1, 4).reshape(L, P, 4, SLAB)
    for k in ("w_gate", "w_up", "w_down", "w_uq"):
        arr[k] = g[k]
    arr["w_uk"] = g["w_uk"].reshape(L, R, NH * NOPE)
    arr["w_ukT"] = g["w_uk"].transpose(0, 3, 2, 1)
    arr["w_uv"] = g["w_uv"].reshape(L, R, NH * VH)
    gw = np.zeros((L, P, 2, 2, P), np.float32)
    for i, k in enumerate(("lru_gate_x_w", "lru_gate_a_w")):
        for j in range(2):
            for h in range(2):
                gw[:, 64 * h:64 * h + 64, i, j, 64 * h:64 * h + 64] = g[k][:, 2 * j + h]
    arr["gatew"] = gw
    rows_ = [g["lru_conv_w"], g["lru_conv_b"][:, None], g["lru_gate_x_b"][:, None], g["lru_gate_a_b"][:, None],
             g["lru_lambda"][:, None], g["sc_conv_w"], g["q_norm_g"][:, None], g["state_lru_h"],
             g["state_lru_conv"].reshape(L, 24, W), g["state_sconv"].reshape(L, 16, W)]
    arr["par"] = np.concatenate(rows_, 1).reshape(L, NPAR, 2, P).transpose(0, 3, 2, 1)
    arr["kvg"] = g["kv_norm_g"][:, None]
    arr["ln_mix"] = np.stack([g["ln_mix_g"], g["ln_mix_b"]], 1)
    arr["ln_ffn"] = np.stack([g["ln_ffn_g"], g["ln_ffn_b"]], 1)
    arr["wr"] = np.concatenate([g["router_group_w"], g["router_expert_w"]], 2).reshape(L, P, KC, 20)
    arr["rbias"] = np.concatenate([g["router_group_b"], g["router_expert_b"]], 1)[:, None]
    n_rows = g["cache_ckv"].shape[1] * ROWS_PAGE
    arr["cache"] = np.concatenate([g["cache_ckv"].reshape(L * n_rows, KEYS_ROW * R),
                                   g["cache_krope"].reshape(L * n_rows, KEYS_ROW * ROPE)], 1)
    arr["page_table"] = g["page_table"].reshape(256)

    nc = _bacc.Bacc("TRN2", target_bir_lowering=False, num_devices=1)
    arrays, a, o = {}, {}, {}
    for k, v in arr.items():
        v = np.ascontiguousarray(v)
        arrays[f"in_{k}"] = v
        a[k] = nc.dram_tensor(f"in_{k}", v.shape, mybir.dt.from_np(v.dtype), kind="ExternalInput").ap()
    for k, shape in _OUTS:
        o[k] = nc.dram_tensor(f"out_{k}", shape, F32, kind="ExternalOutput").ap()
    build(nc, a, o)
    r = _run(nc, [arrays], core_ids=[0])
    return tuple(r.results[0][f"out_{k}"] for k, _ in _OUTS)
```

```python
from contextlib import ExitStack

import numpy as np

import concourse.bass as bass
from concourse import mybir

F32 = mybir.dt.float32
I32 = mybir.dt.int32
ALU = mybir.AluOpType
ACT = mybir.ActivationFunctionType
AX = mybir.AxisListType.X

P = 128
D = 1024
DEPTH = 2
SEQ = 512
NB = 8
NS = 8
NTOK = SEQ + NB * NS
TILES = 5
HALF = NTOK // 2
KC = D // P
W = 256
NH, NOPE, ROPE, VH = 8, 64, 32, 64
QK = NOPE + ROPE
QL, R = 256, 128
PAST, PAGE = 4096, 128
KEYS_ROW = 8
ROWS_PAGE = PAGE // KEYS_ROW
PAGES_CH = P // ROWS_PAGE
CHUNKS = PAST // PAGE // PAGES_CH
NE, FF = 16, 256
C = 128
SCALE = QK ** -0.5
ALPHA = (2 * DEPTH) ** 0.25
LN_EPS, RMS_EPS = 1e-5, 1e-6
MORE = (NTOK - 1) // C
OVER = 2 * NTOK // (C + 1)
SLOTS = (NE + OVER) * C
NEG = -1e30

LA = 3 + SEQ + NB * (3 + NS)
LZ = 2 + SEQ + NB * (2 + NS)
LP = 604
P_CW, P_CB, P_GXB, P_GAB, P_LAM, P_SW, P_QG, P_H0, P_CS, P_SS = 0, 4, 5, 6, 7, 8, 11, 12, 20, 44
NPAR = 60
ST_H, ST_C, ST_S, NST = 0, 9, 36, 54
C_ID, C_TRI, C_ONE, C_MASK, C_NEW, C_CS, C_SEL, C_P16, C_VAL, C_PRI, C_EC, C_GAP, C_IOTA, NCONST = np.cumsum(
    [0, 128, 128, 128, 512, 512, 160, 8, 1, 5, 4, 16, 16, 16]).tolist()

RING = 6
SLAB = KC * W
FIRST_E = 12
LOADS = [10, 9, 10, 10, 10, 10]


def rows(t):
    return P if t < 4 else NTOK - SEQ


def cols(t):
    return slice(P * t, P * t + rows(t))


def loaded(l, slot, k):
    return l * (16 * LOADS[slot]) + (k * 16 + 16)


def eload(slot, i):
    return i + (1 if slot == 1 else 2)


class Own:

    def __init__(self, eng, sem, base=0):
        self.eng, self.sem, self.base, self.n = eng, sem, base, 0

    def __call__(self, ins):
        self.n += 1
        ins.then_inc(self.sem, 1)

    def settle(self):
        self.eng.wait_ge(self.sem, self.base + self.n)

    def link(self, ins):
        self(ins)
        self.settle()


def build(nc, a, o):
    ctx = ExitStack()
    with ctx:
        def sb(name, shape, dt=F32):
            return ctx.enter_context(nc.sbuf_tensor(name, shape, dt))

        lasting = {}
        for name in ["x_loaded", "table_loaded", "const_loaded", "xs_zeroed", "zero_ready",
                     "dve_start", "layer_end", "layer_go"]:
            lasting[name] = ctx.enter_context(nc.semaphore(name))
        x_loaded, table_loaded, const_loaded = (lasting[n] for n in ["x_loaded", "table_loaded", "const_loaded"])
        xs_zeroed, zero_ready = (lasting[n] for n in ["xs_zeroed", "zero_ready"])
        dve_start, layer_end, layer_go = (lasting[n] for n in ["dve_start", "layer_end", "layer_go"])
        ring_loaded = [ctx.enter_context(nc.semaphore(f"ring_loaded{i}")) for i in range(RING)]

        kv_loaded = [ctx.enter_context(nc.semaphore(f"kv_loaded{i}")) for i in range(2 * CHUNKS)]
        scattered = ctx.enter_context(nc.semaphore("scattered"))
        g_loaded = [ctx.enter_context(nc.semaphore(f"g_loaded{i}")) for i in range(4)]

        per_layer = []

        def sem(name):
            s = ctx.enter_context(nc.semaphore(name))
            per_layer.append(s)
            return s

        dve_own, act_own = sem("dve_own"), sem("act_own")
        dve_back, dve_max = sem("dve_back"), sem("dve_max")
        held = sem("held")
        par_loaded, uq_loaded, uk_loaded = sem("par_loaded"), sem("uq_loaded"), sem("uk_loaded")
        gatew_loaded, rout_loaded, kvg_loaded, ln_loaded = sem("gatew_loaded"), sem("rout_loaded"), sem("kvg_loaded"), sem("ln_loaded")
        xt_made, xt_act, xt_dve = sem("xt_made"), sem("xt_act"), sem("xt_dve")
        fm_made, fm_act, fm_dve = sem("fm_made"), sem("fm_act"), sem("fm_dve")
        tm_made, tm_taken = sem("tm_made"), sem("tm_taken")
        conv_ready, gate_made, gate_taken = sem("conv_ready"), sem("gate_made"), sem("gate_taken")
        ssq_ready, rms_ready, norm_ready = sem("ssq_ready"), sem("rms_ready"), sem("norm_ready")
        kt_made, cqt_ready, ckt_ready = sem("kt_made"), sem("cqt_ready"), sem("ckt_ready")
        q_made, q_taken, q_roped = sem("q_made"), sem("q_taken"), sem("q_roped")
        qt_made, qt_act, qt_dve = sem("qt_made"), sem("qt_act"), sem("qt_dve")
        kn_made, kn_taken, v_made, v_taken, kr_ready = sem("kn_made"), sem("kn_taken"), sem("v_made"), sem("v_taken"), sem("kr_ready")
        loga_ready, expa_ready, mult2_ready, mult_ready = sem("loga_ready"), sem("expa_ready"), sem("mult2_ready"), sem("mult_ready")
        lam_exp, lam_ln = sem("lam_exp"), sem("lam_ln")
        st_ready, st_made, st_taken = sem("st_ready"), sem("st_made"), sem("st_taken")
        mixed_ab = sem("mixed_ab")
        s_made, s_taken, nm_ready, p_ready = sem("s_made"), sem("s_taken"), sem("nm_ready"), sem("p_ready")
        pt_made, pt_taken, pv_made, o_ready, ot_made, ot_taken = (
            sem("pt_made"), sem("pt_taken"), sem("pv_made"), sem("o_ready"), sem("ot_made"), sem("ot_taken"))
        ql_made, ql_taken, sn_made, sn_taken, qrb_ready, qrb_zero = (
            sem("ql_made"), sem("ql_taken"), sem("sn_made"), sem("sn_taken"), sem("qrb_ready"), sem("qrb_zero"))
        idx_ready, slot_idx = sem("idx_ready"), sem("slot_idx")
        lat_made, lat_act, lat_dve = sem("lat_made"), sem("lat_act"), sem("lat_dve")
        sc_made, sc_taken = sem("sc_made"), sem("sc_taken")
        m1_ready, mt_made, md_ready, mb_made = sem("m1_ready"), sem("mt_made"), sem("md_ready"), sem("mb_made")
        sub_ready, exp_ready, ps_ready = sem("sub_ready"), sem("exp_ready"), sem("ps_ready")
        pvl_made, sum_made, ol_taken = sem("pvl_made"), sem("sum_made"), sem("ol_taken")
        olt_made, olt_taken = sem("olt_made"), sem("olt_taken")
        yc_made, yc_act, yc_dve = sem("yc_made"), sem("yc_act"), sem("yc_dve")
        y_made, y_taken = sem("y_made"), sem("y_taken")
        nmr_ready, vn_ready = sem("nmr_ready"), sem("vn_ready")
        var_ready, std_ready, g_ready, x_ready = sem("var_ready"), sem("std_ready"), sem("g_ready"), sem("x_ready")
        rt_made, lg_ready, re_ready, le_ready, ree_ready = (
            sem("rt_made"), sem("lg_ready"), sem("re_ready"), sem("le_ready"), sem("ree_ready"))
        m_ready, pos_made, slots_ready = sem("m_ready"), sem("pos_made"), sem("slots_ready")
        ax_ready = sem("ax_ready")
        xe_loaded = [sem("xe_loaded0"), sem("xe_loaded1")]
        xet_made, xet_act, xet_dve = sem("xet_made"), sem("xet_act"), sem("xet_dve")
        gu_made, silu_ready, h_ready = sem("gu_made"), sem("silu_ready"), sem("h_ready")
        dn_made, ye_act, ye_dve = sem("dn_made"), sem("ye_act"), sem("ye_dve")
        ye_stored = [sem("ye_stored0"), sem("ye_stored1")]
        ov_loaded, ov_pe, ov_act, ov_dve, ov_stored, ov_done = (
            sem("ov_loaded"), sem("ov_pe"), sem("ov_act"), sem("ov_dve"), sem("ov_stored"), sem("ov_done"))
        v_used, out_stored, states_stored = sem("v_used"), sem("out_stored"), sem("states_stored")
        numbers = [s.num for s in per_layer]
        layer_range = range(min(numbers), max(numbers) + 1)
        assert len(layer_range) == len(per_layer)

        X = sb("X", [P, TILES, D])
        xt_mem = sb("xt_mem", [P, KC * NTOK])
        ring = sb("ring", [P, RING, SLAB])
        catT = sb("catT", [P, KC, NTOK])
        CKV = sb("CKV", [P, TILES, R])
        KR = sb("KR", [P, TILES, ROPE])
        CKT = sb("CKT", [P, NTOK])
        KRT = sb("KRT", [ROPE, NTOK])
        wq_mem = sb("wq_mem", [P, 2 * D])
        gatew = sb("gatew", [P, 2, 2, P])
        w_ukT = sb("w_ukT", [NOPE, NH, R])
        w_uv = sb("w_uv", [P, NH * VH])
        wr = sb("wr", [P, KC, 20])
        par = sb("par", [P, 2, NPAR])
        kvg = sb("kvg", [P, R])
        rbias = sb("rbias", [P, 20])
        const = sb("const", [P, NCONST])
        zero = sb("zero", [P, 256])
        arena = sb("arena", [P, 17800])
        small = sb("small", [P, 64])
        first_row = sb("first_row", [P, 1])
        idx_f = sb("idx_f", [P, NB * CHUNKS])
        idx_i = sb("idx_i", [P, NB * CHUNKS], I32)
        idx_1 = sb("idx_1", [P, 2 * CHUNKS], I32)
        w12 = sb("w12", [P, 2, TILES])
        slot_i = sb("slot_i", [P, 2, TILES], I32)
        over_i = sb("over_i", [1, 1 + OVER], I32)
        PS = ctx.enter_context(nc.psum_tensor("PS", [P, 8, 512], F32))

        xT = xt_mem[:, :].rearrange("p (c t) -> p c t", c=KC)
        QTp = xt_mem[0:QK, 0:NH * SEQ].rearrange("p (h t) -> p h t", h=NH)
        QTs = xt_mem[0:QK, NH * SEQ:KC * NTOK].rearrange("p (h t) -> p h t", h=NH)
        S_sb = xt_mem[:, 0:2 * CHUNKS * 512].rearrange("p (b g c) -> p b g c", b=2, g=CHUNKS)
        OL = xt_mem[:, NH * SEQ:KC * NTOK]
        w_uq = wq_mem[:, 0:2 * 768].rearrange("p (k n) -> p k n", k=2)
        w_uk = wq_mem[:, 2 * 768:2 * D]
        ln_rows = wq_mem[:, :].rearrange("p (a n) -> p a n", a=2)

        ident = const[:, C_ID:C_ID + P]
        tri = const[:, C_TRI:C_TRI + P]
        ones = const[:, C_ONE:C_ONE + P]
        mask = const[:, C_MASK:C_MASK + SEQ]
        mask_new = const[0:NB * NS, C_NEW:C_NEW + NB * NH * NS]
        cs = const[:, C_CS:C_CS + 160].rearrange("p (t n) -> p t n", t=TILES)
        sel = const[:, C_SEL:C_SEL + PAGES_CH]
        p16 = const[:, C_P16:C_P16 + 1]
        valid = const[:, C_VAL:C_VAL + TILES]
        pri = const[:, C_PRI:C_PRI + 4]
        first_slot = const[:, C_EC:C_EC + NE]
        gap = const[:, C_GAP:C_GAP + NE]
        iota = const[0:1, C_IOTA:C_IOTA + OVER]

        at = [0]

        def take(n):
            at[0] += n
            assert at[0] <= 17800, at[0]
            return arena[:, at[0] - n:at[0]]

        def v3(ap, k):
            return ap.rearrange("p (a b) -> p a b", a=k)

        PT = v3(take(TILES * 416), TILES)
        cqT = v3(take(2 * NTOK), 2)
        Q = v3(take(2 * 768), 2)
        at[0] = 0
        KT = v3(take(NH * SEQ)[0:QK, :], NH)
        V = v3(take(4 * NH * VH), 4)
        lru_at = at[0]
        xa_pad, z_pad, XC, SI, SR, A, U = (v3(take(2 * LP), 2) for _ in range(7))
        ZC = U
        rope_tmp = v3(take(4 * 640), 4)
        junk = take(QL)
        ST = v3(take(2 * NST), 2)
        ST2 = take(2 * P)[0:NST, :]
        pages = junk
        table = catT[:, 7, 0:NB * CHUNKS * PAGES_CH].bitcast(I32)
        at[0] = lru_at
        S2 = v3(take(3 * 512), 3)
        P2, PT2 = (v3(take(2 * 512), 2) for _ in range(2))
        O2 = v3(take(2 * 512), 2)
        at[0] = 0
        latT = take(2 * KEYS_ROW * P).rearrange("p (b k n) -> p b k n", b=2, k=KEYS_ROW)
        ropT = take(2 * 2 * P).rearrange("p (b k n) -> p b k n", b=2, k=2)
        QLb = take(NB * NH * NS).rearrange("p (b h s) -> p b h s", b=NB, h=NH)
        QRB = take(NB * 4 * 64).rearrange("p (b k c) -> p b k c", b=NB, k=4)
        SN = take(NB * 64)[0:64, :]
        OLT = take(NH * 64).rearrange("p (h t) -> p h t", h=NH)
        M1, MD, PS1, PN, M2, PNs, MB = (take(n) for n in (2 * 64, P, 2 * 64, 2 * 64, 2 * 64, 64, 64))
        KV = take(2 * CHUNKS * KEYS_ROW * (R + ROPE)).rearrange("p (s n) -> p s n", s=2 * CHUNKS)
        at[0] = 0
        VV = v3(take(2 * D), 2)
        xe_at = at[0]
        XE = v3(take(2 * D), 2)
        XET = take(2 * D).rearrange("p (b k n) -> p b k n", b=2, k=KC)
        SG = v3(take(2 * 2 * C), 2)
        HT = take(2 * 2 * C).rearrange("p (b k n) -> p b k n", b=2, k=2)
        YE = v3(take(2 * D), 2)
        g_at = at[0]
        take(4 * D)
        G = [v3(arena[:, at_:at_ + 2 * D], 2) for at_ in (g_at, g_at + 2 * D, xe_at, xe_at + 2 * D)]
        rt = take(1200)

        SSQ, RST = small[:, 0:10], small[:, 10:20]
        sp8, lam_t = small[:, 20:22], small[:, 22:26]
        MX, NM = small[:, 26:29], small[:, 29:32]
        MC, RS = small[0:64, 32:33], small[0:64, 33:34]
        BN = sb("BN", [P, 2, 16])
        LSUM = sb("LSUM", [P, 4, NH])
        RL = sb("RL", [P, 4, NH])
        eps = sb("eps", [P, 2])
        HS = sb("HS", [P, 2, NB])

        xs = nc.dram_tensor("xs", (SLOTS, D), F32, kind="Internal").ap()
        ys = nc.dram_tensor("ys", (SLOTS, D), F32, kind="Internal").ap()

        def slot_of(e_half, par_, k):
            return 3 * par_ + k

        def slab(slot):
            return ring[:, slot, :]

        def seg_a(buf, j, lo, n):
            return v3(buf[:, j, 3 + SEQ:LA], NB)[:, :, lo:lo + n]

        def seg_z(buf, j, lo, n):
            return v3(buf[:, j, 2 + SEQ:LZ], NB)[:, :, lo:lo + n]

        def lay(ap, l):
            sub = ap[bass.ds(l, 1)]
            names = "bcdef"[:len(ap.shape) - 1]
            return sub.rearrange(f"a {names[0]} {' '.join(names[1:])} -> (a {names[0]}) {' '.join(names[1:])}")

        def fm_free(m):
            if m < 2:
                return fm_dve, m + 1
            if m < 8:
                return fm_act, m - 1
            return fm_dve, m - 5

        block = ctx.enter_context(nc.Block())

        @block.sync
        def _(sp):
            sp.dma_start(const[:, :], a["const"]).then_inc(const_loaded, 16)
            sp.dma_start(X[:, 0:4, :], a["x_prompt"].rearrange("a (t p) d -> p (a t) d", p=P)).then_inc(x_loaded, 16)
            sp.dma_start(X[0:64, 4, :], a["x_sample"].rearrange("b s d -> (b s) d")).then_inc(x_loaded, 16)

            def w_in_load(l, n):
                sp.dma_start(slab(n % RING), lay(a["w_in"], l)[:, n, :]).then_inc(ring_loaded[n % RING], 16)

            for n in range(RING):
                w_in_load(0, n)

            with sp.Fori(0, DEPTH) as l:
                def w_out_load(n):
                    sp.dma_start(slab(2 + n), lay(a["w_out"], l)[:, n, :]).then_inc(ring_loaded[2 + n], 16)

                def expert_load(e, slot, k):
                    src = lay(a[["w_gate", "w_up", "w_down"][k]], l)[bass.ds(e, 1)]
                    if k < 2:
                        src = src.rearrange("e (p c) f -> (e p) (c f)", c=KC)
                        sp.dma_start(slab(slot), src).then_inc(ring_loaded[slot], 16)
                    else:
                        src = src.rearrange("e (k p) d -> p (e k) d", p=P)
                        sp.dma_start(v3(slab(slot), 2), src).then_inc(ring_loaded[slot], 16)

                sp.wait_ge(tm_made, TILES)
                sp.dma_start(slab(0), lay(a["w_in"], l)[:, 6, :]).then_inc(ring_loaded[0], 16)
                expert_load(0, 1, 1)
                for n in range(4):
                    sp.wait_ge(fm_made, 2 + 2 * n)
                    w_out_load(n)
                sp.wait_ge(fm_made, 10)
                expert_load(0, 0, 0)
                with sp.If(l < 1):
                    sp.wait_ge(zero_ready, 1)
                    sp.dma_start(xs.rearrange("(p k) (j n) -> p (k j) n", p=P, n=256),
                                 zero[:, :].unsqueeze(1).to_broadcast([P, SLOTS // P * 4, 256])).then_inc(xs_zeroed, 16)
                    sp.dma_start(ys[NE * C:SLOTS, :].rearrange("(p k) (j n) -> p (k j) n", p=P, n=256),
                                 zero[:, :].unsqueeze(1).to_broadcast([P, OVER * C // P * 4, 256])).then_inc(xs_zeroed, 16)
                sp.wait_ge(norm_ready, TILES + 1)
                sp.dma_start(lay(o["ckv_p"], l).rearrange("b (t p) r -> p (b t) r", p=P), CKV[:, 0:4, :]).then_inc(out_stored, 16)
                sp.dma_start(lay(o["kr_p"], l).rearrange("b (t p) r -> p (b t) r", p=P), KR[:, 0:4, :]).then_inc(out_stored, 16)
                sp.dma_start(lay(o["ckv_s"], l).rearrange("b s r -> (b s) r"), CKV[0:64, 4, :]).then_inc(out_stored, 16)
                sp.dma_start(lay(o["kr_s"], l).rearrange("b s r -> (b s) r"), KR[0:64, 4, :]).then_inc(out_stored, 16)
                sp.wait_ge(kn_made, NH)
                sp.dma_start(ln_rows, lay(a["ln_mix"], l).partition_broadcast(P)).then_inc(ln_loaded, 16)
                sp.wait_ge(st_taken, 1)
                for name, at0, n in [("h_p", ST_H, 1), ("h_s", ST_H + 1, NB), ("ca_p", ST_C, 3), ("ca_s", ST_C + 3, 3 * NB),
                                     ("cb_p", ST_S, 2), ("cb_s", ST_S + 2, 2 * NB)]:
                    dst = lay(o[name], l)
                    if len(dst.shape) == 3:
                        dst = dst.rearrange("b k w -> (b k) w")
                    sp.dma_start(dst, ST2[at0:at0 + n, :]).then_inc(out_stored, 16)
                sp.wait_ge(out_stored, 16 * 10)
                sp.sem_inc(states_stored, 1)
                sp.wait_ge(y_made, TILES)
                expert_load(0, 2, 2)
                for k in range(3):
                    expert_load(1, 3 + k, k)
                sp.wait_ge(x_ready, TILES)
                sp.dma_start(ln_rows, lay(a["ln_ffn"], l).partition_broadcast(P)).then_inc(ln_loaded, 16)

                def xe_load(e, q):
                    sp.dma_start(XE[:, q, :], xs.rearrange("(e s) d -> e s d", s=C)[bass.ds(e, 1)].rearrange("e s d -> (e s) d")
                                 ).then_inc(xe_loaded[q], 16)

                def ye_store(e, q):
                    sp.wait_ge(ye_act, e + 1)
                    sp.wait_ge(ye_dve, e + 1)
                    sp.sem_inc(held, 1)
                    sp.dma_start(ys.rearrange("(e s) d -> e s d", s=C)[bass.ds(e, 1)].rearrange("e s d -> (e s) d"),
                                 YE[:, q, :]).then_inc(ye_stored[q], 16)

                def moe_step(e, q, load_x=True, load_gu=True, load_dn=True):
                    if load_x:
                        sp.wait_ge(xet_made, 2 * e + 2)
                        sp.sem_inc(held, 1)
                        xe_load(e + 2, q)
                    if load_gu:
                        sp.wait_ge(gu_made, e + 1)
                        sp.sem_inc(held, 1)
                        for k in range(2):
                            expert_load(e + 2, 3 * q + k, k)
                    if load_dn:
                        sp.wait_ge(dn_made, 2 * e)
                        sp.sem_inc(held, 1)
                        expert_load(e + 1, 3 * (1 - q) + 2, 2)
                    ye_store(e - 1, 1 - q)

                sp.wait_ge(scattered, l * (16 * 2 * TILES) + 16 * 2 * TILES)
                xe_load(0, 0)
                xe_load(1, 1)
                sp.wait_ge(xet_made, 2)
                xe_load(2, 0)
                sp.wait_ge(gu_made, 1)
                for k in range(2):
                    expert_load(2, k, k)
                with sp.Fori(0, 6) as i:
                    moe_step(2 * i + 1, 1)
                    moe_step(2 * i + 2, 0)
                moe_step(13, 1)
                moe_step(14, 0, load_x=False, load_gu=False)
                n_over = sp.value_load(over_i[0:1, 0:1], min_val=0, max_val=OVER)

                def next_slabs(early, ns):
                    with sp.If((n_over < 1) if early else (n_over > 0)):
                        with sp.If(l < DEPTH - 1):
                            for n in ns:
                                w_in_load((l + 1) % DEPTH, n)

                sp.wait_ge(gu_made, 15)
                next_slabs(True, [0, 1])
                ye_store(14, 0)
                ye_store(15, 1)
                for q in range(2):
                    sp.wait_ge(ye_stored[q], 16 * NE // 2)

                with sp.If(n_over > 0):
                    with sp.Fori(0, n_over) as i:
                        e = sp.value_load(over_i[0:1, bass.ds(i + 1, 1)], min_val=0, max_val=NE - 1)
                        for k in range(2):
                            src = lay(a[["w_gate", "w_up"][k]], l)[bass.ds(e, 1)].rearrange("e (p c) f -> (e p) (c f)", c=KC)
                            sp.dma_start(slab(k), src).then_inc(ov_loaded, 16)
                        src = lay(a["w_down"], l)[bass.ds(e, 1)].rearrange("e (k p) d -> p (e k) d", p=P)
                        sp.dma_start(v3(slab(2), 2), src).then_inc(ov_loaded, 16)
                        view = xs.rearrange("(e s) d -> e s d", s=C)[bass.ds(i + NE, 1)].rearrange("e s d -> (e s) d")
                        sp.dma_start(XE[:, 0, :], view).then_inc(ov_loaded, 16)
                        sp.wait_ge(ov_act, 3 * i + 3)
                        sp.wait_ge(ov_dve, 3 * i + 3)
                        sp.sem_inc(held, 1)
                        view = ys.rearrange("(e s) d -> e s d", s=C)[bass.ds(i + NE, 1)].rearrange("e s d -> (e s) d")
                        sp.dma_start(view, YE[:, 0, :]).then_inc(ov_stored, 16)
                        sp.wait_ge(ov_stored, i * 16 + 16)
                        sp.sem_inc(held, 1)
                sp.sem_inc(ov_done, 1)

                next_slabs(False, [0, 1])
                sp.wait_ge(v_used, 1)
                with sp.If(l < DEPTH - 1):
                    for n in range(2, RING):
                        w_in_load((l + 1) % DEPTH, n)
                sp.wait_ge(x_ready, 2 * TILES)
                sp.sem_inc(layer_end, 1)
                sp.wait_ge(layer_go, l + 1)
                sp.sem_inc(held, 1)

            sp.dma_start(o["y_p"].rearrange("a (t p) d -> p (a t) d", p=P), X[:, 0:4, :]).then_inc(x_loaded, 16)
            sp.dma_start(o["y_s"].rearrange("b s d -> (b s) d"), X[0:64, 4, :]).then_inc(x_loaded, 16)
            sp.wait_ge(x_loaded, 64)

        @block.gpsimd
        def _(pool):
            pool.memset(zero[:, :], 0.0).then_inc(zero_ready, 1)

            with pool.Fori(0, DEPTH) as l:
                pool.dma_start(table, a["page_table"].partition_broadcast(P)).then_inc(table_loaded, 16)
                pool.wait_ge(ot_taken, 4)
                pool.wait_ge(pt_made, 4 * NH)
                pool.wait_ge(states_stored, 1)
                pool.memset(QRB, 0.0).then_inc(qrb_zero, 1)

                def gather(b, q, g):
                    s = CHUNKS * q + g
                    pool.tensor_copy(idx_1[:, s:s + 1], idx_i[:, bass.ds(b * CHUNKS + g, 1)]).then_inc(slot_idx, 1)
                    pool.wait_ge(slot_idx, b * CHUNKS + g + 1)
                    pool.sem_inc(held, 1)
                    pool.indirect_dma_start(out=KV[:, s, :], out_offset=None, in_=a["cache"],
                                            in_offset=bass.IndirectOffsetOnAxis(ap=idx_1[:, s:s + 1], axis=0)
                                            ).then_inc(kv_loaded[s], 16)

                pool.wait_ge(idx_ready, 1)
                for b in range(2):
                    for g in range(CHUNKS):
                        gather(b, b, g)
                with pool.Fori(0, NB // 2 - 1) as i:
                    for q in range(2):
                        for g in range(CHUNKS):
                            pool.wait_ge(pvl_made, (2 * i + q) * CHUNKS + g + 1)
                            gather(2 * i + 2 + q, q, g)

                for t in range(TILES):
                    pool.wait_ge(g_ready, t + 1)
                    pool.tensor_tensor(X[0:rows(t), t, :], X[0:rows(t), t, :], ln_rows[0:rows(t), 1, :], ALU.add
                                       ).then_inc(x_ready, 1)

                pool.wait_ge(slots_ready, 1)
                pool.wait_ge(xs_zeroed, 32)
                pool.wait_ge(x_ready, TILES)
                for t in range(TILES):
                    for k in range(2):
                        pool.indirect_dma_start(out=xs, out_offset=bass.IndirectOffsetOnAxis(ap=slot_i[0:rows(t), k, t:t + 1], axis=0),
                                                in_=X[0:rows(t), t, :], in_offset=None).then_inc(scattered, 16)
                pool.wait_ge(ov_done, 1)
                for t in range(TILES):
                    if t >= 4:
                        pool.wait_ge(v_used, t - 3)
                    for k in range(2):
                        pool.indirect_dma_start(out=G[t % 4][0:rows(t), k, :], out_offset=None, in_=ys,
                                                in_offset=bass.IndirectOffsetOnAxis(ap=slot_i[0:rows(t), k, t:t + 1], axis=0)
                                                ).then_inc(g_loaded[t % 4], 16)
                for t in range(TILES):
                    pool.wait_ge(g_ready, TILES + t + 1)
                    pool.tensor_tensor(X[0:rows(t), t, :], X[0:rows(t), t, :], ln_rows[0:rows(t), 1, :], ALU.add
                                       ).then_inc(x_ready, 1)
                pool.wait_ge(x_ready, 2 * TILES)
                pool.wait_ge(layer_end, l * 4 + 4)
                pool.sem_inc(held, 1)
                pool.drain()
                pool.sem_clear(layer_range)
                pool.sem_inc(layer_go, 1)

        @block.scalar
        def _(act):
            with act.Fori(0, DEPTH) as l:
                own = Own(act, act_own)
                act.dma_start(par[:, :, :], lay(a["par"], l)).then_inc(par_loaded, 16)
                act.dma_start(gatew[:, :, :, :], lay(a["gatew"], l)).then_inc(gatew_loaded, 16)
                act.dma_start(kvg[:, :], lay(a["kvg"], l).partition_broadcast(P)).then_inc(kvg_loaded, 16)
                act.dma_start(w_uq, lay(a["w_uq"], l).rearrange("(k p) n -> p k n", p=P)).then_inc(uq_loaded, 16)
                act.dma_start(w_uk, lay(a["w_uk"], l)).then_inc(uk_loaded, 16)
                act.dma_start(w_ukT[:, :, :], lay(a["w_ukT"], l)).then_inc(uk_loaded, 16)
                act.dma_start(w_uv[:, :], lay(a["w_uv"], l)).then_inc(uk_loaded, 16)
                act.dma_start(wr[:, :, :], lay(a["wr"], l)).then_inc(rout_loaded, 16)
                act.dma_start(rbias[:, :], lay(a["rbias"], l).partition_broadcast(P)).then_inc(rout_loaded, 16)

                def xt_copy(n, tiles=range(TILES)):
                    for t in tiles:
                        act.wait_ge(xt_made, 10 * n + 2 * t + 1)
                        act.activation(xT[:, 0:4, cols(t)], v3(PS[:, 4 * n + (2 * t) % 4, :], 4)[:, :, 0:rows(t)], ACT.Copy
                                       ).then_inc(xt_act, 1)

                xt_copy(0)
                for t in range(TILES):
                    act.wait_ge(tm_made, t + 1)
                    act.activation(PT[0:rows(t), t, :], PS[0:rows(t), 4 + t % 4, 0:416], ACT.Copy).then_inc(tm_taken, 1)
                act.wait_ge(ssq_ready, 1)
                act.activation(RST, SSQ, ACT.Sqrt, bias=eps[:, 0:1]).then_inc(rms_ready, 1)
                act.wait_ge(lam_exp, 1)
                own.link(act.activation(lam_t[:, 0:2], lam_t[:, 0:2], ACT.Exp))
                act.activation(lam_t[:, 0:2], lam_t[:, 0:2], ACT.Ln, bias=1.0).then_inc(lam_ln, 1)

                def fm_copy(m):
                    act.wait_ge(fm_made, m + 1)
                    j = m % 2
                    if m < 6:
                        f = ACT.Gelu_apprx_tanh if m < 4 else ACT.Copy
                        act.activation(catT[:, m - 2, 0:HALF], PS[:, m % 2, 0:HALF], f)
                        act.activation(catT[:, m - 2, HALF:NTOK], PS[:, 2 + m % 2, 0:HALF], f).then_inc(fm_act, 1)
                    else:
                        act.activation(z_pad[:, j, 2:2 + HALF], PS[:, m % 2, 0:HALF], ACT.Copy)
                        act.activation(z_pad[:, j, 2 + HALF:2 + SEQ], PS[:, 2 + m % 2, 0:SEQ - HALF], ACT.Copy)
                        act.activation(seg_z(z_pad, j, 2, NS), v3(PS[:, 2 + m % 2, SEQ - HALF:HALF], NB), ACT.Copy).then_inc(fm_act, 1)
                for m in range(2, 6):
                    fm_copy(m)
                act.wait_ge(par_loaded, 16)
                for g in range(2):
                    for j in range(2):
                        n = 2 * g + j
                        act.wait_ge(gate_made, n + 1)
                        dst, bias = (SI, SR)[g], par[:, j, P_GXB + g:P_GXB + g + 1]
                        act.activation(dst[:, j, 0:512], PS[:, 4 + n % 2, :], ACT.Sigmoid, bias=bias)
                        act.activation(dst[:, j, 512:600], PS[:, 6 + n % 2, 0:88], ACT.Sigmoid, bias=bias).then_inc(gate_taken, 1)
                act.wait_ge(loga_ready, 1)
                act.activation(A[:, :, 0:600], SR[:, :, 0:600], ACT.Exp)
                act.activation(U[:, :, 0:600], SR[:, :, 0:600], ACT.Tanh, scale=-1.0).then_inc(expa_ready, 1)
                for m in range(6, 8):
                    fm_copy(m)
                act.wait_ge(mult2_ready, 1)
                act.activation(U[:, :, 0:600], SR[:, :, 0:600], ACT.Sqrt).then_inc(mult_ready, 1)
                for t in range(TILES):
                    act.wait_ge(kt_made, t + 1)
                    for k in range(2):
                        ins = act.activation(cqT[:, k, cols(t)], PS[:, t % 2, P * k:P * k + rows(t)], ACT.Identity,
                                             scale=par[:, k, P_QG:P_QG + 1])
                    ins.then_inc(cqt_ready, 1)
                def qt_copy(t):
                    act.wait_ge(qt_made, 2 * t + 1)
                    src = v3(PS[0:QK, 2, :], 4)[:, :, 0:rows(t)]
                    dst = QTp[:, 0:4, cols(t)] if t < 4 else QTs[:, 0:4, :]
                    act.activation(dst, src, ACT.Copy).then_inc(qt_act, 1)

                for t in range(TILES):
                    act.wait_ge(q_made, t + 1)
                    if t >= 2:
                        act.wait_ge(qt_made, 2 * t - 2)
                    act.activation(Q[0:rows(t), t % 2, 0:512], PS[0:rows(t), 4 + 2 * (t % 2), :], ACT.Copy)
                    act.activation(Q[0:rows(t), t % 2, 512:768], PS[0:rows(t), 5 + 2 * (t % 2), 0:256], ACT.Copy
                                   ).then_inc(q_taken, 1)
                    if t >= 1:
                        qt_copy(t - 1)
                qt_copy(4)
                for h in range(NH):
                    act.wait_ge(kn_made, h + 1)
                    act.activation(KT[0:NOPE, h, :], PS[0:NOPE, h % 2, :], ACT.Copy).then_inc(kn_taken, 1)
                act.wait_ge(st_made, 1)
                act.activation(ST2, PS[0:NST, 2, 0:2 * P], ACT.Copy).then_inc(st_taken, 1)

                def ot_copy(qb):
                    act.wait_ge(ot_made, qb + 1)
                    act.activation(catT[:, 4:8, P * qb:P * qb + P], v3(PS[:, 7, :], 4), ACT.Copy).then_inc(ot_taken, 1)

                for i in range(4 * NH):
                    qb, h = i // NH, i % NH
                    nk = P * (qb + 1)
                    act.wait_ge(nm_ready, i + 1)
                    if i >= 2:
                        act.wait_ge(pt_made, i - 1)
                    act.activation(P2[:, i % 2, 0:nk], S2[:, i % 3, 0:nk], ACT.Exp, bias=NM[:, i % 3:i % 3 + 1], scale=SCALE,
                                   accum_out=LSUM[:, qb, h:h + 1]).then_inc(p_ready, 1)
                    if h == 3 and qb > 0:
                        ot_copy(qb - 1)
                ot_copy(3)

                def lat_copy(b, g):
                    n = b * CHUNKS + g
                    act.wait_ge(lat_made, n * 3 + 1)
                    act.activation(ropT[:, g % 2, :, :], v3(PS[:, 4, 0:256], 2), ACT.Copy).then_inc(lat_act, 1)
                    act.wait_ge(lat_made, n * 3 + 2)
                    act.activation(latT[:, g % 2, 0:4, :], v3(PS[:, 2 * (g % 2), :], 4), ACT.Copy).then_inc(lat_act, 1)

                def sc_copy(b, q, g):
                    act.wait_ge(sc_made, b * CHUNKS + g + 1)
                    act.activation(S_sb[:, q, g, :], PS[:, 5 + g % 2, :], ACT.Copy).then_inc(sc_taken, 1)

                def exps(b, q, *chunks):
                    for g in chunks:
                        act.wait_ge(sub_ready, b * (CHUNKS + 1) + g + 1)
                        if g < CHUNKS:
                            act.activation(S_sb[:, q, g, :], S_sb[:, q, g, :], ACT.Exp, scale=SCALE).then_inc(exp_ready, 1)
                        else:
                            act.activation(PN[0:64, 64 * q:64 * q + 64], PNs[0:64, :], ACT.Exp, scale=SCALE).then_inc(exp_ready, 1)

                def step(b, q, back=True):
                    lat_copy(b, 0)
                    lat_copy(b, 1)
                    sc_copy(b, q, 0)
                    lat_copy(b, 2)
                    if back:
                        exps(b - 1, 1 - q, 0, 1)
                    sc_copy(b, q, 1)
                    lat_copy(b, 3)
                    if back:
                        exps(b - 1, 1 - q, 2, 3, 4)
                    sc_copy(b, q, 2)
                    sc_copy(b, q, 3)

                step(0, 0, back=False)
                with act.Fori(0, NB // 2 - 1) as i:
                    step(2 * i + 1, 1)
                    step(2 * i + 2, 0)
                step(NB - 1, 1)
                exps(NB - 1, 1, 0, 1, 2, 3, 4)
                act.wait_ge(yc_made, 1)
                act.activation(catT[0:64, 4:8, SEQ:NTOK], v3(PS[0:64, 0, 0:256], 4), ACT.Copy).then_inc(yc_act, 1)

                def norms(n, tiles=range(TILES)):
                    for t in tiles:
                        r = rows(t)
                        act.wait_ge(var_ready, n * TILES + t + 1)
                        act.activation(BN[0:r, t % 2, 14:15], BN[0:r, t % 2, 13:14], ACT.Sqrt, bias=eps[0:r, 1:2]
                                       ).then_inc(std_ready, 1)
                        act.wait_ge(nmr_ready, n * TILES + t + 1)
                        act.activation(VV[0:r, t % 2, :], VV[0:r, t % 2, :], ACT.Identity, bias=BN[0:r, t % 2, 14:15],
                                       scale=BN[0:r, t % 2, 15:16]).then_inc(vn_ready, 1)

                norms(0, range(4))
                xt_copy(1, range(4))
                norms(0, [4])
                xt_copy(1, [4])
                act.wait_ge(lg_ready, 1)
                act.activation(rt[:, 100:120], rt[:, 100:120], ACT.Exp).then_inc(re_ready, 1)
                act.wait_ge(le_ready, 1)
                act.activation(rt[:, 240:260], rt[:, 240:260], ACT.Exp).then_inc(ree_ready, 1)
                act.wait_ge(scattered, l * (16 * 2 * TILES) + 16 * 2 * TILES)
                act.activation(X[:, 0:4, :], X[:, 0:4, :], ACT.Copy, scale=ALPHA)
                act.activation(X[0:64, 4, :], X[0:64, 4, :], ACT.Copy, scale=ALPHA).then_inc(ax_ready, 1)

                def xet_copy(e, q):
                    act.wait_ge(xet_made, 2 * e + 1)
                    act.activation(XET[:, q, 0:4, :], v3(PS[:, 0, :], 4), ACT.Copy).then_inc(xet_act, 1)

                def silu(e, q):
                    act.wait_ge(gu_made, e + 1)
                    act.activation(SG[:, q, :], PS[:, 2 + q, 0:2 * C], ACT.Silu).then_inc(silu_ready, 1)

                def ye_copy(e, q, wait_store):
                    act.wait_ge(dn_made, 2 * e + 1)
                    if wait_store is not None:
                        act.wait_ge(ye_stored[q], wait_store)
                    act.activation(YE[:, q, 0:512], PS[:, 4 + 2 * q, :], ACT.Copy).then_inc(ye_act, 1)

                xet_copy(0, 0)
                silu(0, 0)
                xet_copy(1, 1)
                silu(1, 1)
                xet_copy(2, 0)
                ye_copy(0, 0, None)
                silu(2, 0)
                xet_copy(3, 1)
                ye_copy(1, 1, None)
                with act.Fori(0, 6) as i:
                    for q in range(2):
                        silu(2 * i + 3 + q, 1 - q)
                        xet_copy(2 * i + 4 + q, q)
                        ye_copy(2 * i + 2 + q, q, i * 16 + 16)
                silu(15, 1)
                ye_copy(14, 0, 16 * 7)
                ye_copy(15, 1, 16 * 7)

                n_over = act.value_load(over_i[0:1, 0:1], min_val=0, max_val=OVER)
                with act.If(n_over > 0):
                    with act.Fori(0, n_over) as i:
                        act.wait_ge(ov_pe, 3 * i + 1)
                        act.activation(XET[:, 0, 0:4, :], v3(PS[:, 0, :], 4), ACT.Copy).then_inc(ov_act, 1)
                        act.wait_ge(ov_pe, 3 * i + 2)
                        act.activation(SG[:, 0, :], PS[:, 2, 0:2 * C], ACT.Silu).then_inc(ov_act, 1)
                        act.wait_ge(ov_pe, 3 * i + 3)
                        act.wait_ge(ye_stored[0], 16 * NE // 2)
                        act.activation(YE[:, 0, 0:512], PS[:, 4, :], ACT.Copy).then_inc(ov_act, 1)

                norms(1)
                act.drain()
                act.sem_inc(layer_end, 1)
                act.wait_ge(layer_go, l + 1)

        @block.vector
        def _(dve):
            dve.memset(PT[64:P, 4, :], 0.0).then_inc(dve_start, 1)
            dve.memset(eps[:, 0:1], RMS_EPS).then_inc(dve_start, 1)
            dve.memset(eps[:, 1:2], LN_EPS).then_inc(dve_start, 1)
            dve.memset(small[:, :], 1.0).then_inc(dve_start, 1)
            dve.memset(first_row[:, :], 0.0).then_inc(dve_start, 1)
            dve.wait_ge(dve_start, 5)
            dve.wait_ge(const_loaded, 16)
            layer_rows = float(a["cache"].shape[0] // DEPTH)

            with dve.Fori(0, DEPTH) as l:
                own = Own(dve, dve_own)

                def xt_copy(n, tiles=range(TILES)):
                    for t in tiles:
                        dve.wait_ge(xt_made, 10 * n + 2 * t + 2)
                        dve.tensor_copy(xT[:, 4:8, cols(t)], v3(PS[:, 4 * n + (2 * t + 1) % 4, :], 4)[:, :, 0:rows(t)]
                                        ).then_inc(xt_dve, 1)

                xt_copy(0)
                dve.wait_ge(par_loaded, 16)
                own(dve.memset(xa_pad[:, :, 0:3], 0.0))
                own(dve.memset(z_pad[:, :, 0:2], 0.0))
                for j in range(2):
                    own(dve.tensor_copy(seg_a(xa_pad, j, 0, 3), v3(par[:, j, P_CS:P_CS + 3 * NB], NB)))
                    own(dve.tensor_copy(seg_z(z_pad, j, 0, 2), v3(par[:, j, P_SS:P_SS + 2 * NB], NB)))
                own.link(dve.tensor_scalar(lam_t[:, 2:4], par[:, :, P_LAM], -1.0, None, ALU.mult))
                dve.tensor_tensor(lam_t[:, 0:2], lam_t[:, 2:4], par[:, :, P_LAM], ALU.min).then_inc(lam_exp, 1)
                for t in range(TILES):
                    r = rows(t)
                    dve.wait_ge(tm_taken, t + 1)
                    for k, (lo, n) in enumerate([(0, QL), (QL, R)]):
                        own.link(dve.tensor_tensor_reduce(out=junk[0:r, 0:n], in0=PT[0:r, t, lo:lo + n], in1=PT[0:r, t, lo:lo + n],
                                                          scale=1.0 / n, scalar=0.0, op0=ALU.mult, op1=ALU.add,
                                                          accum_out=SSQ[0:r, 2 * t + k:2 * t + k + 1]))
                dve.sem_inc(ssq_ready, 1)
                cos = cs[:, :, 0:16]
                sin = cs[:, :, 16:32]
                x1, x2 = PT[:, :, 384:400], PT[:, :, 400:416]
                r4 = [v3(rope_tmp[:, k, 0:80], TILES) for k in range(4)]
                own(dve.tensor_tensor(r4[0], x1, cos, ALU.mult))
                own(dve.tensor_tensor(r4[1], x2, sin, ALU.mult))
                own(dve.tensor_tensor(r4[2], x1, sin, ALU.mult))
                own.link(dve.tensor_tensor(r4[3], x2, cos, ALU.mult))
                own(dve.tensor_tensor(KR[:, :, 0:16], r4[0], r4[1], ALU.subtract))
                own.link(dve.tensor_tensor(KR[:, :, 16:32], r4[2], r4[3], ALU.add))
                dve.wait_ge(rms_ready, 1)
                dve.wait_ge(kvg_loaded, 16)
                own.link(dve.reciprocal(RST, RST))
                for t in range(TILES):
                    r = rows(t)
                    own(dve.tensor_scalar(PT[0:r, t, 0:QL], PT[0:r, t, 0:QL], RST[0:r, 2 * t:2 * t + 1], None, ALU.mult))
                    dve.scalar_tensor_tensor(out=CKV[0:r, t, :], in0=PT[0:r, t, QL:QL + R], scalar=RST[0:r, 2 * t + 1:2 * t + 2],
                                             in1=kvg[0:r, :], op0=ALU.mult, op1=ALU.mult).then_inc(norm_ready, 1)
                own.settle()
                dve.sem_inc(norm_ready, 1)
                for j in range(2):
                    dve.wait_ge(fm_made, j + 1)
                    dve.tensor_copy(xa_pad[:, j, 3:3 + HALF], PS[:, j, 0:HALF])
                    dve.tensor_copy(xa_pad[:, j, 3 + HALF:3 + SEQ], PS[:, 2 + j, 0:SEQ - HALF])
                    dve.tensor_copy(seg_a(xa_pad, j, 3, NS), v3(PS[:, 2 + j, SEQ - HALF:HALF], NB)).then_inc(fm_dve, 1)
                dve.wait_ge(fm_dve, 2)
                own.settle()
                n = LA - 3
                for j in range(2):
                    own.link(dve.tensor_scalar(XC[:, j, 0:n], xa_pad[:, j, 0:n], par[:, j, P_CW:P_CW + 1],
                                               par[:, j, P_CB:P_CB + 1], ALU.mult, ALU.add))
                    for k in range(1, 4):
                        ins = dve.scalar_tensor_tensor(out=XC[:, j, 0:n], in0=xa_pad[:, j, k:k + n], scalar=par[:, j, P_CW + k:P_CW + k + 1],
                                                       in1=XC[:, j, 0:n], op0=ALU.mult, op1=ALU.add)
                        if k < 3:
                            own.link(ins)
                        else:
                            ins.then_inc(conv_ready, 1)
                dve.wait_ge(lam_ln, 1)
                own.link(dve.scalar_tensor_tensor(out=sp8, in0=lam_t[:, 2:4], scalar=0.0, in1=lam_t[:, 0:2], op0=ALU.max, op1=ALU.add))
                own.link(dve.tensor_scalar(sp8, sp8, -8.0, None, ALU.mult))
                dve.wait_ge(gate_taken, 4)
                own(dve.tensor_scalar(SR[:, 0, 0:600], SR[:, 0, 0:600], sp8[:, 0:1], None, ALU.mult))
                own.link(dve.tensor_scalar(SR[:, 1, 0:600], SR[:, 1, 0:600], sp8[:, 1:2], None, ALU.mult))
                dve.sem_inc(loga_ready, 1)
                own.link(dve.tensor_tensor(SI[:, :, 0:600], SI[:, :, 0:600], XC[:, :, 0:600], ALU.mult))
                dve.wait_ge(expa_ready, 1)
                own.link(dve.tensor_scalar(SR[:, :, 0:600], U[:, :, 0:600], 1.0, None, ALU.add))
                own.link(dve.reciprocal(SR[:, :, 0:600], SR[:, :, 0:600]))
                dve.scalar_tensor_tensor(out=SR[:, :, 0:600], in0=U[:, :, 0:600], scalar=2.0, in1=SR[:, :, 0:600],
                                         op0=ALU.mult, op1=ALU.mult).then_inc(mult2_ready, 1)
                dve.wait_ge(mult_ready, 1)
                own.link(dve.tensor_tensor(SI[:, :, 0:600], SI[:, :, 0:600], U[:, :, 0:600], ALU.mult))
                dve.wait_ge(fm_act, 2)
                for j in range(2):
                    fa, fb = seg_a(A, j, 0, 1), seg_a(SI, j, 0, 1)
                    own.link(dve.tensor_tensor(HS[:, j, :].unsqueeze(2), fa, par[:, j, P_H0:P_H0 + NB].unsqueeze(2), ALU.mult))
                    own(dve.tensor_tensor(fb, fb, HS[:, j, :].unsqueeze(2), ALU.add))
                    own.link(dve.memset(fa, 0.0))
                    own.link(dve.tensor_tensor_scan(XC[:, j, 0:600], A[:, j, 0:600], SI[:, j, 0:600], 0.0, ALU.mult, ALU.add))
                    own(dve.tensor_tensor(catT[:, j, 0:SEQ], catT[:, j, 0:SEQ], XC[:, j, 0:SEQ], ALU.mult))
                    own(dve.tensor_tensor(v3(catT[:, j, SEQ:NTOK], NB), v3(catT[:, j, SEQ:NTOK], NB), seg_a(XC, j, 0, NS), ALU.mult))
                    own(dve.tensor_copy(ST[:, j, 0:1], XC[:, j, SEQ - 1:SEQ]))
                    own(dve.tensor_copy(ST[:, j, 1:9].unsqueeze(2), seg_a(XC, j, NS - 1, 1)))
                    own(dve.tensor_copy(ST[:, j, ST_C:ST_C + 3], xa_pad[:, j, SEQ:SEQ + 3]))
                    own(dve.tensor_copy(v3(ST[:, j, ST_C + 3:ST_S], NB), seg_a(xa_pad, j, NS, 3)))
                dve.wait_ge(fm_act, 6)
                for j in range(2):
                    dve.wait_ge(fm_made, 9 + j)
                    dve.tensor_tensor(z_pad[:, j, 2:2 + HALF], z_pad[:, j, 2:2 + HALF], PS[:, j, 0:HALF], ALU.mult)
                    dve.tensor_tensor(z_pad[:, j, 2 + HALF:2 + SEQ], z_pad[:, j, 2 + HALF:2 + SEQ], PS[:, 2 + j, 0:SEQ - HALF], ALU.mult)
                    dve.tensor_tensor(seg_z(z_pad, j, 2, NS), seg_z(z_pad, j, 2, NS), v3(PS[:, 2 + j, SEQ - HALF:HALF], NB), ALU.mult
                                      ).then_inc(fm_dve, 1)
                dve.wait_ge(fm_dve, 4)
                n = LZ - 2
                for j in range(2):
                    own.link(dve.tensor_scalar(ZC[:, j, 0:n], z_pad[:, j, 0:n], par[:, j, P_SW:P_SW + 1], None, ALU.mult))
                    for k in range(1, 3):
                        own.link(dve.scalar_tensor_tensor(out=ZC[:, j, 0:n], in0=z_pad[:, j, k:k + n],
                                                          scalar=par[:, j, P_SW + k:P_SW + k + 1], in1=ZC[:, j, 0:n],
                                                          op0=ALU.mult, op1=ALU.add))
                    own(dve.tensor_tensor(catT[:, 2 + j, 0:SEQ], catT[:, 2 + j, 0:SEQ], ZC[:, j, 0:SEQ], ALU.mult))
                    own(dve.tensor_tensor(v3(catT[:, 2 + j, SEQ:NTOK], NB), v3(catT[:, 2 + j, SEQ:NTOK], NB),
                                          seg_z(ZC, j, 0, NS), ALU.mult))

                for t in range(TILES):
                    r = rows(t)
                    dve.wait_ge(kt_made, t + 1)
                    dve.tensor_copy(CKT[:, cols(t)], PS[:, 2 + t % 2, 0:r])
                    dve.tensor_copy(KRT[:, cols(t)], PS[0:ROPE, 2 + t % 2, P:P + r]).then_inc(ckt_ready, 1)

                def qt_copy(t):
                    dve.wait_ge(qt_made, 2 * t + 2)
                    src = v3(PS[0:QK, 3, :], 4)[:, :, 0:rows(t)]
                    dst = QTp[:, 4:8, cols(t)] if t < 4 else QTs[:, 4:8, :]
                    dve.tensor_copy(dst, src).then_inc(qt_dve, 1)

                for t in range(TILES):
                    r = rows(t)
                    dve.wait_ge(q_taken, t + 1)
                    qv = v3(Q[0:r, t % 2, :], NH)
                    x1, x2 = qv[:, :, 64:80], qv[:, :, 80:96]
                    cb = cs[0:r, t, 0:16].unsqueeze(1).to_broadcast([r, NH, 16])
                    sn_ = cs[0:r, t, 16:32].unsqueeze(1).to_broadcast([r, NH, 16])
                    r4 = [v3(rope_tmp[0:r, k, 0:128], NH) for k in range(4)]
                    own.settle()
                    own(dve.tensor_tensor(r4[0], x1, cb, ALU.mult))
                    own(dve.tensor_tensor(r4[1], x2, sn_, ALU.mult))
                    own(dve.tensor_tensor(r4[2], x1, sn_, ALU.mult))
                    own.link(dve.tensor_tensor(r4[3], x2, cb, ALU.mult))
                    own(dve.tensor_tensor(x1, r4[0], r4[1], ALU.subtract))
                    dve.tensor_tensor(x2, r4[2], r4[3], ALU.add).then_inc(q_roped, 1)
                    dve.wait_ge(q_roped, t + 1)
                    if t >= 1:
                        qt_copy(t - 1)
                qt_copy(4)
                own.settle()
                dve.tensor_copy(KT[NOPE:QK, :, :], KRT[:, 0:SEQ].unsqueeze(1).to_broadcast([ROPE, NH, SEQ])).then_inc(kr_ready, 1)
                for t in range(4):
                    dve.wait_ge(v_made, t + 1)
                    dve.tensor_copy(V[:, t, :], PS[:, 4 + t, :]).then_inc(v_taken, 1)
                for j in range(2):
                    own(dve.tensor_copy(ST[:, j, ST_S:ST_S + 2], z_pad[:, j, SEQ:SEQ + 2]))
                    own(dve.tensor_copy(v3(ST[:, j, ST_S + 2:NST], NB), seg_z(z_pad, j, NS, 2)))
                own.settle()
                dve.sem_inc(st_ready, 1)
                dve.wait_ge(st_made, 1)

                dve.wait_ge(table_loaded, l * 16 + 16)
                own.link(dve.tensor_tensor(v3(pages, NB * CHUNKS), v3(table, NB * CHUNKS),
                                           sel.unsqueeze(1).to_broadcast([P, NB * CHUNKS, PAGES_CH]), ALU.mult))
                own.link(dve.tensor_reduce(idx_f[:, :], v3(pages, NB * CHUNKS), AX, ALU.add))
                own.link(dve.tensor_scalar(idx_f[:, :], idx_f[:, :], float(ROWS_PAGE), p16, ALU.mult, ALU.add))
                own.link(dve.tensor_scalar(idx_f[:, :], idx_f[:, :], first_row[:, :], None, ALU.add))
                own(dve.tensor_scalar(first_row[:, :], first_row[:, :], layer_rows, None, ALU.add))
                dve.tensor_copy(idx_i[:, :], idx_f[:, :]).then_inc(idx_ready, 1)

                def pt_copy(i):
                    n = i // NH + 1
                    dve.wait_ge(pt_made, i + 1)
                    if i >= 2:
                        dve.wait_ge(pv_made, i - 1)
                    dve.tensor_copy(PT2[:, i % 2, 0:P * n], PS[:, 3 + i % 2, 0:P * n]).then_inc(pt_taken, 1)

                def o_scale(qb):
                    dve.wait_ge(pv_made, NH * (qb + 1))
                    if qb >= 2:
                        dve.wait_ge(ot_made, qb - 1)
                    own.link(dve.reciprocal(RL[:, qb, :], LSUM[:, qb, :]))
                    dve.tensor_tensor(v3(O2[:, qb % 2, :], NH), v3(PS[:, 5 + qb % 2, :], NH),
                                      RL[:, qb, :].unsqueeze(2).to_broadcast([P, NH, VH]), ALU.mult).then_inc(o_ready, 1)

                for i in range(4 * NH):
                    qb, h = i // NH, i % NH
                    nk = P * (qb + 1)
                    dve.wait_ge(s_made, i + 1)
                    if i >= 3:
                        dve.wait_ge(p_ready, i - 2)
                    dve.tensor_tensor_reduce(out=S2[:, i % 3, 0:nk], in0=PS[:, i % 3, 0:nk], in1=mask[:, SEQ - nk:SEQ], scale=1.0,
                                             scalar=-3e38, op0=ALU.add, op1=ALU.max, accum_out=MX[:, i % 3:i % 3 + 1]
                                             ).then_inc(s_taken, 1)
                    dve.wait_ge(s_taken, i + 1)
                    dve.tensor_scalar(NM[:, i % 3:i % 3 + 1], MX[:, i % 3:i % 3 + 1], -SCALE, None, ALU.mult).then_inc(nm_ready, 1)
                    if i >= 2:
                        pt_copy(i - 2)
                    if h == 2 and qb > 0:
                        o_scale(qb - 1)
                pt_copy(4 * NH - 2)
                pt_copy(4 * NH - 1)
                o_scale(3)

                dve.wait_ge(ql_made, 1)
                dve.tensor_copy(QLb.rearrange("p b h s -> p h b s"), PS[:, 5, :].rearrange("p (h b s) -> p h b s", h=NH, b=NB)
                                ).then_inc(ql_taken, 1)
                dve.wait_ge(qrb_zero, 1)
                dve.wait_ge(qt_act, TILES)
                for k in range(4):
                    dve.tensor_copy(QRB[32 * k:32 * k + 32, :, k, :].rearrange("p b (h s) -> p b h s", h=NH),
                                    QTs[NOPE:QK, :, :].rearrange("p h (b s) -> p b h s", b=NB)).then_inc(qrb_ready, 1)
                dve.wait_ge(sn_made, 1)
                dve.tensor_tensor(SN, PS[0:64, 7, :], mask_new, ALU.add).then_inc(sn_taken, 1)

                def lat_copy(b, g):
                    dve.wait_ge(lat_made, (b * CHUNKS + g) * 3 + 3)
                    dve.tensor_copy(latT[:, g % 2, 4:8, :], v3(PS[:, 2 * (g % 2) + 1, :], 4)).then_inc(lat_dve, 1)

                def back_1(b, q):
                    dve.wait_ge(sc_taken, b * CHUNKS + CHUNKS)
                    chain = Own(dve, dve_max, b * 3 + 1)
                    m1, m2 = M1[:, 64 * q:64 * q + 64], M2[:, 64 * q:64 * q + 64]
                    chain.link(dve.tensor_reduce(m1, S_sb[:, q, 3, :].rearrange("p (k c) -> p c k", c=64), AX, ALU.max))
                    chain.link(dve.tensor_tensor(m1, m1, m2, ALU.max))
                    dve.tensor_tensor(m1[0:64, :], m1[0:64, :], SN[:, bass.ds(b * 64, 64)], ALU.max).then_inc(m1_ready, 1)

                def back_0(b, q):
                    dve.wait_ge(sc_taken, b * CHUNKS + CHUNKS - 1)
                    chain = Own(dve, dve_max, b * 3)
                    chain.link(dve.tensor_reduce(M2[:, 64 * q:64 * q + 64], S_sb[:, q, 0:3, :].rearrange("p g (k c) -> p c g k", c=64),
                                                 mybir.AxisListType.XY, ALU.max))

                def back_2(b, q):
                    chain = Own(dve, dve_back, b * 3)
                    dve.wait_ge(mt_made, b + 1)
                    chain.link(dve.tensor_reduce(MC, PS[0:64, 7, 256:384], AX, ALU.max))
                    dve.tensor_scalar(MD[0:64, :], ones[0:64, :], MC, None, ALU.mult).then_inc(md_ready, 1)

                def back_3(b, q):
                    dve.wait_ge(mb_made, b + 1)
                    chain = Own(dve, dve_back, b * 3 + 1)
                    chain.link(dve.tensor_copy(MB, PS[:, 7, 384:448]))
                    mb = MB
                    for g in range(CHUNKS):
                        s = v3(S_sb[:, q, g, :], KEYS_ROW)
                        dve.tensor_tensor(s, s, mb.unsqueeze(1).to_broadcast([P, KEYS_ROW, 64]), ALU.subtract).then_inc(sub_ready, 1)
                    dve.tensor_tensor(PNs[0:64, :], SN[:, bass.ds(b * 64, 64)], mb[0:64, :], ALU.subtract).then_inc(sub_ready, 1)

                def back_4(b, q):
                    dve.wait_ge(exp_ready, b * (CHUNKS + 1) + CHUNKS)
                    dve.tensor_reduce(PS1[:, 64 * q:64 * q + 64], S_sb[:, q, :, :].rearrange("p g (k c) -> p c g k", c=64),
                                      mybir.AxisListType.XY, ALU.add).then_inc(ps_ready, 1)

                def back_5(b, q):
                    chain = Own(dve, dve_back, b * 3 + 2)
                    dve.wait_ge(sum_made, b + 1)
                    chain.link(dve.reciprocal(RS, PS[0:64, 7, 128:129]))
                    dve.tensor_scalar(OL[64 * q:64 * q + 64, bass.ds((b // 2) * R, R)] if isinstance(b, int) else
                                      OL[64 * q:64 * q + 64, bass.ds(b * (R // 2) - q * (R // 2), R)],
                                      PS[0:64, 7, 0:R], RS, None, ALU.mult).then_inc(ol_taken, 1)

                def step(b, q, back=True):
                    lat_copy(b, 0)
                    lat_copy(b, 1)
                    if back:
                        back_2(b - 1, 1 - q)
                    lat_copy(b, 2)
                    if back:
                        back_3(b - 1, 1 - q)
                    lat_copy(b, 3)
                    if back:
                        back_4(b - 1, 1 - q)
                    back_0(b, q)
                    back_1(b, q)
                    if back:
                        back_5(b - 1, 1 - q)

                dve.sem_inc(ol_taken, 1)
                step(0, 0, back=False)
                with dve.Fori(0, NB // 2 - 1) as i:
                    step(2 * i + 1, 1)
                    step(2 * i + 2, 0)
                step(NB - 1, 1)
                for back in [back_2, back_3, back_4, back_5]:
                    back(NB - 1, 1)
                dve.wait_ge(olt_made, 1)
                for q in range(2):
                    dve.tensor_copy(OLT.rearrange("p h (j q s) -> p j q h s", j=NB // 2, q=2)[:, :, q],
                                    PS[:, 2, :].rearrange("p (j q h s) -> p j q h s", j=NB // 2, q=2, h=NH)[:, :, q]
                                    ).then_inc(olt_taken, 1)
                dve.wait_ge(yc_made, 1)
                dve.tensor_copy(catT[64:P, 4:8, SEQ:NTOK], v3(PS[0:64, 1, 0:256], 4)).then_inc(yc_dve, 1)

                def stats(n, t):
                    r, v, bn = rows(t), VV[0:rows(t), t % 2, :], BN[0:rows(t), t % 2, :]
                    own(dve.bn_stats(bn[:, 0:6], v[:, 0:512]))
                    own.link(dve.bn_stats(bn[:, 6:12], v[:, 512:1024]))
                    dve.bn_aggr(bn[:, 12:14], bn[:, 0:12]).then_inc(var_ready, 1)

                def inverse(n, t):
                    bn = BN[0:rows(t), t % 2, :]
                    dve.wait_ge(std_ready, n * TILES + t + 1)
                    own.link(dve.reciprocal(bn[:, 15:16], bn[:, 14:15]))
                    dve.tensor_scalar(bn[:, 14:15], bn[:, 12:13], -1.0, bn[:, 15:16], ALU.mult, ALU.mult).then_inc(nmr_ready, 1)

                def gain(n, t):
                    r = rows(t)
                    dve.wait_ge(vn_ready, n * TILES + t + 1)
                    dve.tensor_tensor(X[0:r, t, :], VV[0:r, t % 2, :], ln_rows[0:r, 0, :], ALU.mult).then_inc(g_ready, 1)

                def residual(t):
                    r, b = rows(t), 2 * (t % 2)
                    dve.wait_ge(y_made, t + 1)
                    dve.scalar_tensor_tensor(out=VV[0:r, t % 2, :], in0=X[0:r, t, :], scalar=ALPHA,
                                             in1=PS[0:r, b:b + 2, :].rearrange("p a b -> p (a b)"),
                                             op0=ALU.mult, op1=ALU.add).then_inc(y_taken, 1)
                    dve.wait_ge(y_taken, t + 1)
                    stats(0, t)

                dve.wait_ge(ln_loaded, 16)
                for t in range(4):
                    residual(t)
                    if t >= 1:
                        gain(0, t - 1)
                    inverse(0, t)
                gain(0, 3)
                xt_copy(1, [0, 1])
                residual(4)
                xt_copy(1, [2, 3])
                inverse(0, 4)
                gain(0, 4)
                xt_copy(1, [4])

                def r5(lo, *dims):
                    n = int(np.prod(dims))
                    ap = rt[:, lo:lo + TILES * n].rearrange("p (t n) -> p t n", t=TILES)
                    return ap if len(dims) == 1 else ap.rearrange("p t (g e) -> p t g e", g=dims[0])

                LG = r5(0, 20)
                GE, EE = r5(100, 4), r5(240, 4)
                G1, E1, E2 = r5(120, 4), r5(260, 4), r5(280, 4)
                TMP, PR = r5(140, 16), r5(220, 4)
                sc5 = rt[:, 300:380].rearrange("p (k t) -> p k t", k=16)
                MM = rt[:, 400:640].rearrange("p (k t e) -> p k t e", k=3, t=TILES)
                CUM = rt[:, 640:640 + 96].rearrange("p (t e) -> p t e", t=TILES + 1)
                SL = r5(740, 16)
                NE_, OT, INC, OB = (rt[:, 820 + 16 * k:836 + 16 * k] for k in range(4))
                T2 = r5(890, 16)
                OVT = rt[0:1, 980:980 + OVER * NE].rearrange("p (i e) -> p i e", i=OVER)
                OVF = rt[0:1, 1120:1120 + 1 + OVER]

                def bc(ap, n):
                    return ap.unsqueeze(2).to_broadcast([P, TILES, n])

                def first_of(dst, val, top):
                    own.link(dve.tensor_tensor(dst, val, bc(top, 4), ALU.is_equal))
                    own.link(dve.tensor_tensor(PR, dst, pri.unsqueeze(1).to_broadcast([P, TILES, 4]), ALU.mult))
                    own.link(dve.tensor_reduce(sc5[:, 15, :], PR, AX, ALU.max))
                    own.link(dve.tensor_tensor(dst, PR, bc(sc5[:, 15, :], 4), ALU.is_equal))

                dve.wait_ge(rt_made, 1)
                dve.wait_ge(rout_loaded, 32)
                own.link(dve.memset(LG[:, 4, :], 0.0))
                own(dve.tensor_tensor(LG[:, 0:4, :], v3(PS[:, 2, 0:128], 4)[:, :, 0:20],
                                      rbias[:, :].unsqueeze(1).to_broadcast([P, 4, 20]), ALU.add))
                own.link(dve.tensor_tensor(LG[0:64, 4, :], PS[0:64, 2, 128:148], rbias[0:64, :], ALU.add))
                own.link(dve.tensor_reduce(sc5[:, 0, :], LG[:, :, 0:4], AX, ALU.max))
                dve.tensor_tensor(GE, LG[:, :, 0:4], bc(sc5[:, 0, :], 4), ALU.subtract).then_inc(lg_ready, 1)
                dve.wait_ge(re_ready, 1)
                own(dve.tensor_reduce(sc5[:, 1, :], GE, AX, ALU.add))
                own.link(dve.tensor_reduce(sc5[:, 2, :], GE, AX, ALU.max))
                own.link(dve.reciprocal(sc5[:, 3, :], sc5[:, 1, :]))
                own.link(dve.tensor_tensor(sc5[:, 3, :], sc5[:, 3, :], sc5[:, 2, :], ALU.mult))
                first_of(G1, GE, sc5[:, 2, :])
                el = LG[:, :, 4:20].rearrange("p t (g e) -> p t g e", g=4)
                t4 = TMP.rearrange("p t (g e) -> p t g e", g=4)
                own.link(dve.tensor_tensor(t4, el, G1.unsqueeze(3).to_broadcast([P, TILES, 4, 4]), ALU.mult))
                own.link(dve.tensor_reduce(EE, t4.rearrange("p t g e -> p t e g"), AX, ALU.add))
                own.link(dve.tensor_reduce(sc5[:, 4, :], EE, AX, ALU.max))
                dve.tensor_tensor(EE, EE, bc(sc5[:, 4, :], 4), ALU.subtract).then_inc(le_ready, 1)
                dve.wait_ge(ree_ready, 1)
                own.link(dve.tensor_reduce(sc5[:, 5, :], EE, AX, ALU.max))
                first_of(E1, EE, sc5[:, 5, :])
                own.link(dve.scalar_tensor_tensor(out=EE, in0=E1, scalar=-2.0, in1=EE, op0=ALU.mult, op1=ALU.add))
                own.link(dve.tensor_reduce(sc5[:, 6, :], EE, AX, ALU.max))
                first_of(E2, EE, sc5[:, 6, :])
                own.link(dve.tensor_tensor(G1, G1, bc(valid, 4), ALU.mult))
                g4 = G1.unsqueeze(3).to_broadcast([P, TILES, 4, 4])
                for k, e in enumerate([E1, E2]):
                    own.link(dve.tensor_tensor(MM[:, k, :, :].rearrange("p t (g e) -> p t g e", g=4), g4,
                                               e.unsqueeze(2).to_broadcast([P, TILES, 4, 4]), ALU.mult))
                own(dve.memset(CUM[:, 0, :], 0.0))
                own.link(dve.tensor_tensor(MM[:, 2, :, :], MM[:, 0, :, :], MM[:, 1, :, :], ALU.add))
                for t in range(TILES):
                    own.link(dve.tensor_tensor(CUM[:, t + 1, :], CUM[:, t, :], MM[:, 2, t, :], ALU.add))
                dve.sem_inc(m_ready, 1)
                own.link(dve.tensor_tensor(sc5[:, 7, :], sc5[:, 5, :], sc5[:, 6, :], ALU.add))
                own.link(dve.reciprocal(sc5[:, 7, :], sc5[:, 7, :]))
                own.link(dve.tensor_tensor(sc5[:, 7, :], sc5[:, 7, :], sc5[:, 3, :], ALU.mult))
                own(dve.tensor_tensor(w12[:, 0, :], sc5[:, 5, :], sc5[:, 7, :], ALU.mult))
                own(dve.tensor_tensor(w12[:, 1, :], sc5[:, 6, :], sc5[:, 7, :], ALU.mult))
                dve.wait_ge(pos_made, 1)
                POS = v3(PS[:, 3, 0:TILES * NE], TILES)
                own.link(dve.tensor_copy(NE_, PS[:, 3, 256:256 + NE]))
                own.link(dve.tensor_scalar(OT, NE_, float(C), None, ALU.is_gt))
                for k in range(2, MORE + 1):
                    own.link(dve.scalar_tensor_tensor(out=OT, in0=NE_, scalar=float(C * k), in1=OT, op0=ALU.is_gt, op1=ALU.add))
                own.link(dve.tensor_tensor_scan(INC, ones[:, 0:NE], OT, 0.0, ALU.mult, ALU.add))
                own.link(dve.tensor_tensor(OB, INC, OT, ALU.subtract))
                own.link(dve.scalar_tensor_tensor(out=OB, in0=OB, scalar=float(C), in1=gap, op0=ALU.mult, op1=ALU.add))
                own.link(dve.tensor_scalar(T2, POS, float(C), None, ALU.is_ge))
                own.link(dve.tensor_tensor(T2, T2, OB.unsqueeze(1).to_broadcast([P, TILES, NE]), ALU.mult))
                own.link(dve.tensor_tensor(SL, POS, first_slot.unsqueeze(1).to_broadcast([P, TILES, NE]), ALU.add))
                own.link(dve.tensor_tensor(SL, SL, T2, ALU.add))
                for k in range(2):
                    own.link(dve.tensor_tensor(T2, SL, MM[:, k, :, :], ALU.mult))
                    own.link(dve.tensor_reduce(sc5[:, 8 + k, :], T2, AX, ALU.add))
                dve.tensor_copy(slot_i[:, :, :], sc5[:, 8:10, :]).then_inc(slots_ready, 1)
                own.link(dve.tensor_tensor(OVT, INC[0:1, :].unsqueeze(1).to_broadcast([1, OVER, NE]),
                                           iota.unsqueeze(2).to_broadcast([1, OVER, NE]), ALU.is_le))
                own.link(dve.tensor_reduce(OVF[:, 1:1 + OVER], OVT, AX, ALU.add))
                own.link(dve.tensor_scalar(OVF[:, 1:1 + OVER], OVF[:, 1:1 + OVER], float(NE - 1), None, ALU.min))
                own.link(dve.tensor_copy(OVF[:, 0:1], INC[0:1, NE - 1:NE]))
                dve.tensor_copy(over_i[:, :], OVF).then_inc(slots_ready, 1)

                def xet_copy(e, q):
                    dve.wait_ge(xet_made, 2 * e + 2)
                    dve.tensor_copy(XET[:, q, 4:8, :], v3(PS[:, 1, :], 4)).then_inc(xet_dve, 1)

                def h_mul(e, q):
                    dve.wait_ge(silu_ready, e + 1)
                    dve.tensor_tensor(HT[:, q, :, :], v3(SG[:, q, :], 2), v3(PS[:, 2 + q, 2 * C:4 * C], 2), ALU.mult).then_inc(h_ready, 1)

                def ye_copy(e, q, wait_store):
                    dve.wait_ge(dn_made, 2 * e + 2)
                    if wait_store is not None:
                        dve.wait_ge(ye_stored[q], wait_store)
                    dve.tensor_copy(YE[:, q, 512:1024], PS[:, 5 + 2 * q, :]).then_inc(ye_dve, 1)

                xet_copy(0, 0)
                h_mul(0, 0)
                xet_copy(1, 1)
                h_mul(1, 1)
                xet_copy(2, 0)
                ye_copy(0, 0, None)
                h_mul(2, 0)
                xet_copy(3, 1)
                ye_copy(1, 1, None)
                with dve.Fori(0, 6) as i:
                    for q in range(2):
                        h_mul(2 * i + 3 + q, 1 - q)
                        xet_copy(2 * i + 4 + q, q)
                        ye_copy(2 * i + 2 + q, q, i * 16 + 16)
                h_mul(15, 1)
                ye_copy(14, 0, 16 * 7)
                ye_copy(15, 1, 16 * 7)

                n_over = dve.value_load(over_i[0:1, 0:1], min_val=0, max_val=OVER)
                with dve.If(n_over > 0):
                    with dve.Fori(0, n_over) as i:
                        dve.wait_ge(ov_pe, 3 * i + 1)
                        dve.tensor_copy(XET[:, 0, 4:8, :], v3(PS[:, 1, :], 4)).then_inc(ov_dve, 1)
                        dve.wait_ge(ov_act, 3 * i + 2)
                        dve.tensor_tensor(HT[:, 0, :, :], v3(SG[:, 0, :], 2), v3(PS[:, 2, 2 * C:4 * C], 2), ALU.mult).then_inc(ov_dve, 1)
                        dve.wait_ge(ov_pe, 3 * i + 3)
                        dve.wait_ge(ye_stored[0], 16 * NE // 2)
                        dve.tensor_copy(YE[:, 0, 512:1024], PS[:, 5, :]).then_inc(ov_dve, 1)

                dve.wait_ge(ln_loaded, 32)
                dve.wait_ge(ax_ready, 1)
                for t in range(TILES):
                    r, q = rows(t), t % 2
                    dve.wait_ge(g_loaded[t % 4], l * (64 if t % 4 == 0 else 32) + (64 if t == 4 else 32))
                    own.link(dve.scalar_tensor_tensor(out=VV[0:r, q, :], in0=G[t % 4][0:r, 0, :], scalar=w12[0:r, 0, t:t + 1],
                                                      in1=X[0:r, t, :], op0=ALU.mult, op1=ALU.add))
                    dve.scalar_tensor_tensor(out=VV[0:r, q, :], in0=G[t % 4][0:r, 1, :], scalar=w12[0:r, 1, t:t + 1],
                                             in1=VV[0:r, q, :], op0=ALU.mult, op1=ALU.add).then_inc(v_used, 1)
                    dve.wait_ge(v_used, t + 1)
                    stats(1, t)
                    if t >= 1:
                        gain(1, t - 1)
                    inverse(1, t)
                gain(1, TILES - 1)
                dve.drain()
                dve.sem_inc(layer_end, 1)
                dve.wait_ge(layer_go, l + 1)

        @block.tensor
        def _(pe):
            pe.wait_ge(const_loaded, 16)
            pe.wait_ge(x_loaded, 32)
            with pe.Fori(0, DEPTH) as l:
                def turn_x(n, tiles=range(TILES)):
                    for t in tiles:
                        r = rows(t)
                        if n == 1:
                            pe.wait_ge(x_ready, t + 1)
                        for half in range(2):
                            k = 2 * t + half
                            if k >= 4:
                                pe.wait_ge((xt_act, xt_dve)[half], TILES * n + (k - 4) // 2 + 1)
                            for i in range(4):
                                ins = pe.transpose(PS[:, 4 * n + k % 4, P * i:P * i + r], X[0:r, t, 4 * half + i::KC], ident[0:r, 0:r])
                            ins.then_inc(xt_made, 1)

                turn_x(0)
                pe.wait_ge(xt_act, TILES)
                pe.wait_ge(xt_dve, TILES)
                pe.wait_ge(ring_loaded[0], loaded(l, 0, 0))
                pe.wait_ge(ring_loaded[1], loaded(l, 1, 0))
                for t in range(TILES):
                    if t == 4:
                        pe.wait_ge(tm_taken, 1)
                    for c in range(KC):
                        pe.matmul(PS[0:rows(t), 4 + t % 4, 0:256], xT[:, c, cols(t)], v3(slab(0), KC)[:, c, :], start=(c == 0), stop=(c == KC - 1))
                    for c in range(KC):
                        ins = pe.matmul(PS[0:rows(t), 4 + t % 4, 256:416], xT[:, c, cols(t)], v3(slab(1)[:, 0:KC * 160], KC)[:, c, :],
                                        start=(c == 0), stop=(c == KC - 1))
                    ins.then_inc(tm_made, 1)
                def project(m):
                    s, j = m // 2, m % 2
                    slot = (2 + s) % RING
                    if j == 0:
                        pe.wait_ge(ring_loaded[slot], loaded(l, slot, 1 if s == 4 else 0))
                    if m >= 2:
                        pe.wait_ge(*fm_free(m - 2))
                    w = v3(slab(slot), KC)
                    for lo, n, bank in [(0, HALF, j), (HALF, HALF, 2 + j)]:
                        for c in range(KC):
                            ins = pe.matmul(PS[:, bank, 0:n], w[:, c, P * j:P * j + P], xT[:, c, lo:lo + n], start=(c == 0), stop=(c == KC - 1))
                    ins.then_inc(fm_made, 1)
                for m in range(6):
                    project(m)
                pe.wait_ge(gatew_loaded, 16)
                pe.wait_ge(conv_ready, 2)
                pe.wait_ge(tm_taken, TILES)
                for g in range(2):
                    for j in range(2):
                        n = 2 * g + j
                        if n >= 2:
                            pe.wait_ge(gate_taken, n - 1)
                        pe.matmul(PS[:, 4 + n % 2, :], gatew[:, g, j, :], XC[:, j, 0:512], start=True, stop=True)
                        pe.matmul(PS[:, 6 + n % 2, 0:88], gatew[:, g, j, :], XC[:, j, 512:600], start=True, stop=True).then_inc(gate_made, 1)
                for m in range(6, 10):
                    project(m)
                pe.wait_ge(norm_ready, TILES + 1)
                pe.wait_ge(fm_act, 6)
                pe.wait_ge(fm_dve, 4)
                for t in range(TILES):
                    r = rows(t)
                    if t >= 2:
                        pe.wait_ge(cqt_ready, t - 1)
                        pe.wait_ge(ckt_ready, t - 1)
                    for k in range(2):
                        pe.transpose(PS[:, t % 2, P * k:P * k + r], PT[0:r, t, P * k:P * k + P], ident[0:r, 0:r])
                    pe.transpose(PS[:, 2 + t % 2, 0:r], CKV[0:r, t, :], ident[0:r, 0:r])
                    pe.transpose(PS[0:ROPE, 2 + t % 2, P:P + r], KR[0:r, t, :], ident[0:r, 0:r]).then_inc(kt_made, 1)

                def queries(t):
                    r, b = rows(t), 4 + 2 * (t % 2)
                    pe.wait_ge(cqt_ready, t + 1)
                    if t >= 2:
                        pe.wait_ge(q_taken, t - 1)
                    for lo, n in [(0, 512), (512, 256)]:
                        for k in range(2):
                            ins = pe.matmul(PS[0:r, b + lo // 512, 0:n], cqT[:, k, cols(t)], w_uq[:, k, lo:lo + n], start=(k == 0), stop=(k == 1))
                    ins.then_inc(q_made, 1)

                def turn_q(t):
                    r = rows(t)
                    pe.wait_ge(q_roped, t + 1)
                    for half in range(2):
                        if t >= 1:
                            pe.wait_ge((qt_act, qt_dve)[half], t)
                        for i in range(4):
                            h = 4 * half + i
                            ins = pe.transpose(PS[0:QK, 2 + half, P * i:P * i + r], Q[0:r, t % 2, QK * h:QK * h + QK], ident[0:r, 0:r])
                        ins.then_inc(qt_made, 1)

                pe.wait_ge(uq_loaded, 16)
                pe.wait_ge(gate_taken, 4)
                pe.wait_ge(tm_taken, TILES)
                pe.wait_ge(ckt_ready, TILES)
                queries(0)
                for t in range(TILES):
                    if t + 1 < TILES:
                        queries(t + 1)
                    turn_q(t)
                pe.wait_ge(uk_loaded, 48)
                pe.wait_ge(ckt_ready, TILES)
                pe.wait_ge(cqt_ready, TILES)
                for h in range(NH):
                    if h >= 2:
                        pe.wait_ge(kn_taken, h - 1)
                    pe.matmul(PS[0:NOPE, h % 2, :], w_uk[:, NOPE * h:NOPE * h + NOPE], CKT[:, 0:SEQ], start=True, stop=True).then_inc(kn_made, 1)
                pe.wait_ge(q_taken, TILES)
                for t in range(4):
                    pe.matmul(PS[:, 4 + t, :], CKT[:, cols(t)], w_uv[:, :], start=True, stop=True).then_inc(v_made, 1)
                pe.wait_ge(st_ready, 1)
                pe.wait_ge(qt_act, TILES)
                for j in range(2):
                    ins = pe.transpose(PS[0:NST, 2, P * j:P * j + P], ST[:, j, :], ident)
                ins.then_inc(st_made, 1)

                def scores(i):
                    qb, h = i // NH, i % NH
                    if i >= 3:
                        pe.wait_ge(s_taken, i - 2)
                    pe.matmul(PS[:, i % 3, 0:P * (qb + 1)], QTp[:, h, cols(qb)], KT[:, h, 0:P * (qb + 1)], start=True, stop=True
                              ).then_inc(s_made, 1)

                def turn_p(i):
                    pe.wait_ge(p_ready, i + 1)
                    if i >= 2:
                        pe.wait_ge(pt_taken, i - 1)
                    for j in range(i // NH + 1):
                        ins = pe.transpose(PS[:, 3 + i % 2, P * j:P * j + P], P2[:, i % 2, P * j:P * j + P], ident)
                    ins.then_inc(pt_made, 1)

                def weigh(i):
                    qb, h = i // NH, i % NH
                    if h == 0 and qb >= 2:
                        pe.wait_ge(o_ready, qb - 1)
                    pe.wait_ge(pt_taken, i + 1)
                    for j in range(qb + 1):
                        ins = pe.matmul(PS[:, 5 + qb % 2, VH * h:VH * h + VH], PT2[:, i % 2, P * j:P * j + P], V[:, j, VH * h:VH * h + VH],
                                        start=(j == 0), stop=(j == qb))
                    ins.then_inc(pv_made, 1)

                def turn_o(qb):
                    pe.wait_ge(o_ready, qb + 1)
                    if qb >= 1:
                        pe.wait_ge(ot_taken, qb)
                    for j in range(4):
                        ins = pe.transpose(PS[:, 7, P * j:P * j + P], O2[:, qb % 2, P * j:P * j + P], ident)
                    ins.then_inc(ot_made, 1)

                pe.wait_ge(kn_taken, NH)
                pe.wait_ge(kr_ready, 1)
                pe.wait_ge(v_taken, 4)
                pe.wait_ge(st_taken, 1)
                pe.wait_ge(qt_dve, TILES)
                scores(0)
                scores(1)
                for i in range(4 * NH):
                    if i + 2 < 4 * NH:
                        scores(i + 2)
                    turn_p(i)
                    if i >= 1:
                        weigh(i - 1)
                    if i % NH == 3 and i > NH:
                        turn_o(i // NH - 1)
                weigh(4 * NH - 1)
                turn_o(3)

                pe.wait_ge(o_ready, 4)
                for h in range(NH):
                    ins = pe.matmul(PS[:, 5, 64 * h:64 * h + 64], w_ukT[:, h, :], QTs[0:NOPE, h, :], start=True, stop=True)
                ins.then_inc(ql_made, 1)
                pe.wait_ge(ot_taken, 4)
                pe.wait_ge(qrb_ready, 4)
                pe.wait_ge(ql_taken, 1)
                pe.matmul(PS[0:64, 7, :], CKT[:, SEQ:NTOK], QLb.rearrange("p b h s -> p (b h s)"), start=True, stop=False)
                pe.matmul(PS[0:64, 7, :], KRT[:, SEQ:NTOK], QRB[0:ROPE, :, 0, :], start=False, stop=True).then_inc(sn_made, 1)

                def turn_kv(b, q, g):
                    n, s = b * CHUNKS + g, CHUNKS * q + g
                    pe.wait_ge(kv_loaded[s], l * (16 * NB // 2) + kv_count(b, q))
                    first = isinstance(b, int) and b == 0
                    lat = KV[:, s, 0:KEYS_ROW * R]
                    rop = KV[:, s, KEYS_ROW * R:]
                    if not (first and g == 0):
                        pe.wait_ge(lat_act, 2 * n - 1)
                    for k in range(2):
                        ins = pe.transpose(PS[:, 4, P * k:P * k + P], rop[:, P * k:P * k + P], ident)
                    ins.then_inc(lat_made, 1)
                    if not (first and g < 2):
                        pe.wait_ge(lat_act, 2 * n - 2)
                        pe.wait_ge(lat_dve, n - 1)
                    for h in range(2):
                        for k in range(4):
                            ins = pe.transpose(PS[:, 2 * (g % 2) + h, P * k:P * k + P], lat[:, P * (4 * h + k):P * (4 * h + k) + P], ident)
                        ins.then_inc(lat_made, 1)

                def kv_count(b, q):
                    return 16 * (b // 2 + 1) if isinstance(b, int) else b * 8 + (16 - 8 * q)

                def score_kv(b, q, g):
                    n = b * CHUNKS + g
                    pe.wait_ge(lat_act, 2 * n + 2)
                    pe.wait_ge(lat_dve, n + 1)
                    if not (isinstance(b, int) and b == 0 and g < 2):
                        pe.wait_ge(sc_taken, n - 1)
                    bank = PS[:, 5 + g % 2, :]
                    qr = QRB[:, bass.ds(b, 1), :, :].rearrange("p b k c -> p (b k c)")
                    ql = QLb[:, bass.ds(b, 1), :, :].rearrange("p b h s -> p (b h s)")
                    for h in range(2):
                        pe.matmul(bank[:, 256 * h:256 * h + 256], ropT[:, g % 2, h, :], qr, start=True, stop=True)
                        for k in range(4 * h, 4 * h + 4):
                            ins = pe.matmul(bank[:, 64 * k:64 * k + 64], latT[:, g % 2, k, :], ql, start=False, stop=True,
                                            skip_group_check=True)
                    ins.then_inc(sc_made, 1)

                def turn_max(b, q):
                    pe.wait_ge(ol_taken, b + 1)
                    pe.wait_ge(m1_ready, b + 1)
                    pe.sem_inc(held, 1)
                    pe.transpose(PS[0:64, 7, 256:384], M1[:, 64 * q:64 * q + 64], ident).then_inc(mt_made, 1)

                def spread_max(b):
                    pe.wait_ge(md_ready, b + 1)
                    pe.matmul(PS[:, 7, 384:448], MD[0:64, :], ident[0:64, 0:64], start=True, stop=True).then_inc(mb_made, 1)

                def weigh_kv(b, q, g):
                    pe.wait_ge(exp_ready, b * (CHUNKS + 1) + g + 1)
                    lat = KV[:, CHUNKS * q + g, 0:KEYS_ROW * R]
                    for k in range(KEYS_ROW):
                        ins = pe.matmul(PS[0:64, 7, 0:R], S_sb[:, q, g, 64 * k:64 * k + 64], lat[:, P * k:P * k + P],
                                        start=(g == 0 and k == 0), stop=False)
                    ins.then_inc(pvl_made, 1)

                def weigh_new(b, q):
                    pe.wait_ge(exp_ready, b * (CHUNKS + 1) + CHUNKS + 1)
                    pe.sem_inc(held, 1)
                    pn = PN[0:64, 64 * q:64 * q + 64]
                    pe.matmul(PS[0:64, 7, 0:R], pn, CKV[0:64, 4, :], start=False, stop=True)
                    pe.wait_ge(ps_ready, b + 1)
                    pe.matmul(PS[0:64, 7, 128:136], PS1[:, 64 * q:64 * q + 64], ones[:, 0:8], start=True, stop=False)
                    pe.matmul(PS[0:64, 7, 128:136], pn, ones[0:64, 0:8], start=False, stop=True).then_inc(sum_made, 1)

                def step(b, q, back=True):
                    turn_kv(b, q, 0)
                    turn_kv(b, q, 1)
                    score_kv(b, q, 0)
                    if back:
                        turn_max(b - 1, 1 - q)
                    turn_kv(b, q, 2)
                    if back:
                        spread_max(b - 1)
                    score_kv(b, q, 1)
                    turn_kv(b, q, 3)
                    if back:
                        weigh_kv(b - 1, 1 - q, 0)
                    score_kv(b, q, 2)
                    if back:
                        weigh_kv(b - 1, 1 - q, 1)
                    score_kv(b, q, 3)
                    if back:
                        weigh_kv(b - 1, 1 - q, 2)
                        weigh_kv(b - 1, 1 - q, 3)
                        weigh_new(b - 1, 1 - q)

                pe.wait_ge(sn_taken, 1)
                step(0, 0, back=False)
                with pe.Fori(0, NB // 2 - 1) as i:
                    step(2 * i + 1, 1)
                    step(2 * i + 2, 0)
                step(NB - 1, 1)
                turn_max(NB - 1, 1)
                spread_max(NB - 1)
                for g in range(CHUNKS):
                    weigh_kv(NB - 1, 1, g)
                weigh_new(NB - 1, 1)
                pe.wait_ge(ol_taken, NB + 1)
                for j in range(NB // 2):
                    ins = pe.transpose(PS[:, 2, P * j:P * j + P], OL[:, R * j:R * j + R], ident)
                ins.then_inc(olt_made, 1)
                pe.wait_ge(olt_taken, 2)
                for h in range(NH):
                    ins = pe.matmul(PS[0:VH, h % 2, 64 * (h // 2):64 * (h // 2) + 64], w_uv[:, VH * h:VH * h + VH], OLT[:, h, :], start=True, stop=True)
                ins.then_inc(yc_made, 1)

                pe.wait_ge(yc_act, 1)
                pe.wait_ge(yc_dve, 1)
                for s in range(2, 6):
                    pe.wait_ge(ring_loaded[s], loaded(l, s, 1))
                def mix_out(t):
                    if t >= 2:
                        pe.wait_ge(y_taken, t - 1)
                    for n in range(4):
                        for c in range(KC):
                            ins = pe.matmul(PS[0:rows(t), 2 * (t % 2) + n // 2, 256 * (n % 2):256 * (n % 2) + 256], catT[:, c, cols(t)],
                                            v3(slab(2 + n), KC)[:, c, :], start=(c == 0), stop=(c == KC - 1))
                    ins.then_inc(y_made, 1)
                def logits(t):
                    pe.wait_ge(xt_act, TILES + t + 1)
                    pe.wait_ge(xt_dve, TILES + t + 1)
                    for c in range(KC):
                        ins = pe.matmul(PS[0:rows(t), 2, 32 * t:32 * t + 20], xT[:, c, cols(t)], wr[:, c, :], start=(c == 0), stop=(c == KC - 1))
                    return ins

                for t in range(4):
                    mix_out(t)
                turn_x(1, [0, 1])
                mix_out(4)
                turn_x(1, [2, 3])
                pe.wait_ge(rout_loaded, 32)
                pe.wait_ge(y_taken, TILES)
                for t in range(4):
                    logits(t)
                turn_x(1, [4])
                ins = logits(4)
                ins.then_inc(rt_made, 1)
                pe.wait_ge(m_ready, 1)
                MM2 = rt[:, 400 + 2 * TILES * NE:400 + 3 * TILES * NE]
                pe.matmul(PS[:, 3, 0:TILES * NE], tri, MM2, start=True, stop=False)
                pe.matmul(PS[:, 3, 0:TILES * NE], ones, rt[:, 640:640 + TILES * NE], start=False, stop=True)
                pe.matmul(PS[:, 3, 256:256 + NE], ones, rt[:, 640 + TILES * NE:640 + (TILES + 1) * NE], start=True, stop=True
                          ).then_inc(pos_made, 1)
                pe.wait_ge(slots_ready, 2)

                def turn_e(src, ins_sem):
                    for half in range(2):
                        for i in range(4):
                            ins = pe.transpose(PS[:, half, P * i:P * i + C], src[:, 4 * half + i::KC], ident)
                        if ins_sem is xet_made or half == 1:
                            ins.then_inc(ins_sem, 1)

                def gate_up(q, slots, ins_sem):
                    for n in range(4):
                        w = v3(slab(slots[n // 2]), KC)
                        for c in range(KC):
                            ins = pe.matmul(PS[:, 2 + q, C * n:C * n + C], w[:, c, P * (n % 2):P * (n % 2) + P], XET[:, q, c, :],
                                            start=(c == 0), stop=(c == KC - 1))
                    ins.then_inc(ins_sem, 1)

                def down(q, slot, ins_sem):
                    for n in range(2):
                        for k in range(2):
                            ins = pe.matmul(PS[:, 4 + 2 * q + n, :], HT[:, q, k, :], v3(slab(slot), 2)[:, k, 512 * n:512 * n + 512],
                                            start=(k == 0), stop=(k == 1))
                        if ins_sem is dn_made or n == 1:
                            ins.then_inc(ins_sem, 1)

                def t_step(e, q, i):
                    pe.wait_ge(xe_loaded[q], i * 16 + 16)
                    if not isinstance(e, int) or e > 0:
                        pe.wait_ge(xet_act, e)
                        pe.wait_ge(xet_dve, e)
                    turn_e(XE[:, q, :], xet_made)

                def g_step(e, q, i):
                    for k in range(2):
                        pe.wait_ge(ring_loaded[3 * q + k], loaded(l, 3 * q + k, eload(3 * q + k, i)))
                    pe.wait_ge(xet_act, e + 1)
                    pe.wait_ge(xet_dve, e + 1)
                    if not isinstance(e, int) or e >= 2:
                        pe.wait_ge(h_ready, e - 1)
                    gate_up(q, [3 * q, 3 * q + 1], gu_made)

                def d_step(e, q, i):
                    pe.wait_ge(ring_loaded[3 * q + 2], loaded(l, 3 * q + 2, eload(3 * q + 2, i)))
                    pe.wait_ge(h_ready, e + 1)
                    if not isinstance(e, int) or e >= 2:
                        pe.wait_ge(ye_act, e - 1)
                        pe.wait_ge(ye_dve, e - 1)
                    down(q, 3 * q + 2, dn_made)

                t_step(0, 0, 0)
                g_step(0, 0, 0)
                t_step(1, 1, 0)
                g_step(1, 1, 0)
                t_step(2, 0, 1)
                d_step(0, 0, 0)
                g_step(2, 0, 1)
                t_step(3, 1, 1)
                d_step(1, 1, 0)
                with pe.Fori(0, 6) as i:
                    g_step(2 * i + 3, 1, i + 1)
                    t_step(2 * i + 4, 0, i + 2)
                    d_step(2 * i + 2, 0, i + 1)
                    g_step(2 * i + 4, 0, i + 2)
                    t_step(2 * i + 5, 1, i + 2)
                    d_step(2 * i + 3, 1, i + 1)
                g_step(15, 1, 7)
                d_step(14, 0, 7)
                d_step(15, 1, 7)

                n_over = pe.value_load(over_i[0:1, 0:1], min_val=0, max_val=OVER)
                with pe.If(n_over > 0):
                    pe.wait_ge(ye_act, NE)
                    pe.wait_ge(ye_dve, NE)
                    with pe.Fori(0, n_over) as i:
                        pe.wait_ge(ov_loaded, i * 64 + 64)
                        turn_e(XE[:, 0, :], ov_pe)
                        pe.wait_ge(ov_act, 3 * i + 1)
                        pe.wait_ge(ov_dve, 3 * i + 1)
                        gate_up(0, [0, 1], ov_pe)
                        pe.wait_ge(ov_dve, 3 * i + 2)
                        down(0, 2, ov_pe)
                        pe.wait_ge(ov_act, 3 * i + 3)
                        pe.wait_ge(ov_dve, 3 * i + 3)
                pe.drain()
                pe.sem_inc(layer_end, 1)
                pe.wait_ge(layer_go, l + 1)


_OUTS = [("y_p", (1, 512, 1024)), ("y_s", (8, 8, 1024)), ("ckv_p", (2, 1, 512, 128)), ("kr_p", (2, 1, 512, 32)),
         ("h_p", (2, 1, 256)), ("ca_p", (2, 1, 3, 256)), ("cb_p", (2, 1, 2, 256)), ("ckv_s", (2, 8, 8, 128)),
         ("kr_s", (2, 8, 8, 32)), ("h_s", (2, 8, 256)), ("ca_s", (2, 8, 3, 256)), ("cb_s", (2, 8, 2, 256))]


def _constants():
    c = np.zeros((P, NCONST), np.float32)
    p = np.arange(P)
    c[:, C_ID:C_ID + P] = np.eye(P)
    c[:, C_TRI:C_TRI + P] = p[:, None] < p[None, :]
    c[:, C_ONE:C_ONE + P] = 1
    c[:, C_MASK:C_MASK + SEQ] = np.where(np.arange(SEQ)[None] - (SEQ - P) <= p[:, None], 0, NEG)
    key, col = np.arange(64)[:, None], np.arange(512)[None]
    seen = (key // NS == col // 64) & (key % NS <= col % NS)
    c[0:64, C_NEW:C_NEW + 512] = np.where(seen, 0, NEG)
    pos = np.concatenate([np.arange(SEQ), PAST + np.arange(NB * NS) % NS, np.zeros(64)]).astype(np.float32)
    freqs = np.float32(10000.0) ** (-np.arange(16, dtype=np.float32) / np.float32(16))
    ang = pos[:, None] * freqs[None, :]
    both = np.concatenate([np.cos(ang), np.sin(ang)], 1).reshape(TILES, P, 32)
    c[:, C_CS:C_CS + 160] = both.transpose(1, 0, 2).reshape(P, 160)
    c[:, C_SEL:C_SEL + PAGES_CH] = p[:, None] // ROWS_PAGE == np.arange(PAGES_CH)[None]
    c[:, C_P16] = p % ROWS_PAGE
    c[:, C_VAL:C_VAL + 5] = (np.arange(5)[None] * P + p[:, None]) < NTOK
    c[:, C_PRI:C_PRI + 4] = [4, 3, 2, 1]
    e = np.arange(NE)
    c[:, C_EC:C_EC + NE] = e * C
    c[:, C_GAP:C_GAP + NE] = (NE - 1) * C - e * C
    c[:, C_IOTA:C_IOTA + NE] = e
    return c


def kernel(**inputs):
    import concourse.bacc as _bacc
    from concourse.bass_utils import run_bass_kernel_spmd as _run

    g = {k: np.asarray(v) for k, v in inputs.items()}
    L = DEPTH
    arr = {"const": _constants(), "x_prompt": g["x_prompt"], "x_sample": g["x_sample"]}
    w = g["w_in"].reshape(L, P, KC, 1696)
    w_in = np.zeros((L, P, 7, SLAB), np.float32)
    w_in[:, :, 0] = w[..., 1280:1536].reshape(L, P, SLAB)
    w_in[:, :, 1, 0:KC * 160] = w[..., 1536:1696].reshape(L, P, KC * 160)
    for s in range(5):
        w_in[:, :, 2 + s] = w[..., 256 * s:256 * s + 256].reshape(L, P, SLAB)
    arr["w_in"] = w_in
    arr["w_out"] = g["w_out"].reshape(L, KC, P, 4, 256).transpose(0, 2, 3, 1, 4).reshape(L, P, 4, SLAB)
    for k in ("w_gate", "w_up", "w_down", "w_uq"):
        arr[k] = g[k]
    arr["w_uk"] = g["w_uk"].reshape(L, R, NH * NOPE)
    arr["w_ukT"] = g["w_uk"].transpose(0, 3, 2, 1)
    arr["w_uv"] = g["w_uv"].reshape(L, R, NH * VH)
    gw = np.zeros((L, P, 2, 2, P), np.float32)
    for i, k in enumerate(("lru_gate_x_w", "lru_gate_a_w")):
        for j in range(2):
            for h in range(2):
                gw[:, 64 * h:64 * h + 64, i, j, 64 * h:64 * h + 64] = g[k][:, 2 * j + h]
    arr["gatew"] = gw
    rows_ = [g["lru_conv_w"], g["lru_conv_b"][:, None], g["lru_gate_x_b"][:, None], g["lru_gate_a_b"][:, None],
             g["lru_lambda"][:, None], g["sc_conv_w"], g["q_norm_g"][:, None], g["state_lru_h"],
             g["state_lru_conv"].reshape(L, 24, W), g["state_sconv"].reshape(L, 16, W)]
    arr["par"] = np.concatenate(rows_, 1).reshape(L, NPAR, 2, P).transpose(0, 3, 2, 1)
    arr["kvg"] = g["kv_norm_g"][:, None]
    arr["ln_mix"] = np.stack([g["ln_mix_g"], g["ln_mix_b"]], 1)
    arr["ln_ffn"] = np.stack([g["ln_ffn_g"], g["ln_ffn_b"]], 1)
    arr["wr"] = np.concatenate([g["router_group_w"], g["router_expert_w"]], 2).reshape(L, P, KC, 20)
    arr["rbias"] = np.concatenate([g["router_group_b"], g["router_expert_b"]], 1)[:, None]
    n_rows = g["cache_ckv"].shape[1] * ROWS_PAGE
    arr["cache"] = np.concatenate([g["cache_ckv"].reshape(L * n_rows, KEYS_ROW * R),
                                   g["cache_krope"].reshape(L * n_rows, KEYS_ROW * ROPE)], 1)
    arr["page_table"] = g["page_table"].reshape(256)

    nc = _bacc.Bacc("TRN2", target_bir_lowering=False, num_devices=1)
    arrays, a, o = {}, {}, {}
    for k, v in arr.items():
        v = np.ascontiguousarray(v)
        arrays[f"in_{k}"] = v
        a[k] = nc.dram_tensor(f"in_{k}", v.shape, mybir.dt.from_np(v.dtype), kind="ExternalInput").ap()
    for k, shape in _OUTS:
        o[k] = nc.dram_tensor(f"out_{k}", shape, F32, kind="ExternalOutput").ap()
    build(nc, a, o)
    r = _run(nc, [arrays], core_ids=[0])
    return tuple(r.results[0][f"out_{k}"] for k, _ in _OUTS)
```
